# Optimizing a Trainium2 kernel written in Bass

```python
import jax
import jax.numpy as jnp
from jax import lax
import numpy as np

D_MODEL = 1024
BATCH = 1
SEQ = 512
DEPTH = 2

GRID_W = 64
CTX_LEN = 256
N_EVEN = (DEPTH + 1) // 2
N_ODD = DEPTH // 2
NORM_EPS = 1e-6

HEAD_DIM = 128
N_Q_HEADS = 8
N_KV_HEADS = 2
Q_PER_KV = N_Q_HEADS // N_KV_HEADS
ATTN_W = N_Q_HEADS * HEAD_DIM
KV_W = N_KV_HEADS * HEAD_DIM
ROPE_THETA = 10000.0
ROPE_PAIRS_PER_AXIS = HEAD_DIM // 4
Q_BLOCK = 128

CONV_W = D_MODEL
CONV_TAPS = 3

PROJ_SPLITS = (ATTN_W, ATTN_W + KV_W, ATTN_W + 2 * KV_W,
               ATTN_W + 2 * KV_W + CONV_W, ATTN_W + 2 * KV_W + 2 * CONV_W)
PROJ_W = ATTN_W + 2 * KV_W + 3 * CONV_W
MIX_OUT_W = ATTN_W + CONV_W

RW_N = 64
RW_H = D_MODEL // RW_N
DECAY_LORA = 64
ICLR_LORA = 64
GATE_LORA = 128
GN_EPS = 64e-5

N_EXPERTS = 16
D_EXPERT = 1024
EC_CAPACITY = 2

kernel_name = "hybrid_diffusion_attnconv_rwkv7_ecmoe"

def _rms(t, g):
    tf = t.astype(jnp.float32)
    y = tf * lax.rsqrt(jnp.mean(tf * tf, axis=-1, keepdims=True) + NORM_EPS)
    return (y * g.astype(jnp.float32)).astype(t.dtype)

def _ada(t, g, shift, scale):
    return _rms(t, g) * (1.0 + scale) + shift

def _conv3(u, w):
    up = jnp.pad(u, ((0, 0), (1, 1), (0, 0)))
    return up[:, :-2] * w[0] + up[:, 1:-1] * w[1] + up[:, 2:] * w[2]

def _neighbour_mean(h):
    hp = jnp.pad(h, ((0, 0), (1, 1), (0, 0)))
    return 0.5 * (hp[:, :-2] + hp[:, 2:])

def _axial_rope(n):
    rows = n // GRID_W
    row = jnp.broadcast_to(jnp.arange(rows)[:, None], (rows, GRID_W)).reshape(-1).astype(jnp.float32)
    col = jnp.broadcast_to(jnp.arange(GRID_W)[None, :], (rows, GRID_W)).reshape(-1).astype(jnp.float32)
    inv = ROPE_THETA ** (-jnp.arange(ROPE_PAIRS_PER_AXIS, dtype=jnp.float32) / ROPE_PAIRS_PER_AXIS)
    ang = jnp.concatenate([row[:, None] * inv, col[:, None] * inv], axis=-1)
    return jnp.cos(ang), jnp.sin(ang)

def _rope(t, cos, sin):
    tf = t.astype(jnp.float32)
    half = HEAD_DIM // 2
    t1, t2 = tf[..., :half], tf[..., half:]
    c = cos[None, :, None, :]
    s = sin[None, :, None, :]
    return jnp.concatenate([t1 * c - t2 * s, t2 * c + t1 * s], axis=-1).astype(t.dtype)

def _attend(q, k, v):
    b, tq = q.shape[:2]
    qg = q.reshape(b, tq, N_KV_HEADS, Q_PER_KV, HEAD_DIM)
    s = jnp.einsum('bqhgd,bkhd->bhgqk', qg, k).astype(jnp.float32) * (HEAD_DIM ** -0.5)
    p = jax.nn.softmax(s, axis=-1).astype(v.dtype)
    o = jnp.einsum('bhgqk,bkhd->bqhgd', p, v)
    return o.reshape(b, tq, ATTN_W)

def _block_attention(q, k, v):
    b, n = q.shape[:2]
    nb = n // Q_BLOCK
    qb = jnp.moveaxis(q.reshape(b, nb, Q_BLOCK, N_Q_HEADS, HEAD_DIM), 1, 0)
    ob = lax.map(lambda qi: _attend(qi, k, v), qb)
    return jnp.moveaxis(ob, 0, 1).reshape(b, n, ATTN_W)

def _attn_conv_mixer(h, hc, w_in, w_out, q_g, k_g, conv_w, cos, sin, need_ctx):
    b, n, _ = h.shape
    lc = hc.shape[1]
    q, k, v, gb, gc, xc = jnp.split(h @ w_in, PROJ_SPLITS, axis=-1)
    q = _rope(_rms(q.reshape(b, n, N_Q_HEADS, HEAD_DIM), q_g), cos, sin)
    k = _rope(_rms(k.reshape(b, n, N_KV_HEADS, HEAD_DIM), k_g), cos, sin)
    v = v.reshape(b, n, N_KV_HEADS, HEAD_DIM)
    if need_ctx:
        qc, kc, vc, gbc, gcc, xcc = jnp.split(hc @ w_in, PROJ_SPLITS, axis=-1)
    else:
        kc, vc = jnp.split(hc @ w_in[:, ATTN_W:ATTN_W + 2 * KV_W], 2, axis=-1)
    kc = _rms(kc.reshape(b, lc, N_KV_HEADS, HEAD_DIM), k_g)
    vc = vc.reshape(b, lc, N_KV_HEADS, HEAD_DIM)
    k_all = jnp.concatenate([kc, k], axis=1)
    v_all = jnp.concatenate([vc, v], axis=1)
    o_attn = _block_attention(q, k_all, v_all)
    o_conv = gb * _conv3(gc * xc, conv_w)
    y = jnp.concatenate([o_attn, o_conv], axis=-1) @ w_out
    if not need_ctx:
        return y, None
    qc = _rms(qc.reshape(b, lc, N_Q_HEADS, HEAD_DIM), q_g)
    oc_attn = _attend(qc, kc, vc)
    oc_conv = gbc * _conv3(gcc * xcc, conv_w)
    yc = jnp.concatenate([oc_attn, oc_conv], axis=-1) @ w_out
    return y, yc

def _heads(t):
    return t.reshape(t.shape[:-1] + (RW_H, RW_N))

def _rwkv_features(h, mu, w_k, w_v, w0, w1, w2, a0, a1, a2, k_k, k_a):
    xx = _neighbour_mean(h) - h
    k = ((h + xx * mu[2]) @ w_k).astype(jnp.float32)
    v = ((h + xx * mu[3]) @ w_v).astype(jnp.float32)
    xw = h + xx * mu[1]
    xa = h + xx * mu[4]
    kk = _heads(k * k_k.astype(jnp.float32))
    kk = kk * lax.rsqrt(jnp.maximum(jnp.sum(kk * kk, axis=-1, keepdims=True), 1e-24))
    dirs = []
    for d in range(2):
        w_log = -jax.nn.softplus(-(w0[d] + jnp.tanh(xw @ w1[d]) @ w2[d]).astype(jnp.float32)) - 0.5
        a = jax.nn.sigmoid((a0[d] + (xa @ a1[d]) @ a2[d]).astype(jnp.float32))
        kd = k * (1.0 + (a - 1.0) * k_a.astype(jnp.float32))
        dirs.append((_heads(jnp.exp(-jnp.exp(w_log))), _heads(kd), _heads(a)))
    return xx, _heads(v), kk, dirs

def _rwkv_scan(s0, decay, kd, v, kk, a, r, reverse):
    emit = r is not None
    seq = (decay, kd, v, kk, a) + ((r,) if emit else ())
    seq = tuple(jnp.moveaxis(t, 1, 0) for t in seq)

    def step(s, inp):
        w_t, k_t, v_t, kk_t, a_t = inp[:5]
        s_kk = jnp.einsum('bhvk,bhk->bhv', s, kk_t)
        s = (s * w_t[:, :, None, :] - s_kk[..., None] * (kk_t * a_t)[:, :, None, :]
             + v_t[..., None] * k_t[:, :, None, :])
        y_t = jnp.einsum('bhvk,bhk->bhv', s, inp[5]) if emit else None
        return s, y_t

    s_final, ys = lax.scan(step, s0, seq, reverse=reverse)
    return s_final, (jnp.moveaxis(ys, 0, 1) if emit else None)

def _rwkv_readout(h, xx, y_fwd, y_bwd, r, v, kd_fwd, kd_bwd, mu_g, g1, g2, r_k, ln_w, ln_b, w_o):
    y = y_fwd + y_bwd
    mean = jnp.mean(y, axis=-1, keepdims=True)
    var = jnp.mean(jnp.square(y - mean), axis=-1, keepdims=True)
    y = ((y - mean) * lax.rsqrt(var + GN_EPS)).reshape(h.shape) * ln_w + ln_b
    rk = r_k.astype(jnp.float32)
    bonus = (jnp.sum(r * kd_fwd * rk, axis=-1, keepdims=True)
             + jnp.sum(r * kd_bwd * rk, axis=-1, keepdims=True)) * v
    g = jax.nn.sigmoid((h + xx * mu_g) @ g1) @ g2
    return ((y + bonus.reshape(h.shape)).astype(h.dtype) * g) @ w_o

def _rwkv_mixer(h, hc, mu, w_r, w_k, w_v, w_o, w0, w1, w2, a0, a1, a2, g1, g2,
                k_k, k_a, r_k, ln_w, ln_b, need_ctx):
    xx, v, kk, dirs = _rwkv_features(h, mu, w_k, w_v, w0, w1, w2, a0, a1, a2, k_k, k_a)
    xxc, vc, kkc, dirsc = _rwkv_features(hc, mu, w_k, w_v, w0, w1, w2, a0, a1, a2, k_k, k_a)
    r = _heads(((h + xx * mu[0]) @ w_r).astype(jnp.float32))
    rc = _heads(((hc + xxc * mu[0]) @ w_r).astype(jnp.float32)) if need_ctx else None
    s0 = jnp.zeros((h.shape[0], RW_H, RW_N, RW_N), jnp.float32)
    ys, ycs = [], []
    for d, reverse in enumerate((False, True)):
        dec, kd, a = dirs[d]
        decc, kdc, ac = dirsc[d]
        s_ctx, yc = _rwkv_scan(s0, decc, kdc, vc, kkc, ac, rc, reverse)
        _, y = _rwkv_scan(s_ctx, dec, kd, v, kk, a, r, reverse)
        ys.append(y)
        ycs.append(yc)
    out = _rwkv_readout(h, xx, ys[0], ys[1], r, v, dirs[0][1], dirs[1][1],
                        mu[5], g1, g2, r_k, ln_w, ln_b, w_o)
    if not need_ctx:
        return out, None
    out_c = _rwkv_readout(hc, xxc, ycs[0], ycs[1], rc, vc, dirsc[0][1], dirsc[1][1],
                          mu[5], g1, g2, r_k, ln_w, ln_b, w_o)
    return out, out_c

def _ec_moe(h, router, w_gate, w_up, w_down):
    b, n, d = h.shape
    cap = EC_CAPACITY * n // N_EXPERTS
    aff = jax.nn.softmax((h @ router).astype(jnp.float32), axis=-1)
    top_aff, top_idx = lax.top_k(jnp.swapaxes(aff, 1, 2), cap)
    xs = jax.vmap(lambda hb, ib: hb[ib])(h, top_idx)
    gate = jnp.einsum('becd,edf->becf', xs, w_gate)
    up = jnp.einsum('becd,edf->becf', xs, w_up)
    out = jnp.einsum('becf,efd->becd', jax.nn.silu(gate) * up, w_down)
    out = out * top_aff[..., None].astype(out.dtype)
    flat = (jnp.arange(b)[:, None, None] * n + top_idx).reshape(-1)
    y = jnp.zeros((b * n, d), out.dtype).at[flat].add(out.reshape(-1, d))
    return y.reshape(b, n, d)

def setup_inputs(seed: int = 0) -> dict:
    key = jax.random.key(seed)
    ks = iter(jax.random.split(key, 40))
    D = D_MODEL

    def nrm(shape, scale):
        return scale * jax.random.normal(next(ks), shape, jnp.float32)

    return {
        "x": nrm((BATCH, SEQ, D), 1.0),
        "c": nrm((BATCH, D), 1.0),
        "ctx": nrm((BATCH, CTX_LEN, D), 1.0),
        "c_ctx": nrm((D,), 1.0),
        "ada_w": nrm((DEPTH, D, 6 * D), 0.5 * D ** -0.5),
        "ada_b": nrm((DEPTH, 6 * D), 0.02),
        "norm_g": 1.0 + nrm((DEPTH, 2, D), 0.05),
        "final_g": 1.0 + nrm((D,), 0.05),
        "mix_w_in": nrm((N_EVEN, D, PROJ_W), D ** -0.5),
        "mix_w_out": nrm((N_EVEN, MIX_OUT_W, D), MIX_OUT_W ** -0.5),
        "q_norm_g": 1.0 + nrm((N_EVEN, HEAD_DIM), 0.05),
        "k_norm_g": 1.0 + nrm((N_EVEN, HEAD_DIM), 0.05),
        "conv_w": nrm((N_EVEN, CONV_TAPS, CONV_W), CONV_TAPS ** -0.5),
        "rw_mu": jax.random.uniform(next(ks), (N_ODD, 6, D), jnp.float32),
        "rw_w_r": nrm((N_ODD, D, D), D ** -0.5),
        "rw_w_k": nrm((N_ODD, D, D), D ** -0.5),
        "rw_w_v": nrm((N_ODD, D, D), D ** -0.5),
        "rw_w_o": nrm((N_ODD, D, D), D ** -0.5),
        "rw_w0": -1.0 + nrm((N_ODD, 2, D), 0.5),
        "rw_w1": nrm((N_ODD, 2, D, DECAY_LORA), D ** -0.5),
        "rw_w2": nrm((N_ODD, 2, DECAY_LORA, D), 0.5 * DECAY_LORA ** -0.5),
        "rw_a0": nrm((N_ODD, 2, D), 0.1),
        "rw_a1": nrm((N_ODD, 2, D, ICLR_LORA), D ** -0.5),
        "rw_a2": nrm((N_ODD, 2, ICLR_LORA, D), 0.5 * ICLR_LORA ** -0.5),
        "rw_g1": nrm((N_ODD, D, GATE_LORA), D ** -0.5),
        "rw_g2": nrm((N_ODD, GATE_LORA, D), GATE_LORA ** -0.5),
        "rw_k_k": 0.85 + nrm((N_ODD, D), 0.05),
        "rw_k_a": 1.0 + nrm((N_ODD, D), 0.05),
        "rw_r_k": nrm((N_ODD, RW_H, RW_N), 0.1),
        "rw_ln_w": 1.0 + nrm((N_ODD, D), 0.05),
        "rw_ln_b": nrm((N_ODD, D), 0.02),
        "moe_router": nrm((DEPTH, D, N_EXPERTS), D ** -0.5),
        "moe_w_gate": nrm((DEPTH, N_EXPERTS, D, D_EXPERT), D ** -0.5),
        "moe_w_up": nrm((DEPTH, N_EXPERTS, D, D_EXPERT), D ** -0.5),
        "moe_w_down": nrm((DEPTH, N_EXPERTS, D_EXPERT, D), D_EXPERT ** -0.5),
    }

def reference(x, c, ctx, c_ctx, ada_w, ada_b, norm_g, final_g,
              mix_w_in, mix_w_out, q_norm_g, k_norm_g, conv_w,
              rw_mu, rw_w_r, rw_w_k, rw_w_v, rw_w_o, rw_w0, rw_w1, rw_w2,
              rw_a0, rw_a1, rw_a2, rw_g1, rw_g2, rw_k_k, rw_k_a, rw_r_k, rw_ln_w, rw_ln_b,
              moe_router, moe_w_gate, moe_w_up, moe_w_down):
    n = x.shape[1]
    cos, sin = _axial_rope(n)
    for i in range(DEPTH):
        need_ctx = i < DEPTH - 1
        mod = jax.nn.silu(c) @ ada_w[i] + ada_b[i]
        mod_c = jax.nn.silu(c_ctx) @ ada_w[i] + ada_b[i]
        sh1, sc1, gt1, sh2, sc2, gt2 = jnp.split(mod[:, None, :], 6, axis=-1)
        sh1c, sc1c, gt1c, sh2c, sc2c, gt2c = jnp.split(mod_c, 6, axis=-1)

        h = _ada(x, norm_g[i, 0], sh1, sc1)
        hc = _ada(ctx, norm_g[i, 0], sh1c, sc1c)
        j = i // 2
        if i % 2 == 0:
            y, yc = _attn_conv_mixer(h, hc, mix_w_in[j], mix_w_out[j], q_norm_g[j], k_norm_g[j],
                                     conv_w[j], cos, sin, need_ctx)
        else:
            y, yc = _rwkv_mixer(h, hc, rw_mu[j], rw_w_r[j], rw_w_k[j], rw_w_v[j], rw_w_o[j],
                                rw_w0[j], rw_w1[j], rw_w2[j], rw_a0[j], rw_a1[j], rw_a2[j],
                                rw_g1[j], rw_g2[j], rw_k_k[j], rw_k_a[j], rw_r_k[j],
                                rw_ln_w[j], rw_ln_b[j], need_ctx)
        x = x + gt1 * y
        x = x + gt2 * _ec_moe(_ada(x, norm_g[i, 1], sh2, sc2),
                              moe_router[i], moe_w_gate[i], moe_w_up[i], moe_w_down[i])
        if need_ctx:
            ctx = ctx + gt1c * yc
            ctx = ctx + gt2c * _ec_moe(_ada(ctx, norm_g[i, 1], sh2c, sc2c),
                                       moe_router[i], moe_w_gate[i], moe_w_up[i], moe_w_down[i])
    return _rms(x, final_g)


_drawn_inputs = setup_inputs


def setup_inputs(seed=0):
    import zlib

    import numpy as np

    out = dict(_drawn_inputs(seed))
    spreads = {}
    factors = {'ctx': 3.758,
     'q_norm_g': 8.0,
     'k_norm_g': 8.0,
     'rw_w1': 4.286,
     'rw_w2': 4.242,
     'rw_a0': 6.779,
     'rw_k_k': 23.646,
     'rw_k_a': 5.003,
     'rw_ln_w': 6.87,
     'rw_ln_b': 27.728}
    for name, (base, spread) in spreads.items():
        noise = np.random.default_rng([zlib.crc32(name.encode()), seed]).standard_normal(out[name].shape)
        drawn = base * np.exp(spread * noise) if base else spread * noise
        out[name] = jnp.asarray(drawn.astype(out[name].dtype))
    for name, factor in factors.items():
        out[name] = (out[name] * factor).astype(out[name].dtype)
    return out
```

```python
from contextlib import ExitStack

import numpy as np

import concourse.bass as bass
from concourse import mybir

ALU = mybir.AluOpType
ACT = mybir.ActivationFunctionType
AX = mybir.AxisListType
F32 = mybir.dt.float32

P = 128
D = 1024
KD = D // P
CTX, LAT = 256, 512
TOK = CTX + LAT
NT = TOK // P
CT = CTX // P
DEPTH = 2
HD = 128
NQ, NKV = 8, 2
QPK = NQ // NKV
GRID_W = 64
E = 16
CAP_L, CAP_C = 2 * LAT // E, 2 * CTX // E
EPS = 1e-6
GN_EPS = 64e-5
NH = 64
CH = 64
NCOL = 6 * D // 512

LATR, CTXR = slice(CTX, TOK), slice(0, CTX)
RANGES = ((1, CTXR), (0, LATR))

VEC = {}
_at = 0
for _name, _n in (("c", KD), ("c_ctx", KD), ("ada_b", DEPTH * 6 * KD), ("norm_g", DEPTH * 2 * KD),
                  ("final_g", KD), ("conv_w", 3 * KD), ("mu", 6 * KD), ("w0", 2 * KD), ("a0", 2 * KD),
                  ("k_k", KD), ("k_a", KD), ("r_k", KD), ("ln_w", KD), ("ln_b", KD), ("q_g", 1), ("k_g", 1)):
    VEC[_name] = _at
    _at += _n
NVEC = _at

LEVELS = (2, 4, 8, 16, 32)
GROUPS = {
    "base": (("ident", P), ("ones", P), ("iota", 64)),
    "attn": (("swap", P), ("cos", LAT), ("sin", LAT)),
    "rwkv": (("heads", P), ("causal", 2 * 4 * P), ("first", 2 * P), ("level", 2 * len(LEVELS) * P),
             ("half", 2), ("start", TOK), ("end", TOK)),
}
CON, NCON = {}, {}
for _group, _names in GROUPS.items():
    _at = 0
    for _name, _n in _names:
        CON[_name] = (_group, _at)
        _at += _n
    NCON[_group] = _at


def constants():
    c = {g: np.zeros((P, n), np.float32) for g, n in NCON.items()}

    def put(name, a, at=0):
        g, o = CON[name]
        c[g][:, o + at:o + at + a.shape[1]] = a

    i = np.arange(P)
    put("ident", np.eye(P))
    put("ones", np.ones((P, P)))
    put("heads", (i[:, None] // NH == i[None] // NH) * 1.0)
    swap = np.zeros((P, P))
    swap[i[:64] + 64, i[:64]] = -1.0
    swap[i[:64], i[:64] + 64] = 1.0
    put("swap", swap)
    t = np.arange(LAT)
    n = HD // 4
    inv = (10000.0 ** (-np.arange(n, dtype=np.float32) / n)).astype(np.float32)
    ang = np.concatenate([(t // GRID_W).astype(np.float32)[:, None] * inv,
                          (t % GRID_W).astype(np.float32)[:, None] * inv], -1).T
    put("cos", np.concatenate([np.cos(ang)] * 2))
    put("sin", np.concatenate([np.sin(ang)] * 2))
    put("iota", np.broadcast_to(np.arange(64.0), (P, 64)))
    s, tt = i[:, None], i[None]
    same = s // CH == tt // CH
    for d in range(2):
        before = (s < tt) if d == 0 else (s > tt)
        for m in range(4):
            put("causal", same & (before | ((s == tt) & (m >= 2))), (4 * d + m) * P)
        put("first", same & before & (s // 2 == tt // 2), d * P)
        for j, b in enumerate(LEVELS):
            put("level", (s // (2 * b) == tt // (2 * b)) & before & (s // b != tt // b), (d * len(LEVELS) + j) * P)
    put("half", (i[:, None] // NH == np.arange(2)[None]) * 1.0)
    tok = np.arange(TOK)
    put("start", np.broadcast_to((tok % CH != 0) * 1.0, (P, TOK)))
    put("end", np.broadcast_to((tok % CH != CH - 1) * 1.0, (P, TOK)))
    return {"con_" + g: a for g, a in c.items()}


class Core:

    def __init__(self, nc, ctx):
        self.nc, self.ctx = nc, ctx
        self.sems, self.sem_scope = [], ExitStack()
        self.x = self.sb("x", [P, KD, TOK])
        self.h = self.sb("h", [P, KD, TOK])
        self.con = {"base": self.sb("con_base", [P, NCON["base"]])}
        self.vec = self.sb("vec", [P, NVEC])
        self.mod = self.sb("mod", [P, 2, DEPTH * 6 * KD])
        self.scale = self.sb("scale", [P, 2, DEPTH * 2 * KD])

    def sb(self, name, shape, ctx=None, dt=F32):
        return (ctx or self.ctx).enter_context(self.nc.sbuf_tensor(name, shape, dt))

    def hold(self, group, ctx):
        self.con[group] = self.sb("con_" + group, [P, NCON[group]], ctx)

    def ps(self, name, shape, ctx=None, dt=F32):
        return (ctx or self.ctx).enter_context(self.nc.psum_tensor(name, shape, dt))

    def sem(self, name):
        self.sems.append(self.sem_scope.enter_context(self.nc.semaphore(name)))
        return self.sems[-1]

    def clear_semaphores(self):
        used = self.sems
        with self.nc.Block() as block:
            @block.gpsimd
            def _(pool):
                for s in used:
                    pool.sem_clear(s)
        self.sem_scope.close()
        self.sems, self.sem_scope = [], ExitStack()

    def c(self, name, n=P, at=0):
        g, o = CON[name]
        return self.con[g][:, o + at:o + at + n]

    def v(self, name, j=0, n=1):
        return self.vec[:, VEC[name] + j:VEC[name] + j + n]

    def m(self, src, layer, which, k):
        j = (layer * 6 + which) * KD + k
        return self.mod[:, src, j:j + 1]


def modulation(K, A, mod_dram):
    nc, vec, mod, scale = K.nc, K.vec, K.mod, K.scale
    NB = 4
    with ExitStack() as ctx:
        w = [K.sb(f"ada_w{j}", [P, KD, 512], ctx) for j in range(NB)]
        sc = K.sb("silu_c", [P, KD, 2], ctx)
        row = K.sb("mod_row", [2, NB, 512], ctx)
        rows = K.sb("mod_rows", [DEPTH * 6 * KD, 2, P], ctx)
        pr = [K.ps(f"mod_p{j}", [2, 512], ctx) for j in range(NB)]
        pt = K.ps("mod_t", [P, 2, DEPTH * 6 * KD], ctx)
        small = K.sem("mod_small_loaded")
        w_ready = [K.sem(f"mod_w_ready{j}") for j in range(NB)]
        silu = K.sem("mod_silu_done")
        prod = [K.sem(f"mod_product_done{j}") for j in range(NB)]
        copied = [K.sem(f"mod_row_copied{j}") for j in range(NB)]
        stored = [K.sem(f"mod_row_stored{j}") for j in range(NB)]
        back = K.sem("mod_rows_loaded")
        turned = K.sem("mod_rows_turned")
        done = K.sem("mod_columns_done")
        n_it = DEPTH * NCOL // NB
        with nc.Block() as block:
            @block.sync
            def _(sp):
                sp.dma_start(vec[:], A["vecs"]).then_inc(small, 16)
                for g, t in K.con.items():
                    sp.dma_start(t[:], A["con_" + g]).then_inc(small, 16)
                for j in range(NB):
                    sp.dma_start(w[j][:], A["ada"][j]).then_inc(w_ready[j], 16)
                with sp.Fori(1, n_it) as i:
                    for j in range(NB):
                        sp.wait_ge(prod[j], i)
                        sp.dma_start(w[j][:], A["ada"][bass.ds(i * NB + j, 1)].rearrange("o p k n -> (o p) k n")
                                     ).then_inc(w_ready[j], 16)
                sp.dma_start(K.x[:], A["xT"]).then_inc(small, 16)
                for j in range(NB):
                    sp.wait_ge(stored[j], 16 * n_it)
                for s in range(2):
                    sp.dma_start(rows[:, s, :], mod_dram[s].rearrange("c (b p) -> (c b) p", p=P)).then_inc(back, 16)
                sp.wait_ge(small, 16 * (2 + len(K.con)))

            @block.scalar
            def _(act):
                act.wait_ge(small, 16 * (1 + len(K.con)))
                for s, name in enumerate(("c", "c_ctx")):
                    nc.scalar.activation(sc[:, :, s], K.v(name, 0, KD), ACT.Silu).then_inc(silu, 1)
                with act.Fori(0, n_it) as i:
                    for j in range(NB):
                        act.wait_ge(copied[j], i + 1)
                        act.dma_start(mod_dram[:, bass.ds(i * NB + j, 1), :], row[:, j:j + 1, :]
                                      ).then_inc(stored[j], 16)

            @block.tensor
            def _(pe):
                pe.wait_ge(silu, 2)
                with pe.Fori(0, n_it) as i:
                    for j in range(NB):
                        pe.wait_ge(w_ready[j], 16 * i + 16)
                        pe.wait_ge(copied[j], i)
                        for k in range(KD):
                            last = nc.tensor.matmul(pr[j][:], sc[:, k, :], w[j][:, k, :], start=k == 0, stop=k == KD - 1)
                        last.then_inc(prod[j], 1)
                pe.wait_ge(back, 32)
                n = DEPTH * 6 * KD
                for s in range(2):
                    last = nc.tensor.transpose(pt[:, s, :], rows[:, s, :], K.c("ident")[0:n, 0:n])
                last.then_inc(turned, 1)

            @block.vector
            def _(dve):
                with dve.Fori(0, n_it) as i:
                    for j in range(NB):
                        dve.wait_ge(prod[j], i + 1)
                        dve.wait_ge(stored[j], 16 * i)
                        nc.vector.tensor_copy(row[:, j, :], pr[j][:]).then_inc(copied[j], 1)
                dve.wait_ge(turned, 1)
                n = DEPTH * 6 * KD
                for s in range(2):
                    nc.vector.tensor_tensor(mod[:, s, :], pt[:, s, :], K.v("ada_b", 0, n), ALU.add).then_inc(done, 1)
                dve.wait_ge(done, 2)
                for s in range(2):
                    for l in range(DEPTH):
                        for j in range(2):
                            at = (l * 6 + 3 * j + 1) * KD
                            o = (l * 2 + j) * KD
                            last = nc.vector.scalar_tensor_tensor(out=scale[:, s, o:o + KD], in0=mod[:, s, at:at + KD],
                                                                  scalar=1.0, in1=K.v("norm_g", o, KD),
                                                                  op0=ALU.add, op1=ALU.mult)


def norm(K, tag, layer, sub, final=None):
    nc, x, h = K.nc, K.x, K.h
    with ExitStack() as ctx:
        sq = K.sb(f"{tag}_sq", [P, KD, TOK], ctx)
        ms = K.sb(f"{tag}_ms", [P, TOK], ctx)
        rstd = K.sb(f"{tag}_rstd", [P, TOK], ctx)
        ps = K.ps(f"{tag}_ps", [P, 1024], ctx)
        squared = K.sem(f"{tag}_squared")
        summed = K.sem(f"{tag}_summed")
        mean = K.sem(f"{tag}_mean")
        rooted = K.sem(f"{tag}_rooted")
        inv = K.sem(f"{tag}_inverse")
        scaled = K.sem(f"{tag}_scaled")
        stored = K.sem(f"{tag}_stored")
        spans = ((LATR, slice(0, LAT)), (CTXR, slice(512, 512 + CTX)))
        with nc.Block() as block:
            @block.scalar
            def _(act):
                for k in range(KD):
                    nc.scalar.activation(sq[:, k, :], x[:, k, :], ACT.Square).then_inc(squared, 1)
                act.wait_ge(mean, 2)
                nc.scalar.activation(rstd[:], ms[:], ACT.Sqrt).then_inc(rooted, 1)
                if final is None:
                    for k in range(KD):
                        act.wait_ge(scaled, 2 * k + 2)
                        for s, r in RANGES:
                            nc.scalar.activation(h[:, k, r], h[:, k, r], ACT.Identity,
                                                 bias=K.m(s, layer, 3 * sub, k))

            @block.tensor
            def _(pe):
                for k in range(KD):
                    pe.wait_ge(squared, k + 1)
                    for r, b in spans:
                        last = nc.tensor.matmul(ps[:, b], K.c("ones"), sq[:, k, r], start=k == 0, stop=k == KD - 1)
                last.then_inc(summed, 1)

            @block.vector
            def _(dve):
                dve.wait_ge(summed, 1)
                for r, b in spans:
                    nc.vector.tensor_scalar(ms[:, r], ps[:, b], 1.0 / D, EPS, ALU.mult, ALU.add).then_inc(mean, 1)
                dve.wait_ge(rooted, 1)
                nc.vector.reciprocal(ms[:], rstd[:]).then_inc(inv, 1)
                dve.wait_ge(inv, 1)
                for k in range(KD):
                    if final is not None:
                        nc.vector.scalar_tensor_tensor(out=h[:, k, LATR], in0=x[:, k, LATR], scalar=K.v("final_g", k),
                                                       in1=ms[:, LATR], op0=ALU.mult, op1=ALU.mult).then_inc(scaled, 1)
                        continue
                    for s, r in RANGES:
                        o = (layer * 2 + sub) * KD + k
                        nc.vector.scalar_tensor_tensor(out=h[:, k, r], in0=x[:, k, r], scalar=K.scale[:, s, o:o + 1],
                                                       in1=ms[:, r], op0=ALU.mult, op1=ALU.mult).then_inc(scaled, 1)

            if final is not None:
                @block.sync
                def _(sp):
                    for k in range(KD):
                        sp.wait_ge(scaled, k + 1)
                        sp.dma_start(final[:, k, :], h[:, k, LATR]).then_inc(stored, 16)
                    sp.wait_ge(stored, 16 * KD)


def project_qk(K, A, qk):
    nc, h = K.nc, K.h
    with ExitStack() as ctx:
        w = [K.sb(f"qk_w{j}", [P, KD, P], ctx) for j in range(2)]
        g = K.sb("qk_g", [P, NQ + NKV], ctx)
        sq = [K.sb(f"qk_sq{j}", [P, TOK], ctx) for j in range(2)]
        ms = [K.sb(f"qk_ms{j}", [P, TOK], ctx) for j in range(2)]
        rt = [K.sb(f"qk_rt{j}", [P, TOK], ctx) for j in range(2)]
        qn = [K.sb(f"qk_qn{j}", [P, TOK], ctx) for j in range(2)]
        qc = [K.sb(f"qk_cos{j}", [P, LAT], ctx) for j in range(2)]
        qs = [K.sb(f"qk_sin{j}", [P, LAT], ctx) for j in range(2)]
        raw = [K.ps(f"qk_raw{j}", [P, 1024], ctx) for j in range(2)]
        ss = K.ps("qk_ss", [P, 1024], ctx)
        rot = [K.ps(f"qk_rot{j}", [P, LAT], ctx) for j in range(2)]
        sems = {n: [K.sem(f"qk_{n}{j}") for j in range(2)] for n in
                ("w_ready", "proj_lat", "proj", "squared", "summed", "mean", "rooted", "inverse", "normed",
                 "swapped", "cosed", "sined", "written", "ctx_copied")}
        gains = K.sem("qk_gains")
        n_it = (NQ + NKV) // 2
        spans = ((LATR, slice(0, LAT)), (CTXR, slice(512, 512 + CTX)))
        S = lambda n, j: sems[n][j]
        with nc.Block() as block:
            @block.sync
            def _(sp):
                for j in range(2):
                    sp.dma_start(w[j][:], A["w_in"][j]).then_inc(S("w_ready", j), 16)
                with sp.Fori(1, n_it) as i:
                    for j in range(2):
                        sp.wait_ge(S("proj", j), i)
                        sp.dma_start(w[j][:], A["w_in"][bass.ds(2 * i + j, 1)].rearrange("o p k n -> (o p) k n")
                                     ).then_inc(S("w_ready", j), 16)

            @block.tensor
            def _(pe):
                def project(i, j):
                    pe.wait_ge(S("w_ready", j), 16 * i + 16)
                    pe.wait_ge(S("normed", j), 2 * i)
                    for r, b in spans:
                        for k in range(KD):
                            last = nc.tensor.matmul(raw[j][:, b], w[j][:, k, :], h[:, k, r], start=k == 0, stop=k == KD - 1)
                        last.then_inc(S("proj_lat" if r is LATR else "proj", j), 1)

                def sums(i, j):
                    pe.wait_ge(S("mean", 1 - j), 2 * i + 2 * j)
                    for n, (r, b) in enumerate(spans):
                        pe.wait_ge(S("squared", j), 2 * i + 1 + n)
                        last = nc.tensor.matmul(ss[:, b], K.c("ones"), sq[j][:, r], start=True, stop=True)
                    last.then_inc(S("summed", j), 1)

                def swap(i, j):
                    pe.wait_ge(S("normed", j), 2 * i + 2)
                    pe.wait_ge(S("sined", j), i)
                    nc.tensor.matmul(rot[j][:], K.c("swap"), qn[j][:, LATR], start=True, stop=True
                                     ).then_inc(S("swapped", j), 1)

                with pe.Fori(0, n_it) as i:
                    project(i, 0)
                    sums(i, 0)
                    project(i, 1)
                    swap(i, 0)
                    sums(i, 1)
                    swap(i, 1)

            @block.scalar
            def _(act):
                with act.Fori(0, n_it) as i:
                    for j in range(2):
                        act.wait_ge(S("summed", j), i)
                        for n, (r, b) in enumerate(spans):
                            act.wait_ge(S("proj_lat" if n == 0 else "proj", j), i + 1)
                            nc.scalar.activation(sq[j][:, r], raw[j][:, b], ACT.Square).then_inc(S("squared", j), 1)
                        act.wait_ge(S("mean", j), 2 * i + 2)
                        act.wait_ge(S("inverse", j), i)
                        nc.scalar.activation(rt[j][:], ms[j][:], ACT.Sqrt).then_inc(S("rooted", j), 1)

            @block.vector
            def _(dve):
                for n in range(NQ + NKV):
                    nc.vector.tensor_copy(g[:, n:n + 1], K.v("q_g" if n < NQ else "k_g")).then_inc(gains, 1)
                dve.wait_ge(gains, NQ + NKV)
                with dve.Fori(0, n_it) as i:
                    for j in range(2):
                        dve.wait_ge(S("summed", j), i + 1)
                        for r, b in spans:
                            nc.vector.tensor_scalar(ms[j][:, r], ss[:, b], 1.0 / HD, EPS, ALU.mult, ALU.add
                                                    ).then_inc(S("mean", j), 1)
                        dve.wait_ge(S("rooted", j), i + 1)
                        nc.vector.reciprocal(ms[j][:], rt[j][:]).then_inc(S("inverse", j), 1)
                        dve.wait_ge(S("inverse", j), i + 1)
                        dve.wait_ge(S("cosed", j), i)
                        dve.wait_ge(S("ctx_copied", j), i)
                        for r, b in spans:
                            nc.vector.scalar_tensor_tensor(out=qn[j][:, r], in0=raw[j][:, b], scalar=g[:, bass.ds(2 * i + j, 1)],
                                                           in1=ms[j][:, r], op0=ALU.mult, op1=ALU.mult
                                                           ).then_inc(S("normed", j), 1)
                        dve.wait_ge(S("swapped", j), i + 1)
                        dve.wait_ge(S("written", j), i)
                        nc.vector.tensor_tensor(qs[j][:], rot[j][:], K.c("sin", LAT), ALU.mult).then_inc(S("sined", j), 1)

            @block.gpsimd
            def _(pool):
                with pool.Fori(0, n_it) as i:
                    for j in range(2):
                        pool.wait_ge(S("normed", j), 2 * i + 2)
                        pool.wait_ge(S("written", j), i)
                        nc.gpsimd.tensor_tensor(qc[j][:], qn[j][:, LATR], K.c("cos", LAT), ALU.mult).then_inc(S("cosed", j), 1)
                        head = qk[:, bass.ds(2 * i + j, 1), :].rearrange("p o t -> p (o t)")
                        nc.gpsimd.tensor_copy(head[:, CTXR], qn[j][:, CTXR]).then_inc(S("ctx_copied", j), 1)
                        pool.wait_ge(S("cosed", j), i + 1)
                        pool.wait_ge(S("sined", j), i + 1)
                        nc.gpsimd.tensor_tensor(head[:, LATR], qc[j][:], qs[j][:], ALU.add).then_inc(S("written", j), 1)


def project_v_conv(K, A, v, o):
    nc, h = K.nc, K.h
    with ExitStack() as ctx:
        wv = K.sb("v_w", [P, NKV, KD, P], ctx)
        w = [[K.sb(f"conv_w{j}_{m}", [P, KD, P], ctx) for m in range(3)] for j in range(2)]
        PADC, PADL = 1, CTX + 3
        gc = [K.sb(f"conv_gc{j}", [P, TOK], ctx) for j in range(2)]
        u = [K.sb(f"conv_u{j}", [P, TOK + 4], ctx) for j in range(2)]
        y = [K.sb(f"conv_y{j}", [P, TOK], ctx) for j in range(2)]
        pv = [K.ps(f"v_p{j}", [P, 512], ctx) for j in range(2)]
        pg = [K.ps(f"conv_p{m}", [P, 1024], ctx) for m in range(3)]
        wv_ready, v_prod, v_out, zeroed = (K.sem(f"v_{n}") for n in ("w_ready", "product", "copied", "pads_zeroed"))
        sems = {n: [K.sem(f"conv_{n}{j}") for j in range(2)] for n in
                ("w_ready", "copied", "gated", "mid", "left", "right", "written")}
        prod = [K.sem(f"conv_product{m}") for m in range(3)]
        S = lambda n, j: sems[n][j]
        spans = ((LATR, slice(0, LAT)), (CTXR, slice(512, 512 + CTX)))
        segs = ((LATR, PADL, slice(0, LAT)), (CTXR, PADC, slice(512, 512 + CTX)))
        FIRST = (28, 20, 12)
        ORDER = (1, 0, 2)
        n_it = KD // 2
        VCH = NQ + NKV

        def col(name, c):
            return K.vec[:, bass.ds(c + VEC[name], 1)]

        with nc.Block() as block:
            @block.sync
            def _(sp):
                for m in range(NKV):
                    sp.dma_start(wv[:, m], A["w_in"][VCH + m]).then_inc(wv_ready, 16)
                with sp.Fori(0, n_it) as i:
                    for j in range(2):
                        sp.wait_ge(prod[2], 2 * i if j == 0 else 2 * i)
                        if j == 1:
                            sp.wait_ge(S("written", 1), i)
                        else:
                            sp.wait_ge(S("written", 0), i)
                        for m in ORDER:
                            sp.dma_start(w[j][m][:], A["w_in"][bass.ds(2 * i + j + FIRST[m], 1)].rearrange("o p k n -> (o p) k n")
                                         ).then_inc(S("w_ready", j), 16)

            @block.tensor
            def _(pe):
                pe.wait_ge(wv_ready, 16 * NKV)
                for t in range(NT):
                    if t >= 2:
                        pe.wait_ge(v_out, t - 1)
                    for m in range(NKV):
                        for k in range(KD):
                            last = nc.tensor.matmul(pv[t % 2][:, m * P:(m + 1) * P], h[:, k, t * P:(t + 1) * P], wv[:, m, k, :],
                                                    start=k == 0, stop=k == KD - 1)
                    last.then_inc(v_prod, 1)
                with pe.Fori(0, n_it) as i:
                    for j in range(2):
                        pe.wait_ge(S("w_ready", j), 48 * i + 48)
                        for m in ORDER:
                            if j == 1:
                                pe.wait_ge(S(("gated", "copied", "written")[m], 0), (2, 2, 1)[m] * (i + 1))
                            else:
                                pe.wait_ge(S(("gated", "copied", "written")[m], 1), (2, 2, 1)[m] * i)
                            for r, b in spans:
                                for k in range(KD):
                                    last = nc.tensor.matmul(pg[m][:, b], w[j][m][:, k, :], h[:, k, r], start=k == 0, stop=k == KD - 1)
                            last.then_inc(prod[m], 1)

            @block.scalar
            def _(act):
                for t in range(NT):
                    act.wait_ge(v_prod, t + 1)
                    nc.scalar.activation(v[:, t, :], pv[t % 2][:, 0:NKV * P], ACT.Copy).then_inc(v_out, 1)
                with act.Fori(0, n_it) as i:
                    for j in range(2):
                        act.wait_ge(prod[1], 2 * i + j + 1)
                        act.wait_ge(S("gated", j), 2 * i)
                        for r, b in spans:
                            nc.scalar.activation(gc[j][:, r], pg[1][:, b], ACT.Copy).then_inc(S("copied", j), 1)

            @block.vector
            def _(dve):
                for j in range(2):
                    nc.vector.memset(u[j][:], 0.0).then_inc(zeroed, 1)
                dve.wait_ge(zeroed, 2)
                with dve.Fori(0, n_it) as i:
                    for j in range(2):
                        c = 2 * i + j
                        dve.wait_ge(prod[0], 2 * i + j + 1)
                        dve.wait_ge(S("copied", j), 2 * i + 2)
                        dve.wait_ge(S("written", j), i)
                        for r, at, b in segs:
                            n = r.stop - r.start
                            nc.vector.tensor_tensor(u[j][:, at:at + n], pg[0][:, b], gc[j][:, r], ALU.mult
                                                    ).then_inc(S("gated", j), 1)
                        dve.wait_ge(S("gated", j), 2 * i + 2)
                        for r, at, b in segs:
                            n = r.stop - r.start
                            nc.vector.tensor_scalar(y[j][:, r], u[j][:, at:at + n], col("conv_w", c + KD), None, ALU.mult
                                                    ).then_inc(S("mid", j), 1)
                        dve.wait_ge(S("mid", j), 2 * i + 2)
                        for r, at, b in segs:
                            n = r.stop - r.start
                            nc.vector.scalar_tensor_tensor(out=y[j][:, r], in0=u[j][:, at - 1:at - 1 + n], scalar=col("conv_w", c),
                                                           in1=y[j][:, r], op0=ALU.mult, op1=ALU.add).then_inc(S("left", j), 1)
                        dve.wait_ge(S("left", j), 2 * i + 2)
                        for r, at, b in segs:
                            n = r.stop - r.start
                            nc.vector.scalar_tensor_tensor(out=y[j][:, r], in0=u[j][:, at + 1:at + 1 + n], scalar=col("conv_w", c + 2 * KD),
                                                           in1=y[j][:, r], op0=ALU.mult, op1=ALU.add).then_inc(S("right", j), 1)
                        dve.wait_ge(S("right", j), 2 * i + 2)
                        dve.wait_ge(prod[2], 2 * i + j + 1)
                        dst = o[:, bass.ds(c + NQ, 1), :].rearrange("p o t -> p (o t)")
                        for r, at, b in segs:
                            op = nc.vector.tensor_tensor(dst[:, r], pg[2][:, b], y[j][:, r], ALU.mult)
                        op.then_inc(S("written", j), 1)


def attend(K, qk, v, o):
    nc = K.nc
    SCALE = HD ** -0.5
    TILES = [(kv, t, NT if t >= CT else CT) for kv in range(NKV) for t in list(range(CT, NT)) + list(range(CT))]
    n_tiles = len(TILES)
    half = n_tiles // 2
    with ExitStack() as ctx:
        qs = [K.sb(f"at_q{kv}", [P, TOK], ctx) for kv in range(NKV)]
        p = [K.sb(f"at_p{j}", [P, TOK], ctx) for j in range(2)]
        mx = [K.sb(f"at_max{j}", [P, 1], ctx) for j in range(2)]
        sm = [K.sb(f"at_sum{j}", [P, 1], ctx) for j in range(2)]
        rc = [K.sb(f"at_rec{j}", [P, 1], ctx) for j in range(2)]
        nb = [K.sb(f"at_bias{j}", [P, 1], ctx) for j in range(2)]
        ptl = [K.sb(f"at_ptl{kv}", [P, NT, LAT], ctx) for kv in range(NKV)]
        ptc = [K.sb(f"at_ptc{kv}", [P, CT, CTX], ctx) for kv in range(NKV)]
        sc = [K.ps(f"at_s{j}", [P, 1024], ctx) for j in range(2)]
        tr = K.ps("at_t", [P, 1024], ctx)
        po = K.ps("at_o", [P, 1024], ctx)
        per = {n: [K.sem(f"at_{n}{j}") for j in range(2)] for n in
               ("scored", "maxed", "biased", "exped", "summed", "scaled", "turned", "copied_a", "copied_v")}
        staged = [K.sem(f"at_staged{kv}") for kv in range(NKV)]
        summed_up = [K.sem(f"at_weighed{kv}") for kv in range(NKV)]
        out = [K.sem(f"at_out{kv}") for kv in range(NKV)]
        S = lambda n, j: per[n][j]
        with nc.Block() as block:
            @block.gpsimd
            def _(pool):
                with pool.Fori(0, QPK) as g:
                    for kv in range(NKV):
                        pool.wait_ge(summed_up[kv], g)
                        nc.gpsimd.tensor_copy(qs[kv][:], qk[:, bass.ds(g + kv * QPK, 1), :].rearrange("p o t -> p (o t)")
                                              ).then_inc(staged[kv], 1)

            @block.tensor
            def _(pe):
                def scores(g, n):
                    kv, t, keys = TILES[n]
                    j = n % 2
                    pe.wait_ge(staged[kv], g + 1)
                    pe.wait_ge(S("exped", j), half * g + n // 2)
                    last = nc.tensor.matmul(sc[j][:, 0:min(keys * P, 512)], qs[kv][:, t * P:(t + 1) * P],
                                            qk[:, NQ + kv, 0:min(keys * P, 512)], start=True, stop=True)
                    if keys > 4:
                        last = nc.tensor.matmul(sc[j][:, 512:keys * P], qs[kv][:, t * P:(t + 1) * P],
                                                qk[:, NQ + kv, 512:keys * P], start=True, stop=True)
                    last.then_inc(S("scored", j), 1)

                def turn(g, n):
                    kv, t, keys = TILES[n]
                    j = n % 2
                    pe.wait_ge(S("scaled", j), half * g + n // 2 + 1)
                    m = (half * g + n // 2 + (0 if j == 0 else 1))
                    pe.wait_ge(S("copied_a", 1 - j), m)
                    pe.wait_ge(S("copied_v", 1 - j), m)
                    for b in range(keys):
                        at = b * P if b < keys // 2 else 512 + (b - keys // 2) * P
                        last = nc.tensor.transpose(tr[:, at:at + P], p[j][:, b * P:(b + 1) * P], K.c("ident"))
                    last.then_inc(S("turned", j), 1)

                def weigh(g, kv):
                    for j in range(2):
                        m = half * g + (kv + 1) * half // 2
                        pe.wait_ge(S("copied_a", j), m)
                        pe.wait_ge(S("copied_v", j), m)
                    if kv == 1:
                        pe.wait_ge(out[0], 2 * g + 2)
                    else:
                        pe.wait_ge(out[1], 2 * g)
                    for b in range(NT):
                        nc.tensor.matmul(po[:, 0:LAT], v[:, b, kv * HD:(kv + 1) * HD], ptl[kv][:, b, :], start=b == 0, stop=b == NT - 1)
                    for b in range(CT):
                        last = nc.tensor.matmul(po[:, 512:512 + CTX], v[:, b, kv * HD:(kv + 1) * HD], ptc[kv][:, b, :],
                                                start=b == 0, stop=b == CT - 1)
                    last.then_inc(summed_up[kv], 1)

                with pe.Fori(0, QPK) as g:
                    scores(g, 0)
                    for n in range(n_tiles):
                        if n + 1 < n_tiles:
                            scores(g, n + 1)
                        turn(g, n)
                        if n == half:
                            weigh(g, 0)
                    weigh(g, 1)

            @block.vector
            def _(dve):
                def tile(g, n):
                    kv, t, keys = TILES[n]
                    j = n % 2
                    m = half * g + n // 2
                    dve.wait_ge(S("scored", j), m + 1)
                    dve.wait_ge(S("biased", j), m)
                    nc.vector.tensor_reduce(mx[j][:], sc[j][:, 0:keys * P], AX.X, ALU.max).then_inc(S("maxed", j), 1)

                def scale(g, n):
                    kv, t, keys = TILES[n]
                    j = n % 2
                    m = half * g + n // 2
                    dve.wait_ge(S("exped", j), m + 1)
                    nc.vector.reciprocal(rc[j][:], sm[j][:]).then_inc(S("summed", j), 1)
                    dve.wait_ge(S("summed", j), m + 1)
                    nc.vector.tensor_scalar(p[j][:, 0:keys * P], p[j][:, 0:keys * P], rc[j][:], None, ALU.mult
                                            ).then_inc(S("scaled", j), 1)

                def copy(g, n):
                    kv, t, keys = TILES[n]
                    j = n % 2
                    m = half * g + n // 2
                    dve.wait_ge(S("turned", j), m + 1)
                    dve.wait_ge(summed_up[kv], g)
                    lo = keys // 2
                    dst = ptl[kv][:, lo:keys, (t - CT) * P:(t - CT + 1) * P] if t >= CT else ptc[kv][:, lo:keys, t * P:(t + 1) * P]
                    nc.vector.tensor_copy(dst, tr[:, 512:512 + (keys - lo) * P].rearrange("p (b q) -> p b q", q=P)
                                          ).then_inc(S("copied_v", j), 1)

                def store(g, kv):
                    dve.wait_ge(summed_up[kv], g + 1)
                    dst = o[:, bass.ds(g + kv * QPK, 1), :].rearrange("p o t -> p (o t)")
                    nc.vector.tensor_copy(dst[:, LATR], po[:, 0:LAT]).then_inc(out[kv], 1)
                    nc.vector.tensor_copy(dst[:, CTXR], po[:, 512:512 + CTX]).then_inc(out[kv], 1)

                with dve.Fori(0, QPK) as g:
                    tile(g, 0)
                    for n in range(n_tiles):
                        scale(g, n)
                        if n + 1 < n_tiles:
                            tile(g, n + 1)
                        copy(g, n)
                        if n == half + 1:
                            store(g, 0)
                    store(g, 1)

            @block.scalar
            def _(act):
                def exps(g, n):
                    kv, t, keys = TILES[n]
                    j = n % 2
                    m = half * g + n // 2
                    act.wait_ge(S("maxed", j), m + 1)
                    act.wait_ge(S("exped", j), m)
                    nc.scalar.mul(nb[j][:], mx[j][:], -SCALE).then_inc(S("biased", j), 1)
                    act.wait_ge(S("biased", j), m + 1)
                    act.wait_ge(S("turned", j), m)
                    act.wait_ge(S("summed", j), m)
                    nc.scalar.activation(p[j][:, 0:keys * P], sc[j][:, 0:keys * P], ACT.Exp, bias=nb[j][:], scale=SCALE,
                                         accum_out=sm[j][:]).then_inc(S("exped", j), 1)

                def copy(g, n):
                    kv, t, keys = TILES[n]
                    j = n % 2
                    m = half * g + n // 2
                    act.wait_ge(S("turned", j), m + 1)
                    act.wait_ge(summed_up[kv], g)
                    hi = keys // 2
                    dst = ptl[kv][:, 0:hi, (t - CT) * P:(t - CT + 1) * P] if t >= CT else ptc[kv][:, 0:hi, t * P:(t + 1) * P]
                    nc.scalar.activation(dst, tr[:, 0:hi * P].rearrange("p (b q) -> p b q", q=P), ACT.Copy
                                         ).then_inc(S("copied_a", j), 1)

                with act.Fori(0, QPK) as g:
                    exps(g, 0)
                    for n in range(n_tiles):
                        if n + 1 < n_tiles:
                            exps(g, n + 1)
                        copy(g, n)


def project_out(K, tag, weights, o, chunks, layer, ranges, spilled=None):
    nc, x = K.nc, K.x
    with ExitStack() as ctx:
        w = [K.sb(f"{tag}_w{j}", [P, chunks, P], ctx) for j in range(2)]
        ps = [K.ps(f"{tag}_p{j}", [P, 1024], ctx) for j in range(2)]
        w_ready = [K.sem(f"{tag}_w_ready{j}") for j in range(2)]
        prod = [K.sem(f"{tag}_product{j}") for j in range(2)]
        added = [K.sem(f"{tag}_added{j}") for j in range(2)]
        x_back = K.sem(f"{tag}_x_back")
        bank = {0: slice(0, LAT), 1: slice(512, 512 + CTX)}
        n_it = KD // 2
        with nc.Block() as block:
            @block.sync
            def _(sp):
                if spilled is not None:
                    sp.dma_start(x[:], spilled).then_inc(x_back, 16)
                with sp.Fori(0, n_it) as i:
                    for j in range(2):
                        sp.wait_ge(prod[j], i)
                        sp.dma_start(w[j][:], weights[bass.ds(2 * i + j, 1)].rearrange("o p k n -> (o p) k n")
                                     ).then_inc(w_ready[j], 16)

            @block.tensor
            def _(pe):
                with pe.Fori(0, n_it) as i:
                    for j in range(2):
                        pe.wait_ge(w_ready[j], 16 * i + 16)
                        pe.wait_ge(added[j], len(ranges) * i)
                        for s, r in ranges:
                            ro = slice(r.start - TOK + o.shape[2], r.stop - TOK + o.shape[2])
                            for k in range(chunks):
                                last = nc.tensor.matmul(ps[j][:, bank[s]], w[j][:, k, :], o[:, k, ro], start=k == 0, stop=k == chunks - 1)
                        last.then_inc(prod[j], 1)

            @block.vector
            def _(dve):
                if spilled is not None:
                    dve.wait_ge(x_back, 16)
                with dve.Fori(0, n_it) as i:
                    for j in range(2):
                        dve.wait_ge(prod[j], i + 1)
                        xs = x[:, bass.ds(2 * i + j, 1), :].rearrange("p o t -> p (o t)")
                        for s, r in ranges:
                            gate = K.mod[:, s, bass.ds(2 * i + j + (layer * 6 + 2) * KD, 1)]
                            nc.vector.scalar_tensor_tensor(out=xs[:, r], in0=ps[j][:, bank[s]], scalar=gate, in1=xs[:, r],
                                                           op0=ALU.mult, op1=ALU.add).then_inc(added[j], 1)


def route(K, A, tag, layer, h2, slot, aff):
    nc, h = K.nc, K.h
    ctx_too = layer == 0
    tiles = list(range(0 if ctx_too else CT, NT))
    t0 = tiles[0]
    n = len(tiles)
    kinds = [(LATR, slice(0, LAT), CAP_L)] + ([(CTXR, slice(512, 512 + CTX), CAP_C)] if ctx_too else [])
    at = lambda t: (t - CT) * P if t >= CT else 512 + t * P
    with ExitStack() as ctx:
        rw = K.sb(f"{tag}_router", [P, KD, E], ctx)
        lg = K.sb(f"{tag}_logits", [E, TOK], ctx)
        ex = K.sb(f"{tag}_ex", [P, n, E], ctx)
        mx = K.sb(f"{tag}_mx", [P, n], ctx)
        rs = K.sb(f"{tag}_rs", [P, n], ctx)
        rr = K.sb(f"{tag}_rr", [P, n], ctx)
        work = K.sb(f"{tag}_work", [E, TOK], ctx)
        top = K.sb(f"{tag}_top", [E, 8], ctx)
        ones = K.sb(f"{tag}_ones", [E, TOK], ctx)
        cnt = K.sb(f"{tag}_cnt", [E, TOK], ctx)
        pl = K.ps(f"{tag}_pl", [E, 1024], ctx)
        pt = K.ps(f"{tag}_pt", [P, 512], ctx)
        pa = K.ps(f"{tag}_pa", [E, 1024], ctx)
        ph = [K.ps(f"{tag}_ph{j}", [P, 512], ctx) for j in range(2)]
        (loaded, logits, copied, turned, maxed, shifted, exped, summed, inv, affs, aff_turned, worked, found, replaced,
         picked, counted, placed, slot_turned) = (K.sem(f"{tag}_{x}") for x in (
             "router_loaded", "logits", "logits_copied", "logits_turned", "max", "shifted", "exped", "summed", "inverse",
             "affinity", "affinity_turned", "work", "top", "replaced", "picked", "counted", "placed", "slot_turned"))
        h_turned = [K.sem(f"{tag}_h_turned{j}") for j in range(2)]
        h_copied = [K.sem(f"{tag}_h_copied{j}") for j in range(2)]
        groups = [(t, g) for t in tiles for g in range(KD // 4)]
        with nc.Block() as block:
            @block.sync
            def _(sp):
                sp.dma_start(rw[:], A["router"][layer]).then_inc(loaded, 16)

            @block.tensor
            def _(pe):
                pe.wait_ge(loaded, 16)
                for r, b, _ in kinds:
                    for k in range(KD):
                        last = nc.tensor.matmul(pl[:, b], rw[:, k, :], h[:, k, r], start=k == 0, stop=k == KD - 1)
                last.then_inc(logits, 1)

                def turn_h(lo, hi):
                    for m in range(lo, hi):
                        t, g = groups[m]
                        if m >= 2:
                            pe.wait_ge(h_copied[m % 2], m // 2)
                        for k in range(4):
                            last = nc.tensor.transpose(ph[m % 2][:, k * P:(k + 1) * P], h[:, 4 * g + k, t * P:(t + 1) * P], K.c("ident"))
                        last.then_inc(h_turned[m % 2], 1)

                turn_h(0, 2)
                pe.wait_ge(copied, len(kinds))
                for m, t in enumerate(tiles):
                    last = nc.tensor.transpose(pt[:, m * E:(m + 1) * E], lg[:, t * P:(t + 1) * P], K.c("ident")[0:E, 0:E])
                last.then_inc(turned, 1)
                turn_h(2, len(groups) // 2)
                pe.wait_ge(affs, 1)
                for m, t in enumerate(tiles):
                    last = nc.tensor.transpose(pa[:, at(t):at(t) + P], aff[:, t, :], K.c("ident"))
                last.then_inc(aff_turned, 1)
                turn_h(len(groups) // 2, len(groups))
                pe.wait_ge(placed, len(kinds))
                pe.wait_ge(shifted, 1)
                for m, t in enumerate(tiles):
                    last = nc.tensor.transpose(pt[:, m * E:(m + 1) * E], cnt[:, t * P:(t + 1) * P], K.c("ident")[0:E, 0:E])
                last.then_inc(slot_turned, 1)

            @block.scalar
            def _(act):
                act.wait_ge(logits, 1)
                for r, b, _ in kinds:
                    nc.scalar.activation(lg[:, r], pl[:, b], ACT.Copy).then_inc(copied, 1)

                def copy_h(lo, hi):
                    for m in range(lo, hi):
                        t, g = groups[m]
                        act.wait_ge(h_turned[m % 2], m // 2 + 1)
                        nc.scalar.activation(h2[:, t, 4 * g * P:(4 * g + 4) * P], ph[m % 2][:], ACT.Copy).then_inc(h_copied[m % 2], 1)

                copy_h(0, 2)
                act.wait_ge(shifted, 1)
                nc.scalar.activation(ex[:], ex[:], ACT.Exp).then_inc(exped, 1)
                copy_h(2, len(groups))

            @block.vector
            def _(dve):
                nc.vector.memset(ones[:], 1.0).then_inc(worked, 1)
                logit = pt[:, 0:n * E].rearrange("p (t e) -> p t e", e=E)
                dve.wait_ge(turned, 1)
                nc.vector.tensor_reduce(mx[:], logit, AX.X, ALU.max).then_inc(maxed, 1)
                dve.wait_ge(maxed, 1)
                nc.vector.tensor_tensor(ex[:], logit, mx[:].unsqueeze(2).broadcast_to([P, n, E]), ALU.subtract).then_inc(shifted, 1)
                dve.wait_ge(exped, 1)
                nc.vector.tensor_reduce(rs[:], ex[:], AX.X, ALU.add).then_inc(summed, 1)
                dve.wait_ge(summed, 1)
                nc.vector.reciprocal(rr[:], rs[:]).then_inc(inv, 1)
                dve.wait_ge(inv, 1)
                nc.vector.tensor_tensor(aff[:, t0:NT, :], ex[:], rr[:].unsqueeze(2).broadcast_to([P, n, E]), ALU.mult).then_inc(affs, 1)
                dve.wait_ge(aff_turned, 1)
                for r, b, _ in kinds:
                    nc.vector.tensor_copy(work[:, r], pa[:, b]).then_inc(worked, 1)
                rounds = 0
                for r, b, cap in kinds:
                    dve.wait_ge(worked, 1 + len(kinds))
                    for _ in range(cap // 8):
                        dve.wait_ge(replaced, rounds) if rounds else None
                        nc.vector.max(top[:], work[:, r]).then_inc(found, 1)
                        rounds += 1
                        dve.wait_ge(found, rounds)
                        nc.vector.match_replace(work[:, r], top[:], work[:, r], -1.0).then_inc(replaced, 1)
                dve.wait_ge(replaced, rounds)
                for m, (r, b, _) in enumerate(kinds):
                    nc.vector.tensor_scalar(work[:, r], work[:, r], 0.0, None, ALU.is_lt).then_inc(picked, 1)
                    dve.wait_ge(picked, m + 1)
                    nc.vector.tensor_tensor_scan(cnt[:, r], ones[:, r], work[:, r], 0.0, ALU.mult, ALU.add).then_inc(counted, 1)
                    dve.wait_ge(counted, 2 * m + 1)
                    nc.vector.tensor_tensor(cnt[:, r], cnt[:, r], work[:, r], ALU.mult).then_inc(counted, 1)
                    dve.wait_ge(counted, 2 * m + 2)
                    nc.vector.tensor_scalar(cnt[:, r], cnt[:, r], -1.0, None, ALU.add).then_inc(placed, 1)
                dve.wait_ge(slot_turned, 1)
                nc.vector.tensor_copy(slot[:, t0:NT, :], logit)


def experts(K, A, tag, layer, h2, slot, aff):
    nc, x = K.nc, K.x
    ctx_too = layer == 0
    Q = 4
    NS = CAP_L + CAP_C if ctx_too else CAP_L
    NR = CAP_L + CAP_C
    with ExitStack() as ctx:
        hm_ = K.h[:].rearrange("p k t -> p (k t)")
        XS, SL, SCX = KD * Q * NS, NT - CT, CT
        xs = hm_[:, 0:XS].rearrange("p (k e j) -> p k e j", k=KD, e=Q)
        o = XS
        sel_l = hm_[:, o:o + SL * Q * CAP_L].rearrange("p (t e j) -> p t e j", t=SL, e=Q)
        o += SL * Q * CAP_L
        sw_l = hm_[:, o:o + SL * Q * CAP_L].rearrange("p (t e j) -> p t e j", t=SL, e=Q)
        o += SL * Q * CAP_L
        sel_c = hm_[:, o:o + SCX * Q * CAP_C].rearrange("p (t e j) -> p t e j", t=SCX, e=Q)
        o += SCX * Q * CAP_C
        sw_c = hm_[:, o:o + SCX * Q * CAP_C].rearrange("p (t e j) -> p t e j", t=SCX, e=Q)
        w = [K.sb(f"{tag}_w{s}", [P, 4096], ctx) for s in range(6)]
        put_l = K.sb(f"{tag}_put_l", [P, 2, LAT], ctx)
        put_c = K.sb(f"{tag}_put_c", [P, CTX], ctx)
        sg = [K.sb(f"{tag}_sg{f}", [NS, 512], ctx) for f in range(2)]
        hid = [K.sb(f"{tag}_hid{f}", [NR, 512], ctx) for f in range(2)]
        hidT = [K.sb(f"{tag}_hidT{f}", [P, 4, NS], ctx) for f in range(2)]
        out_l = K.sb(f"{tag}_out_l", [P, D], ctx)
        out_c = K.sb(f"{tag}_out_c", [P, D], ctx)
        pg = [K.ps(f"{tag}_pg{f}", [P, 512], ctx) for f in range(2)]
        pu = [K.ps(f"{tag}_pu{f}", [P, 512], ctx) for f in range(2)]
        pt = [K.ps(f"{tag}_pt{f}", [P, 512], ctx) for f in range(2)]
        pd = [K.ps(f"{tag}_pd{f}", [P, 512], ctx) for f in range(2)]
        sem = lambda n: K.sem(f"{tag}_{n}")
        two = lambda n: [sem(f"{n}{f}") for f in range(2)]
        w_ready = [sem(f"w_ready{s}") for s in range(6)]
        selected, weighted, put_turned, put_copied = (sem(n) for n in ("selected", "weighted", "put_turned", "put_copied"))
        gathered, xs_copied = two("gathered"), two("xs_copied")
        gated, upped, silued, hidden, turned, hid_copied, downed = (two(n) for n in (
            "gated", "upped", "silued", "hidden", "turned", "hid_copied", "downed"))
        out_copied = two("out_copied")
        spread, added = two("spread"), two("added")
        NB = KD // 2 * (3 if ctx_too else 2)
        padded = sem("padded")
        NPUT = 3 if ctx_too else 2
        views = [w[s][:].rearrange("p (k n) -> p k n", n=512) for s in range(4)] + \
                [w[s][:].rearrange("p (k n) -> p k n", n=D) for s in (4, 5)]
        gate_w, up_w, down_w = (A["moe_" + n][layer] for n in ("gate", "up", "down"))
        with nc.Block() as block:
            @block.sync
            def _(sp):
                with sp.Fori(0, E // Q) as q:
                    for e in range(Q):
                        for s in range(6):
                            sp.wait_ge((gated[0], upped[0], gated[1], upped[1], downed[0], downed[1])[s], Q * q + e)
                            if s < 4:
                                m = (gate_w, up_w)[s % 2][bass.ds(Q * q + e, 1)]
                                src = m.rearrange("o (k p) f -> (o p) k f", p=P)[:, :, 512 * (s // 2):512 * (s // 2) + 512]
                            else:
                                m = down_w[bass.ds(Q * q + e, 1)]
                                src = m.rearrange("o (k p) f -> (o p) k f", p=P)[:, 4 * (s - 4):4 * (s - 4) + 4, :]
                            sp.dma_start(views[s], src).then_inc(w_ready[s], 16)

            @block.tensor
            def _(pe):
                def gather(q):
                    pe.wait_ge(selected, q + 1)
                    for k in range(KD):
                        b = k % 2
                        pe.wait_ge(xs_copied[b], 4 * q + k // 2)
                        if k < 2:
                            pe.wait_ge(hid_copied[b], Q * q)
                        for t in range(SL):
                            last = nc.tensor.matmul(pt[b][:, 0:Q * CAP_L], h2[:, CT + t, k * P:(k + 1) * P], sel_l[:, t].rearrange("p e j -> p (e j)"),
                                                    start=t == 0, stop=t == SL - 1)
                        if ctx_too:
                            for t in range(CT):
                                last = nc.tensor.matmul(pt[b][:, 256:256 + Q * CAP_C], h2[:, t, k * P:(k + 1) * P], sel_c[:, t].rearrange("p e j -> p (e j)"),
                                                        start=t == 0, stop=t == CT - 1)
                        last.then_inc(gathered[b], 1)

                def turn_put(q):
                    pe.wait_ge(weighted, q + 1)
                    for f in range(2):
                        pe.wait_ge(silued[f], Q * q)
                    for pr in range(2):
                        for t in range(SL):
                            last = nc.tensor.transpose(pg[pr][:, t * P:(t + 1) * P], sw_l[:, t, 2 * pr:2 * pr + 2, :].rearrange("p e j -> p (e j)"), K.c("ident"))
                        last.then_inc(put_turned, 1)
                    if ctx_too:
                        pe.wait_ge(hidden[0], Q * q)
                        for t in range(CT):
                            last = nc.tensor.transpose(pu[0][:, t * P:(t + 1) * P], sw_c[:, t].rearrange("p e j -> p (e j)"), K.c("ident"))
                        last.then_inc(put_turned, 1)

                def gate_up(q, e):
                    n = Q * q + e
                    if e == 0:
                        for b in range(2):
                            pe.wait_ge(xs_copied[b], 4 * q + 4)
                        pe.wait_ge(put_copied, NPUT * q + NPUT)
                    for f in range(2):
                        for m, (bank, done, used) in enumerate(((pg, gated, silued), (pu, upped, hidden))):
                            s = 2 * f + m
                            pe.wait_ge(w_ready[s], 16 * n + 16)
                            pe.wait_ge(used[f], n)
                            for k in range(KD):
                                last = nc.tensor.matmul(bank[f][0:NS, :], xs[:, k, e, :], views[s][:, k, :], start=k == 0, stop=k == KD - 1)
                            last.then_inc(done[f], 1)

                def down(q, e):
                    n = Q * q + e
                    for f in range(2):
                        pe.wait_ge(hidden[f], n + 1)
                        if not (e == 0):
                            pe.wait_ge(hid_copied[f], n)
                        else:
                            pe.wait_ge(xs_copied[f], 4 * q + 4)
                        for c in range(4):
                            last = nc.tensor.transpose(pt[f][:, c * NR:(c + 1) * NR], hid[f][:, c * P:(c + 1) * P], K.c("ident")[0:NR, 0:NR])
                        last.then_inc(turned[f], 1)
                        pe.wait_ge(hid_copied[f], n + 1)
                        pe.wait_ge(w_ready[4 + f], 16 * n + 16)
                        if f == 0:
                            for b in range(2):
                                pe.wait_ge(out_copied[b], n)
                                pe.wait_ge(added[b], NB * q + (4 if e >= 2 else 0))
                        for b in range(2):
                            for c in range(4):
                                last = nc.tensor.matmul(pd[b][0:NS, :], hidT[f][:, c, :], views[4 + f][:, c, b * 512:(b + 1) * 512],
                                                        start=f == 0 and c == 0, stop=f == 1 and c == 3)
                        last.then_inc(downed[f], 1)

                def spread_out(q, part):
                    n = Q * q + (2, 4, 4)[part]
                    for b in range(2):
                        pe.wait_ge(out_copied[b], n)
                    for k in range(KD):
                        b = k % 2
                        pe.wait_ge(added[b], NB * q + 4 * part + k // 2)
                        if part < 2:
                            last = nc.tensor.matmul(pd[b][:], out_l[:, k * P:(k + 1) * P], put_l[:, part, :], start=True, stop=True)
                        else:
                            last = nc.tensor.matmul(pd[b][:, 0:CTX], out_c[:, k * P:(k + 1) * P], put_c[:], start=True, stop=True)
                        last.then_inc(spread[b], 1)

                with pe.Fori(0, E // Q) as q:
                    gather(q)
                    turn_put(q)
                    for e in range(Q):
                        gate_up(q, e)
                        if e == 2:
                            spread_out(q, 0)
                        down(q, e)
                    spread_out(q, 1)
                    if ctx_too:
                        spread_out(q, 2)

            @block.scalar
            def _(act):
                def copy_xs(q):
                    for k in range(0, KD, 2):
                        act.wait_ge(gathered[0], 4 * q + k // 2 + 1)
                        if k == 0:
                            act.wait_ge(upped[1], Q * q)
                        last = nc.scalar.activation(xs[:, k, :, 0:CAP_L], pt[0][:, 0:Q * CAP_L].rearrange("p (e j) -> p e j", e=Q), ACT.Copy)
                        if ctx_too:
                            last = nc.scalar.activation(xs[:, k, :, CAP_L:NS], pt[0][:, 256:256 + Q * CAP_C].rearrange("p (e j) -> p e j", e=Q), ACT.Copy)
                        last.then_inc(xs_copied[0], 1)

                def copy_out(q, e):
                    n = Q * q + e
                    act.wait_ge(downed[1], n + 1)
                    act.wait_ge(spread[1], NB * q + (4 if e >= 2 else 0))
                    row = CAP_L * (e % 2)
                    last = nc.scalar.activation(out_l[row:row + CAP_L, 0:512], pd[0][0:CAP_L, :], ACT.Copy)
                    if ctx_too:
                        last = nc.scalar.activation(out_c[CAP_C * e:CAP_C * e + CAP_C, 0:512], pd[0][CAP_L:NS, :], ACT.Copy)
                    last.then_inc(out_copied[0], 1)

                with act.Fori(0, E // Q) as q:
                    copy_xs(q)
                    for pr in range(2):
                        act.wait_ge(put_turned, NPUT * q + pr + 1)
                        act.wait_ge(spread[1], NB * q)
                        nc.scalar.activation(put_l[:, pr, :], pg[pr][:], ACT.Copy).then_inc(put_copied, 1)
                    if ctx_too:
                        act.wait_ge(put_turned, NPUT * q + 3)
                        nc.scalar.activation(put_c[:], pu[0][:, 0:CTX], ACT.Copy).then_inc(put_copied, 1)
                    for e in range(Q):
                        n = Q * q + e
                        for f in range(2):
                            act.wait_ge(gated[f], n + 1)
                            act.wait_ge(hidden[f], n)
                            nc.scalar.activation(sg[f][:], pg[f][0:NS, :], ACT.Silu).then_inc(silued[f], 1)
                        act.wait_ge(turned[0], n + 1)
                        act.wait_ge(downed[0], n)
                        nc.scalar.activation(hidT[0][:], pt[0][:, 0:4 * NR].rearrange("p (c j) -> p c j", c=4)[:, :, 0:NS], ACT.Copy).then_inc(hid_copied[0], 1)
                        copy_out(q, e)

            @block.vector
            def _(dve):
                def select(q):
                    dve.wait_ge(gathered[1], 4 * q)
                    kinds = [(sel_l, sw_l, CT, SL, CAP_L)] + ([(sel_c, sw_c, 0, CT, CAP_C)] if ctx_too else [])
                    for sel, sw, t0, nt, cap in kinds:
                        for t in range(nt):
                            place = slot[:, t0 + t, bass.ds(Q * q, Q)].unsqueeze(2).broadcast_to([P, Q, cap])
                            last = nc.vector.tensor_tensor(sel[:, t], K.c("iota", cap).unsqueeze(1).broadcast_to([P, Q, cap]), place, ALU.is_equal)
                    last.then_inc(selected, 1)
                    dve.wait_ge(selected, q + 1)
                    dve.wait_ge(put_turned, NPUT * q)
                    for sel, sw, t0, nt, cap in kinds:
                        for t in range(nt):
                            a = aff[:, t0 + t, bass.ds(Q * q, Q)].unsqueeze(2).broadcast_to([P, Q, cap])
                            last = nc.vector.tensor_tensor(sw[:, t], sel[:, t], a, ALU.mult)
                    last.then_inc(weighted, 1)

                def copy_xs(q):
                    for k in range(1, KD, 2):
                        dve.wait_ge(gathered[1], 4 * q + k // 2 + 1)
                        if k == 1:
                            dve.wait_ge(upped[1], Q * q)
                        last = nc.vector.tensor_copy(xs[:, k, :, 0:CAP_L], pt[1][:, 0:Q * CAP_L].rearrange("p (e j) -> p e j", e=Q))
                        if ctx_too:
                            last = nc.vector.tensor_copy(xs[:, k, :, CAP_L:NS], pt[1][:, 256:256 + Q * CAP_C].rearrange("p (e j) -> p e j", e=Q))
                        last.then_inc(xs_copied[1], 1)

                def add(q, part):
                    for k in range(KD):
                        b = k % 2
                        dve.wait_ge(spread[b], NB * q + 4 * part + k // 2 + 1)
                        dve.wait_ge(added[b], NB * q + 4 * part + k // 2)
                        s, r, n = (0, LATR, LAT) if part < 2 else (1, CTXR, CTX)
                        nc.vector.scalar_tensor_tensor(out=x[:, k, r], in0=pd[b][:, 0:n], scalar=K.m(s, layer, 5, k), in1=x[:, k, r],
                                                       op0=ALU.mult, op1=ALU.add).then_inc(added[b], 1)

                def multiply(q, e):
                    n = Q * q + e
                    for f in range(2):
                        dve.wait_ge(silued[f], n + 1)
                        dve.wait_ge(upped[f], n + 1)
                        dve.wait_ge(turned[f], n)
                        nc.vector.tensor_tensor(hid[f][0:NS, :], sg[f][:], pu[f][0:NS, :], ALU.mult).then_inc(hidden[f], 1)

                def finish(q, e):
                    n = Q * q + e
                    dve.wait_ge(turned[1], n + 1)
                    dve.wait_ge(downed[1], n)
                    nc.vector.tensor_copy(hidT[1][:], pt[1][:, 0:4 * NR].rearrange("p (c j) -> p c j", c=4)[:, :, 0:NS]).then_inc(hid_copied[1], 1)
                    dve.wait_ge(downed[1], n + 1)
                    row = CAP_L * (e % 2)
                    dve.wait_ge(spread[1], NB * q + (4 if e >= 2 else 0))
                    last = nc.vector.tensor_copy(out_l[row:row + CAP_L, 512:D], pd[1][0:CAP_L, :])
                    if ctx_too:
                        last = nc.vector.tensor_copy(out_c[CAP_C * e:CAP_C * e + CAP_C, 512:D], pd[1][CAP_L:NS, :])
                    last.then_inc(out_copied[1], 1)

                if NR > NS:
                    for f in range(2):
                        nc.vector.memset(hid[f][NS:NR, :], 0.0).then_inc(padded, 1)
                    dve.wait_ge(padded, 2)
                with dve.Fori(0, E // Q) as q:
                    select(q)
                    copy_xs(q)
                    for e in range(Q):
                        multiply(q, e)
                        if e == 2:
                            add(q, 0)
                        finish(q, e)
                    add(q, 1)
                    if ctx_too:
                        add(q, 2)


def mixture(K, A, layer):
    with ExitStack() as ctx:
        tag = f"moe{layer}"
        norm(K, tag + "n", layer, 1)
        h2 = K.sb(f"{tag}_h2", [P, NT, D], ctx)
        slot = K.sb(f"{tag}_slot", [P, NT, E], ctx)
        aff = K.sb(f"{tag}_aff", [P, NT, E], ctx)
        route(K, A, tag + "r", layer, h2, slot, aff)
        experts(K, A, tag + "x", layer, h2, slot, aff)


def mix_and_project(K, A, scr, hid):
    nc, h = K.nc, K.h
    JOBS = (("k", 2), ("v", 3), ("r", 0), ("w1", 1), ("a1", 4), ("g1", 5))
    LORA_F = {"w1": ACT.Tanh, "a1": ACT.Copy, "g1": ACT.Sigmoid}
    with ExitStack() as ctx:
        xx = K.sb("mp_xx", [P, KD, TOK], ctx)
        mix = [K.sb(f"mp_mix{j}", [P, KD, TOK], ctx) for j in range(2)]
        w = [K.sb(f"mp_w{j}", [P, KD, P], ctx) for j in range(2)]
        lw = [K.sb(f"mp_lw{n}", [P, KD, P], ctx) for n in range(3)]
        st = [K.sb(f"mp_st{j}", [P, TOK], ctx) for j in range(2)]
        ps = [K.ps(f"mp_p{j}", [P, 1024], ctx) for j in range(2)]
        w_ready = [K.sem(f"mp_w_ready{j}") for j in range(2)]
        prod = [K.sem(f"mp_product{j}") for j in range(2)]
        copied = [K.sem(f"mp_copied{j}") for j in range(2)]
        stored = [K.sem(f"mp_stored{j}") for j in range(2)]
        spilled = K.sem("mp_x_stored")
        lora_ready, neighbours, mixed, lora = (K.sem(f"mp_{n}") for n in ("lora_ready", "neighbours", "mixed", "lora"))
        spans = ((LATR, slice(0, LAT)), (CTXR, slice(512, 512 + CTX)))
        n_it = KD // 2
        with nc.Block() as block:
            @block.sync
            def _(sp):
                for n, (name, _) in enumerate(JOBS[3:]):
                    sp.dma_start(lw[n][:], A[name]).then_inc(lora_ready, 16)
                sp.dma_start(scr["x"], K.x[:]).then_inc(spilled, 16)
                for m, (name, _) in enumerate(JOBS[:3]):
                    with sp.Fori(0, n_it) as i:
                        for j in range(2):
                            sp.wait_ge(prod[j], i + m * n_it)
                            sp.dma_start(w[j][:], A["rw_" + name][bass.ds(2 * i + j, 1)].rearrange("o p k n -> (o p) k n")
                                         ).then_inc(w_ready[j], 16)

            @block.vector
            def _(dve):
                for r in (CTXR, LATR):
                    lo, hi = r.start, r.stop
                    nc.vector.tensor_tensor(xx[:, :, lo + 1:hi - 1], h[:, :, lo:hi - 2], h[:, :, lo + 2:hi], ALU.add).then_inc(neighbours, 1)
                    nc.vector.tensor_copy(xx[:, :, lo:lo + 1], h[:, :, lo + 1:lo + 2]).then_inc(neighbours, 1)
                    nc.vector.tensor_copy(xx[:, :, hi - 1:hi], h[:, :, hi - 2:hi - 1]).then_inc(neighbours, 1)
                dve.wait_ge(neighbours, 6)
                for k in range(KD):
                    nc.vector.scalar_tensor_tensor(out=xx[:, k, :], in0=xx[:, k, :], scalar=0.5, in1=h[:, k, :],
                                                   op0=ALU.mult, op1=ALU.subtract).then_inc(neighbours, 1)
                for m, (name, row) in enumerate(JOBS):
                    if m == 0:
                        dve.wait_ge(neighbours, 6 + KD)
                    elif m >= 2 and m <= 4:
                        for j in range(2):
                            dve.wait_ge(prod[j], (m - 1) * n_it)
                    elif m == 5:
                        dve.wait_ge(lora, 1)
                    for k in range(KD):
                        nc.vector.scalar_tensor_tensor(out=mix[m % 2][:, k, :], in0=xx[:, k, :], scalar=K.v("mu", row * KD + k),
                                                       in1=h[:, k, :], op0=ALU.mult, op1=ALU.add).then_inc(mixed, 1)

            @block.tensor
            def _(pe):
                for m, (name, _) in enumerate(JOBS[:3]):
                    pe.wait_ge(mixed, KD * (m + 1))
                    with pe.Fori(0, n_it) as i:
                        for j in range(2):
                            pe.wait_ge(w_ready[j], 16 * i + 16 * (m * n_it + 1))
                            pe.wait_ge(copied[j], i + m * n_it)
                            for r, b in spans:
                                for k in range(KD):
                                    last = nc.tensor.matmul(ps[j][:, b], w[j][:, k, :], mix[m % 2][:, k, r], start=k == 0, stop=k == KD - 1)
                            last.then_inc(prod[j], 1)
                pe.wait_ge(lora_ready, 48)
                for n, (name, _) in enumerate(JOBS[3:]):
                    m = 3 + n
                    pe.wait_ge(mixed, KD * (m + 1))
                    pe.wait_ge(copied[n % 2], 3 * n_it + n // 2)
                    for r, b in spans:
                        for k in range(KD):
                            last = nc.tensor.matmul(ps[n % 2][:, b], lw[n][:, k, :], mix[m % 2][:, k, r], start=k == 0, stop=k == KD - 1)
                    last.then_inc(lora, 1)

            @block.scalar
            def _(act):
                for m, (name, _) in enumerate(JOBS[:3]):
                    with act.Fori(0, n_it) as i:
                        for j in range(2):
                            act.wait_ge(prod[j], i + (m * n_it + 1))
                            act.wait_ge(stored[j], 16 * i + 16 * m * n_it)
                            for r, b in spans:
                                last = nc.scalar.activation(st[j][:, r], ps[j][:, b], ACT.Copy)
                            last.then_inc(copied[j], 1)
                            act.wait_ge(copied[j], i + (m * n_it + 1))
                            act.dma_start(scr[name][bass.ds(2 * i + j, 1)].rearrange("o p t -> (o p) t"), st[j][:]
                                          ).then_inc(stored[j], 16)
                for n, (name, _) in enumerate(JOBS[3:]):
                    act.wait_ge(lora, n + 1)
                    for r, b in spans:
                        last = nc.scalar.activation(hid[name][:, r], ps[n % 2][:, b], LORA_F[name])
                    last.then_inc(copied[n % 2], 1)
                for j in range(2):
                    act.wait_ge(stored[j], 16 * 3 * n_it)
                act.wait_ge(spilled, 16)


class Chain:

    def __init__(self, eng, sem, i, per):
        self.eng, self.sem, self.i, self.per, self.n = eng, sem, i, per, 0

    def step(self, ins):
        self.n += 1
        ins.then_inc(self.sem, 1)

    def wait(self):
        self.eng.wait_ge(self.sem, self.i * self.per + self.n)

    def end(self):
        assert self.n == self.per, (self.n, self.per)


def rwkv(K, A, scr, hid, o):
    nc = K.nc
    NEG = -float(np.exp(np.float32(-0.5)))
    NC = TOK // CH
    LV = len(LEVELS)
    T3 = [0, 1, 2]
    with ExitStack() as ctx:
        sb = lambda n, s: K.sb("rk_" + n, s, ctx)
        kT, vT, rT = sb("k", [P, TOK]), sb("v", [P, TOK]), sb("r", [P, TOK])
        w2z = [sb(f"w2z{d}", [P, P]) for d in range(2)]
        a2z = [sb(f"a2z{d}", [P, P]) for d in range(2)]
        g2c = sb("g2c", [P, P])
        kk, sq, ms = sb("kk", [P, TOK]), sb("sq", [P, TOK]), sb("ms", [P, TOK])
        lw, L, aa, kd = sb("lw", [P, TOK]), sb("L", [P, TOK]), sb("a", [P, TOK]), sb("kd", [P, TOK])
        Lx = ms
        eL, eLx, emL = sb("eL", [P, TOK]), sb("eLx", [P, TOK]), sb("emL", [P, TOK])
        b = sq
        Bh, kh = lw, aa
        kds = sb("kds", [P, LAT])
        xm = K.x[:].rearrange("p k t -> p (k t)")
        zr = xm[:, 0:4 * TOK].rearrange("p (m t) -> p m t", m=4)
        Zz = xm[:, 4 * TOK:6 * TOK].rearrange("p (t h c) -> p t h c", t=NT, h=2)
        S = xm[:, 6 * TOK:6 * TOK + NC * P].rearrange("p (n c) -> p n c", c=P)
        spare = K.h[:].rearrange("p k t -> p (k t)")[:, KD * LAT:KD * TOK]
        U = spare[:, 0:TOK].rearrange("p (t c) -> p t c", c=P)
        TKT = spare[:, TOK:2 * TOK]
        Y = spare[:, 2 * TOK:2 * TOK + LAT].rearrange("p (t c) -> p t c", c=P)
        Rt, Bt, kt = sb("Rt", [P, LAT]), sb("Bt", [P, TOK]), sb("kt", [P, TOK])
        Kz = sb("Kz", [P, NT, 2, P])
        BKz = sb("BKz", [P, NT, 2, 2, P])
        Vz = sb("Vz", [P, NT, 2, P])
        xy = sb("xy", [P, NT, 2, 4, P])
        A4 = [sb(f"A4_{q}", [P, 4, P]) for q in T3]
        W4 = [sb(f"W4_{q}", [P, 4, P]) for q in T3]
        TT4 = [sb(f"T4_{q}", [P, 4, P]) for q in T3]
        Y4 = [sb(f"Y4_{q}", [P, 4, P]) for q in T3]
        AVz = Kz
        tmpS = sb("tmpS", [P, P])
        stat = sb("stat", [P, 4, 8])
        yT, bon, gg = eL[:, 0:LAT], eLx[:, 0:LAT], emL[:, 0:LAT]
        prod3 = lw[:, 0:LAT]
        bank = [K.ps(f"rk_b{n}", [P, 512], ctx) for n in range(8)]
        sem = lambda n: K.sem("rk_" + n)
        loaded, zeroed, hp_done = sem("loaded"), sem("zeroed"), sem("heads_done")
        d_vec, d_act, d_pool = sem("vec_steps"), sem("act_steps"), sem("pool_steps")
        raw_sq, sq_sum, sq_max, sq_root, v_turned = (sem(n) for n in ("kk_squared", "kk_summed", "kk_max", "kk_root", "v_turned"))
        uw, sig, cum, exps, ready_b, feat, hats, turned_tok, tok_a, tok_v = (sem(n) for n in (
            "lora_out", "sigmoids", "cumsum", "exps", "b_and_kd", "features", "hats", "tokens_turned", "tok_copied_a", "tok_copied_v"))
        aq, masked, n_turned, a_copied, w_first, w_turned, t_copied, y_prod, y_masked, w_prod, w_added = (sem(n) for n in (
            "causal_products", "masked", "n_turned", "a_copied", "w_first", "w_turned", "t_copied", "y_products", "y_masked",
            "w_products", "w_added"))
        av, av_copied, utk, u_copied, tk_copied = (sem(n) for n in ("av", "av_copied", "u_and_tk", "u_copied", "tk_copied"))
        z_prod, z_added, s_prod, s_next, y_out, y_added = (sem(n) for n in ("z_products", "z_added", "s_products", "s_next", "y_out", "y_added"))
        centred, gn_var, gn_root, y_normed, y_back, bonus_in, bonus, gate = (sem(n) for n in (
            "centred", "gn_variance", "gn_root", "y_normed", "y_turned", "bonus_in", "bonus", "gate"))
        s_zero = sem("s_zero")
        diag = lambda ap: ap.rearrange("p h (a j) -> p (h a) j", j=NH)[:, 0:4:3, :]
        spans = ((LATR, 0), (CTXR, 1))
        order = [list(range(NC)), list(range(CTX // CH))[::-1] + list(range(CTX // CH, NC))[::-1]]
        n_it = KD

        def col(name, i, at=0):
            return K.vec[:, bass.ds(i + (VEC[name] + at), 1)]

        with nc.Block() as block:
            @block.sync
            def _(sp):
                sp.wait_ge(zeroed, 4)
                with sp.Fori(0, n_it) as i:
                    sp.wait_ge(hp_done, i)
                    one = lambda t: t[bass.ds(i, 1)].rearrange("o p t -> (o p) t")
                    sp.dma_start(kT[:], one(scr["k"])).then_inc(loaded, 16)
                    sp.dma_start(vT[:], one(scr["v"])).then_inc(loaded, 16)
                    sp.dma_start(rT[:], one(scr["r"])).then_inc(loaded, 16)
                    for d in range(2):
                        sp.dma_start(w2z[d][64 * d:64 * d + 64, :], one(A["w2"])[64 * d:64 * d + 64, :]).then_inc(loaded, 16)
                        sp.dma_start(a2z[d][64 * d:64 * d + 64, :], one(A["a2"])[64 * d:64 * d + 64, :]).then_inc(loaded, 16)
                    sp.dma_start(g2c[:], one(A["g2"])).then_inc(loaded, 16)

            @block.gpsimd
            def _(pool):
                for d in range(2):
                    nc.gpsimd.memset(w2z[d][:], 0.0).then_inc(zeroed, 1)
                    nc.gpsimd.memset(a2z[d][:], 0.0).then_inc(zeroed, 1)
                nc.gpsimd.memset(Vz[:], 0.0).then_inc(zeroed, 1)
                nc.gpsimd.memset(Zz, 0.0).then_inc(zeroed, 1)
                nc.gpsimd.memset(S, 0.0).then_inc(zeroed, 1)
                with pool.Fori(0, n_it) as i:
                    for d in range(2):
                        u = 2 * i + d
                        pool.wait_ge(exps, 3 * u + 3)
                        pool.wait_ge(ready_b, 2 * u + 2)
                        nc.gpsimd.tensor_tensor(Bt[:], b[:], emL[:], ALU.mult).then_inc(hats, 1)
                        nc.gpsimd.tensor_tensor(kt[:], kd[:], emL[:], ALU.mult).then_inc(hats, 1)
                        pool.wait_ge(hats, 4 * u + 2)
                        end = CH - 1 if d == 0 else 0
                        pc = eL[:].rearrange("p (c j) -> p c j", j=CH)[:, :, end:end + 1].broadcast_to([P, NC, CH])
                        cj = lambda t: t[:].rearrange("p (c j) -> p c j", j=CH)
                        nc.gpsimd.tensor_tensor(cj(Bh), cj(Bt), pc, ALU.mult).then_inc(hats, 1)
                        nc.gpsimd.tensor_tensor(cj(kh), cj(kt), pc, ALU.mult).then_inc(hats, 1)

            @block.scalar
            def _(act):
                with act.Fori(0, n_it) as i:
                    act.wait_ge(raw_sq, 2 * i + 1)
                    nc.scalar.activation(sq[:], kk[:], ACT.Square).then_inc(raw_sq, 1)
                    act.wait_ge(sq_max, 2 * i + 2)
                    nc.scalar.activation(ms[:], ms[:], ACT.Sqrt).then_inc(sq_root, 1)
                    for d in range(2):
                        u = 2 * i + d
                        act.wait_ge(uw, 2 * u + 1)
                        for r, n in spans:
                            nc.scalar.activation(lw[:, r], bank[n][:, 0:r.stop - r.start], ACT.Sigmoid, bias=col("w0", i, KD * d)).then_inc(sig, 1)
                        act.wait_ge(uw, 2 * u + 2)
                        for r, n in spans:
                            nc.scalar.activation(aa[:, r], bank[2 + n][:, 0:r.stop - r.start], ACT.Sigmoid, bias=col("a0", i, KD * d)).then_inc(sig, 1)
                        act.wait_ge(cum, 3 * u + 3)
                        nc.scalar.activation(eL[:], L[:], ACT.Exp).then_inc(exps, 1)
                        nc.scalar.activation(eLx[:], Lx[:], ACT.Exp).then_inc(exps, 1)
                        nc.scalar.activation(emL[:], L[:], ACT.Exp, scale=-1.0).then_inc(exps, 1)
                        for t in range(NT):
                            act.wait_ge(turned_tok, NT * u + t + 1)
                            nc.scalar.activation(Kz[:, t, :, :], bank[2 * (t % 2)][:, 0:2 * P].rearrange("p (h c) -> p h c", h=2), ACT.Copy).then_inc(tok_a, 1)
                        for q in T3:
                            act.wait_ge(n_turned, 3 * u + q + 1)
                            nc.scalar.activation(A4[q][:], bank[q][:].rearrange("p (m c) -> p m c", m=4), ACT.Copy).then_inc(a_copied, 1)
                        for lv in range(LV):
                            for q in T3:
                                act.wait_ge(w_turned, 3 * (LV * u + lv) + q + 1)
                                nc.scalar.activation(TT4[q][:], bank[q][:].rearrange("p (m c) -> p m c", m=4), ACT.Copy).then_inc(t_copied, 1)
                        act.wait_ge(utk, 2 * u + 1)
                        for n in range(2):
                            w = (4, 2)[n] * P
                            nc.scalar.activation(TKT[:, 4 * P * n:4 * P * n + w], bank[2 + n][:, 0:w], ACT.Copy).then_inc(tk_copied, 1)
                        act.wait_ge(utk, 2 * u + 2)
                        for n in range(2):
                            w = (4, 2)[n]
                            nc.scalar.activation(U[:, 4 * n:4 * n + w, :], bank[4 + n][:, 0:w * P].rearrange("p (t c) -> p t c", c=P), ACT.Copy).then_inc(u_copied, 1)
                    act.wait_ge(gn_var, i + 1)
                    nc.scalar.activation(stat[:, 3, :], stat[:, 2, :], ACT.Sqrt).then_inc(gn_root, 1)

            @block.tensor
            def _(pe):
                tile = lambda t: slice(t * P, (t + 1) * P)
                at = lambda q, m: (2 * q + m // 2, m % 2)

                def lora_out(u, d):
                    pe.wait_ge(zeroed, 7)
                    for n, (z, hname) in enumerate(((w2z, "w1"), (a2z, "a1"))):
                        for r, bn in spans:
                            last = nc.tensor.matmul(bank[2 * n + bn][:, 0:r.stop - r.start], z[d][:], hid[hname][:, r], start=True, stop=True)
                        last.then_inc(uw, 1)

                def direction(i, d):
                    u = 2 * i + d
                    if d == 1:
                        pe.wait_ge(y_added, u)
                    lora_out(u, d)
                    pe.wait_ge(feat, 5 * u + 5)
                    pe.wait_ge(hats, 4 * u + 4)
                    pe.wait_ge(sig, 4 * u + 4)
                    for t in range(NT):
                        if t >= 2:
                            pe.wait_ge(tok_a, NT * u + t - 1)
                            pe.wait_ge(tok_v, NT * u + t - 1)
                        j = 2 * (t % 2)
                        for hh in range(2):
                            nc.tensor.transpose(bank[j][:, hh * P:(hh + 1) * P], zr[:, hh, tile(t)], K.c("ident"))
                        nc.tensor.transpose(bank[j + 1][:, 0:P], Bh[:, tile(t)], K.c("ident"))
                        nc.tensor.transpose(bank[j + 1][:, P:2 * P], kh[:, tile(t)], K.c("ident")).then_inc(turned_tok, 1)
                    for t in range(NT):
                        w = 4 if t >= CT else 2
                        j = 4 + 2 * (t % 2)
                        if t >= 2:
                            pe.wait_ge(masked, 2 * (NT * u + t - 1))
                        for n, m in enumerate((Bt, kt)):
                            last = nc.tensor.matmul(bank[j + n][:, 0:w * P], m[:, tile(t)], zr[:, 0:w, tile(t)], start=True, stop=True)
                            last.then_inc(aq, 1)
                    pe.wait_ge(tok_a, NT * (u + 1))
                    pe.wait_ge(tok_v, NT * (u + 1))
                    for q in T3:
                        pe.wait_ge(masked, 2 * (NT * u + 2 * q + 2))
                        for m in range(4):
                            t, hh = at(q, m)
                            last = nc.tensor.transpose(bank[q][:, m * P:(m + 1) * P], xy[:, t, 0, hh, :], K.c("ident"))
                        last.then_inc(n_turned, 1)
                    pe.wait_ge(masked, 2 * NT * (u + 1))
                    for lv in range(LV):
                        for q in T3:
                            if lv == 0:
                                pe.wait_ge(w_first, 2 * (3 * u + q + 1))
                                pe.wait_ge(a_copied, 3 * u + q + 1)
                            else:
                                pe.wait_ge(w_added, 3 * ((LV * u) + lv - 1) + q + 1)
                            for m in range(4):
                                last = nc.tensor.transpose(bank[q][:, m * P:(m + 1) * P], W4[q][:, m, :], K.c("ident"))
                            last.then_inc(w_turned, 1)
                        for q in T3:
                            pe.wait_ge(t_copied, 3 * (LV * u + lv) + q + 1)
                            for m in range(4):
                                last = nc.tensor.matmul(bank[q][:, m * P:(m + 1) * P], A4[q][:, m, :], W4[q][:, m, :], start=True, stop=True)
                            last.then_inc(y_prod, 1)
                        for q in T3:
                            pe.wait_ge(y_masked, 3 * (LV * u + lv) + q + 1)
                            for m in range(4):
                                last = nc.tensor.matmul(bank[3 + q][:, m * P:(m + 1) * P], TT4[q][:, m, :], Y4[q][:, m, :], start=True, stop=True)
                            last.then_inc(w_prod, 1)
                    pe.wait_ge(w_added, 3 * LV * (u + 1))
                    for t in range(NT):
                        for hh in range(2):
                            last = nc.tensor.matmul(bank[2 + t // 4][:, (t % 4) * P:(t % 4 + 1) * P], Kz[:, t, hh, :],
                                                    W4[t // 2][:, 2 * (t % 2) + hh, :], start=hh == 0, stop=hh == 1)
                    last.then_inc(utk, 1)
                    for t in range(NT):
                        for hh in range(2):
                            last = nc.tensor.matmul(bank[t // 4][:, (t % 4) * P:(t % 4 + 1) * P], xy[:, t, 1, hh, :], Vz[:, t, hh, :],
                                                    start=hh == 0, stop=hh == 1)
                    last.then_inc(av, 1)
                    pe.wait_ge(av_copied, 2 * u + 2)
                    for t in range(NT):
                        for hh in range(2):
                            last = nc.tensor.matmul(bank[4 + t // 4][:, (t % 4) * P:(t % 4 + 1) * P], W4[t // 2][:, 2 * (t % 2) + hh, :],
                                                    AVz[:, t, hh, :], start=hh == 0, stop=hh == 1)
                    last.then_inc(utk, 1)
                    pe.wait_ge(tk_copied, 2 * u + 2)
                    pe.wait_ge(u_copied, 2 * u + 2)
                    pe.wait_ge(s_zero, u + 1)
                    for n, c in enumerate(order[d][:-1] + order[d][-1:]):
                        t, half = c // 2, c % 2
                        rows = slice(CH * half, CH * half + CH)
                        last_chunk = n == NC - 1
                        if n:
                            pe.wait_ge(s_next, (NC - 1) * u + n)
                        nc.tensor.matmul(bank[4 + n % 2][rows, 0:P], TKT[:, c * CH:(c + 1) * CH], S[:, n, :], start=True, stop=True).then_inc(z_prod, 1)
                        if last_chunk:
                            break
                        nc.tensor.matmul(bank[6 + n % 2][:, 0:P], BKz[:, t, half, 1, :], diag(Vz[:, t]), start=True, stop=False)
                        pe.wait_ge(z_added, NC * u + n + 1)
                        nc.tensor.matmul(bank[6 + n % 2][:, 0:P], BKz[:, t, half, 0, :], diag(Zz[:, t]), start=False, stop=True).then_inc(s_prod, 1)
                    pe.wait_ge(z_added, NC * (u + 1))
                    for t in range(CT, NT):
                        oc = slice((t - CT) * P, (t - CT + 1) * P)
                        for half in range(2):
                            c = 2 * t + half
                            n = order[d].index(c)
                            rows = slice(CH * half, CH * half + CH)
                            nc.tensor.matmul(bank[0][rows, oc], Rt[:, c * CH - CTX:(c + 1) * CH - CTX], S[:, n, :], start=True, stop=False,
                                             skip_group_check=True)
                        for hh in range(2):
                            nc.tensor.matmul(bank[0][:, oc], xy[:, t, 0, 2 + hh, :], Zz[:, t, hh, :], start=False, stop=False, skip_group_check=True)
                            last = nc.tensor.matmul(bank[0][:, oc], xy[:, t, 1, 2 + hh, :], Vz[:, t, hh, :], start=False, stop=hh == 1, skip_group_check=True)
                    last.then_inc(y_out, 1)

                with pe.Fori(0, n_it) as i:
                    pe.wait_ge(loaded, 128 * i + 128)
                    pe.wait_ge(raw_sq, 2 * i + 2)
                    pe.wait_ge(hp_done, i)
                    for r, bn in spans:
                        last = nc.tensor.matmul(bank[bn][:, 0:r.stop - r.start], K.c("heads"), sq[:, r], start=True, stop=True)
                    last.then_inc(sq_sum, 1)
                    for t in range(NT):
                        last = nc.tensor.transpose(bank[4 + t // 4][:, (t % 4) * P:(t % 4 + 1) * P], vT[:, tile(t)], K.c("ident"))
                    last.then_inc(v_turned, 1)
                    pe.wait_ge(sq_max, 2 * i + 2)
                    direction(i, 0)
                    direction(i, 1)
                    nc.tensor.matmul(bank[1][:], g2c[:], hid["g1"][:, LATR], start=True, stop=True).then_inc(gate, 1)
                    pe.wait_ge(bonus_in, i + 1)
                    nc.tensor.matmul(bank[2][:], K.c("heads"), prod3, start=True, stop=True).then_inc(bonus, 1)
                    pe.wait_ge(y_normed, i + 1)
                    for t in range(4):
                        last = nc.tensor.transpose(bank[3][:, t * P:(t + 1) * P], Y[:, t, :], K.c("ident"))
                    last.then_inc(y_back, 1)

            @block.vector
            def _(dve):
                PER = RWKV_VEC_STEPS
                with dve.Fori(0, n_it) as i:
                    ch = Chain(dve, d_vec, i, PER)

                    def step(ins):
                        ch.step(ins)
                        ch.wait()

                    dve.wait_ge(loaded, 128 * i + 128)
                    dve.wait_ge(hp_done, i)
                    nc.vector.tensor_scalar(kk[:], kT[:], col("k_k", i), None, ALU.mult).then_inc(raw_sq, 1)
                    dve.wait_ge(sq_sum, i + 1)
                    for r, bn in spans:
                        nc.vector.tensor_scalar(ms[:, r], bank[bn][:, 0:r.stop - r.start], 1e-24, None, ALU.max).then_inc(sq_max, 1)
                    dve.wait_ge(v_turned, i + 1)
                    dve.wait_ge(zeroed, 7)
                    for n in range(2):
                        w = (4, 2)[n]
                        for hh in range(2):
                            ch.step(nc.vector.tensor_copy(Vz[:, 4 * n:4 * n + w, hh, NH * hh:NH * hh + NH],
                                                          bank[4 + n][:, 0:w * P].rearrange("p (t c) -> p t c", c=P)[:, :, NH * hh:NH * hh + NH]))
                    dve.wait_ge(sq_root, i + 1)
                    step(nc.vector.reciprocal(eL[:], ms[:]))
                    step(nc.vector.tensor_tensor(kk[:], kk[:], eL[:], ALU.mult))
                    for d in range(2):
                        u = 2 * i + d
                        dve.wait_ge(sig, 4 * u + 2)
                        step(nc.vector.tensor_scalar(lw[:], lw[:], NEG, None, ALU.mult))
                        if d == 0:
                            ins = nc.vector.tensor_tensor_scan(L[:], K.c("start", TOK), lw[:], 0.0, ALU.mult, ALU.add)
                        else:
                            ins = nc.vector.tensor_tensor_scan(L[:, ::-1], K.c("end", TOK)[:, ::-1], lw[:, ::-1], 0.0, ALU.mult, ALU.add)
                        ins.then_inc(cum, 1)
                        dve.wait_ge(cum, 3 * u + 1)
                        nc.vector.tensor_tensor(Lx[:], L[:], lw[:], ALU.subtract).then_inc(cum, 1)
                        dve.wait_ge(sig, 4 * u + 4)
                        nc.vector.scalar_tensor_tensor(out=b[:], in0=kk[:], scalar=-1.0, in1=aa[:], op0=ALU.mult, op1=ALU.mult).then_inc(ready_b, 1)
                        step(nc.vector.tensor_scalar(kd[:], aa[:], -1.0, col("k_a", i), ALU.add, ALU.mult))
                        nc.vector.scalar_tensor_tensor(out=kd[:], in0=kd[:], scalar=1.0, in1=kT[:], op0=ALU.add, op1=ALU.mult).then_inc(ready_b, 1)
                        dve.wait_ge(ready_b, 2 * u + 2)
                        if d == 0:
                            nc.vector.tensor_copy(kds[:], kd[:, LATR]).then_inc(cum, 1)
                        else:
                            nc.vector.tensor_tensor(kds[:], kds[:], kd[:, LATR], ALU.add).then_inc(cum, 1)
                        dve.wait_ge(cum, 3 * u + 3)
                        dve.wait_ge(exps, 3 * u + 2)
                        for hh in range(2):
                            nc.vector.scalar_tensor_tensor(out=zr[:, hh, :], in0=kk[:], scalar=K.c("half", 1, hh), in1=eLx[:],
                                                           op0=ALU.mult, op1=ALU.mult).then_inc(feat, 1)
                            nc.vector.scalar_tensor_tensor(out=zr[:, 2 + hh, LATR], in0=rT[:, LATR], scalar=K.c("half", 1, hh), in1=eL[:, LATR],
                                                           op0=ALU.mult, op1=ALU.mult).then_inc(feat, 1)
                        nc.vector.tensor_tensor(Rt[:], rT[:, LATR], eL[:, LATR], ALU.mult).then_inc(feat, 1)
                        ch.step(nc.vector.memset(S[:, 0, :], 0.0))
                        ch.wait()
                        nc.vector.memset(tmpS[:], 0.0).then_inc(s_zero, 1)
                        dve.wait_ge(s_zero, u + 1)
                        for t in range(NT):
                            dve.wait_ge(turned_tok, NT * u + t + 1)
                            for half in range(2):
                                last = nc.vector.tensor_scalar(BKz[:, t, half, :, :], bank[2 * (t % 2) + 1][:, 0:2 * P].rearrange("p (m c) -> p m c", m=2),
                                                               K.c("half", 1, half), None, ALU.mult)
                            last.then_inc(tok_v, 1)
                        for t in range(NT):
                            w = 4 if t >= CT else 2
                            for n in range(2):
                                dve.wait_ge(aq, 2 * (NT * u + t) + n + 1)
                                nc.vector.tensor_tensor(xy[:, t, n, 0:w, :], bank[4 + 2 * (t % 2) + n][:, 0:w * P].rearrange("p (m c) -> p m c", m=w),
                                                        K.c("causal", w * P, 4 * P * d).rearrange("p (m c) -> p m c", m=w), ALU.mult).then_inc(masked, 1)
                        dve.wait_ge(masked, 2 * NT * (u + 1))
                        for q in T3:
                            n4 = xy[:, 2 * q:2 * q + 2, 0, 0:2, :]
                            for x in range(2):
                                last = nc.vector.tensor_tensor(Y4[q][:, 2 * x:2 * x + 2, :], xy[:, 2 * q + x, 0, 0:2, :],
                                                               K.c("first", P, P * d).unsqueeze(1).broadcast_to([P, 2, P]), ALU.mult)
                            last.then_inc(w_first, 1)
                            dve.wait_ge(w_first, 2 * (3 * u + q) + 1)
                            nc.vector.tensor_tensor(W4[q][:], Y4[q][:], K.c("ident").unsqueeze(1).broadcast_to([P, 4, P]), ALU.add).then_inc(w_first, 1)
                        for lv in range(LV):
                            for q in T3:
                                dve.wait_ge(y_prod, 3 * (LV * u + lv) + q + 1)
                                nc.vector.tensor_tensor(Y4[q][:], bank[q][:].rearrange("p (m c) -> p m c", m=4),
                                                        K.c("level", P, (d * LV + lv) * P).unsqueeze(1).broadcast_to([P, 4, P]), ALU.mult).then_inc(y_masked, 1)
                            for q in T3:
                                dve.wait_ge(w_prod, 3 * (LV * u + lv) + q + 1)
                                nc.vector.tensor_tensor(W4[q][:], W4[q][:], bank[3 + q][:].rearrange("p (m c) -> p m c", m=4), ALU.add).then_inc(w_added, 1)
                        dve.wait_ge(w_added, 3 * LV * (u + 1))
                        dve.wait_ge(utk, 2 * u + 1)
                        step(nc.vector.memset(AVz[:], 0.0))
                        dve.wait_ge(av, u + 1)
                        for n in range(2):
                            w = (4, 2)[n]
                            for hh in range(2):
                                last = nc.vector.tensor_copy(AVz[:, 4 * n:4 * n + w, hh, NH * hh:NH * hh + NH],
                                                             bank[n][:, 0:w * P].rearrange("p (t c) -> p t c", c=P)[:, :, NH * hh:NH * hh + NH])
                            last.then_inc(av_copied, 1)
                        end = CH - 1 if d == 0 else 0
                        dve.wait_ge(u_copied, 2 * u + 2)
                        for n, c in enumerate(order[d]):
                            t, half = c // 2, c % 2
                            rows = slice(CH * half, CH * half + CH)
                            dve.wait_ge(z_prod, NC * u + n + 1)
                            nc.vector.tensor_tensor(diag(Zz[rows, t]), bank[4 + n % 2][rows, 0:P].rearrange("p (h j) -> p h j", h=2),
                                                    U[rows, t, :].rearrange("p (h j) -> p h j", h=2), ALU.add).then_inc(z_added, 1)
                            if n == NC - 1:
                                break
                            dve.wait_ge(s_prod, (NC - 1) * u + n + 1)
                            if n:
                                dve.wait_ge(s_next, (NC - 1) * u + n)
                            step(nc.vector.tensor_tensor(tmpS[:], bank[6 + n % 2][:, 0:P], K.c("heads"), ALU.mult))
                            nc.vector.scalar_tensor_tensor(out=S[:, n + 1, :], in0=S[:, n, :], scalar=eL[:, c * CH + end:c * CH + end + 1],
                                                           in1=tmpS[:], op0=ALU.mult, op1=ALU.add).then_inc(s_next, 1)
                            dve.wait_ge(s_next, (NC - 1) * u + n + 1)
                        dve.wait_ge(y_out, u + 1)
                        pb = bank[0][:].rearrange("p (t c) -> p t c", c=P)
                        if d == 0:
                            nc.vector.tensor_copy(Y, pb).then_inc(y_added, 1)
                        else:
                            nc.vector.tensor_tensor(Y, Y, pb, ALU.add).then_inc(y_added, 1)
                        dve.wait_ge(y_added, u + 1)
                    step(nc.vector.tensor_scalar(prod3, rT[:, LATR], col("r_k", i), None, ALU.mult))
                    nc.vector.tensor_tensor(prod3, prod3, kds[:], ALU.mult).then_inc(bonus_in, 1)
                    y8 = Y.rearrange("p t (h j) -> p (t h) j", h=2)
                    bc = lambda n: stat[:, n, :].unsqueeze(2).broadcast_to([P, 8, NH])
                    step(nc.vector.tensor_reduce(stat[:, 0, :], y8, AX.X, ALU.add))
                    step(nc.vector.tensor_scalar(stat[:, 0, :], stat[:, 0, :], 1.0 / NH, None, ALU.mult))
                    step(nc.vector.tensor_tensor(y8, y8, bc(0), ALU.subtract))
                    sqv = Y4[0][:].rearrange("p m (h j) -> p (m h) j", h=2)
                    step(nc.vector.tensor_tensor(sqv, y8, y8, ALU.mult))
                    step(nc.vector.tensor_reduce(stat[:, 1, :], sqv, AX.X, ALU.add))
                    nc.vector.tensor_scalar(stat[:, 2, :], stat[:, 1, :], 1.0 / NH, GN_EPS, ALU.mult, ALU.add).then_inc(gn_var, 1)
                    dve.wait_ge(gn_root, i + 1)
                    step(nc.vector.reciprocal(stat[:, 1, :], stat[:, 3, :]))
                    nc.vector.tensor_tensor(y8, y8, bc(1), ALU.mult).then_inc(y_normed, 1)
                    dve.wait_ge(bonus, i + 1)
                    step(nc.vector.tensor_tensor(bon, bank[2][:], vT[:, LATR], ALU.mult))
                    dve.wait_ge(y_back, i + 1)
                    step(nc.vector.tensor_scalar(yT, bank[3][:], col("ln_w", i), col("ln_b", i), ALU.mult, ALU.add))
                    step(nc.vector.tensor_tensor(bon, bon, yT, ALU.add))
                    dve.wait_ge(gate, i + 1)
                    nc.vector.tensor_tensor(o[:, bass.ds(i, 1), :].rearrange("p o t -> p (o t)"), bon, bank[1][:], ALU.mult).then_inc(hp_done, 1)
                    ch.end()


def rwkv_layer(K, A, scr, layer):
    nc, x = K.nc, K.x
    norm(K, "n1", layer, 0)
    with ExitStack() as ctx:
        hid = {n: K.sb("hid_" + n, [P, TOK], ctx) for n in ("w1", "a1", "g1")}
        mix_and_project(K, A, scr, hid)
        o = K.h[:].rearrange("p k t -> p (k t)")[:, 0:KD * LAT].rearrange("p (k t) -> p k t", k=KD)
        rwkv(K, A, scr, hid, o)
    project_out(K, "out1", A["rw_o"], o, KD, layer, ((0, LATR),), spilled=scr["x"])


RWKV_VEC_STEPS = 46


def build(nc, A, out):
    with ExitStack() as ctx:
        K = Core(nc, ctx)
        mod_dram = nc.dram_tensor("mod_rows_scratch", (2, DEPTH * NCOL, 512), F32, kind="Internal").ap()
        scr = {n: nc.dram_tensor(f"rw_{n}_scratch", (KD, P, TOK), F32, kind="Internal").ap() for n in ("k", "v", "r")}
        scr["x"] = nc.dram_tensor("x_scratch", (P, KD, TOK), F32, kind="Internal").ap()
        with ExitStack() as first:
            K.hold("attn", first)
            modulation(K, A, mod_dram)
            norm(K, "n0", 0, 0)
            qk = K.sb("qk", [P, NQ + NKV, TOK], first)
            v = K.sb("v", [P, NT, NKV * HD], first)
            o = K.sb("o", [P, NQ + KD, TOK], first)
            project_qk(K, A, qk)
            project_v_conv(K, A, v, o)
            attend(K, qk, v, o)
            project_out(K, "out0", A["w_out"], o, NQ + KD, 0, RANGES)
        del K.con["attn"]
        K.clear_semaphores()
        mixture(K, A, 0)
        K.clear_semaphores()
        with ExitStack() as second:
            K.hold("rwkv", second)
            load_constants(K, A, "rwkv")
            rwkv_layer(K, A, scr, 1)
        K.clear_semaphores()
        mixture(K, A, 1)
        norm(K, "final", None, None, final=out)


def load_constants(K, A, group):
    nc = K.nc
    loaded = K.sem(f"con_{group}_loaded")
    with nc.Block() as block:
        @block.sync
        def _(sp):
            sp.dma_start(K.con[group][:], A["con_" + group]).then_inc(loaded, 16)
            sp.wait_ge(loaded, 16)


def lay_out(a):
    f = lambda n: np.asarray(a[n])
    cols = lambda *names: [f(n).reshape(-1, P) for n in names]
    w = {}
    rows = cols("c", "c_ctx", "ada_b", "norm_g", "final_g", "conv_w", "rw_mu", "rw_w0", "rw_a0", "rw_k_k", "rw_k_a",
                "rw_r_k", "rw_ln_w", "rw_ln_b", "q_norm_g", "k_norm_g")
    w["vecs"] = np.ascontiguousarray(np.concatenate(rows, 0).T)
    x = np.concatenate([f("ctx")[0], f("x")[0]], 0)
    w["xT"] = np.ascontiguousarray(x.T.reshape(KD, P, TOK).transpose(1, 0, 2))

    def by_columns(m, n=P):
        k, c = m.shape
        return np.ascontiguousarray(m.reshape(k // P, P, c // n, n).transpose(2, 1, 0, 3))

    w["ada"] = np.concatenate([by_columns(f("ada_w")[l], 512) for l in range(DEPTH)], 0)
    w["w_in"] = by_columns(f("mix_w_in")[0])
    w["w_out"] = by_columns(f("mix_w_out")[0])
    for n in ("r", "k", "v", "o"):
        w["rw_" + n] = by_columns(f("rw_w_" + n)[0])
    for n in ("w1", "a1"):
        m = f("rw_" + n)[0]
        w[n] = by_columns(np.concatenate([m[0], m[1]], 1))[0]
    w["g1"] = by_columns(f("rw_g1")[0])[0]
    for n in ("w2", "a2"):
        w[n] = np.ascontiguousarray(f("rw_" + n)[0].reshape(2 * 64, KD, P).transpose(1, 0, 2))
    w["g2"] = np.ascontiguousarray(f("rw_g2")[0].reshape(P, KD, P).transpose(1, 0, 2))
    w["router"] = np.ascontiguousarray(f("moe_router").reshape(DEPTH, KD, P, E).transpose(0, 2, 1, 3))
    for n in ("gate", "up", "down"):
        w["moe_" + n] = np.ascontiguousarray(f("moe_w_" + n))
    return w


def kernel(**inputs):
    import concourse.bacc as _bacc
    from concourse.bass_utils import run_bass_kernel_spmd as _run

    arrays = {**lay_out(inputs), **constants()}
    nc = _bacc.Bacc("TRN2", target_bir_lowering=False, num_devices=1)
    A = {n: nc.dram_tensor("in_" + n, a.shape, mybir.dt.from_np(a.dtype), kind="ExternalInput").ap() for n, a in arrays.items()}
    out = nc.dram_tensor("outT", (P, KD, LAT), F32, kind="ExternalOutput").ap()
    build(nc, A, out)
    r = _run(nc, [{"in_" + n: a for n, a in arrays.items()}], core_ids=[0]).results[0]["outT"]
    return np.ascontiguousarray(r.transpose(2, 1, 0).reshape(1, LAT, D))
```

```python
from contextlib import ExitStack

import numpy as np

import concourse.bass as bass
from concourse import mybir

ALU = mybir.AluOpType
ACT = mybir.ActivationFunctionType
AX = mybir.AxisListType
F32 = mybir.dt.float32

P = 128
D = 1024
KD = D // P
CTX, LAT = 256, 512
TOK = CTX + LAT
NT = TOK // P
CT = CTX // P
DEPTH = 2
HD = 128
NQ, NKV = 8, 2
QPK = NQ // NKV
GRID_W = 64
E = 16
CAP_L, CAP_C = 2 * LAT // E, 2 * CTX // E
EPS = 1e-6
GN_EPS = 64e-5
NH = 64
CH = 64
NCOL = 6 * D // 512

LATR, CTXR = slice(CTX, TOK), slice(0, CTX)
RANGES = ((1, CTXR), (0, LATR))

FROM = 1

SEMAPHORES = {
    "mixer0":
        "mod_small_loaded mod_w_ready0 mod_w_ready1 mod_w_ready2 mod_w_ready3 mod_silu_done mod_product_done0 "
        "mod_product_done1 mod_product_done2 mod_product_done3 mod_row_copied0 mod_row_copied1 mod_row_copied2 "
        "mod_row_copied3 mod_row_stored mod_rows_loaded mod_rows_turned mod_columns_done n0_squared n0_summed "
        "n0_mean n0_rooted n0_inverse n0_scaled n0_stored qk_w_ready0 qk_w_ready1 qk_proj_lat0 qk_proj_lat1 "
        "qk_proj0 qk_proj1 qk_squared0 qk_squared1 qk_summed0 qk_summed1 qk_mean0 qk_mean1 qk_rooted0 qk_rooted1 "
        "qk_inverse0 qk_inverse1 qk_normed0 qk_normed1 qk_swapped0 qk_swapped1 qk_cosed0 qk_cosed1 qk_sined0 "
        "qk_sined1 qk_written0 qk_written1 qk_ctx_copied0 qk_ctx_copied1 qk_gains v_w_ready v_product v_copied "
        "v_pads_zeroed conv_w_ready0 conv_w_ready1 conv_copied0 conv_copied1 conv_gated0 conv_gated1 conv_mid0 "
        "conv_mid1 conv_left0 conv_left1 conv_right0 conv_right1 conv_written0 conv_written1 conv_product0 "
        "conv_product1 conv_product2 at_scored0 at_scored1 at_maxed0 at_maxed1 at_biased0 at_biased1 at_exped0 "
        "at_exped1 at_summed0 at_summed1 at_scaled0 at_scaled1 at_turned0 at_turned1 at_copied_a0 at_copied_a1 "
        "at_copied_v0 at_copied_v1 at_staged0 at_staged1 at_weighed0 at_weighed1 at_out0 at_out1 out0_w_ready0 "
        "out0_w_ready1 out0_product0 out0_product1 out0_added0 out0_added1 out0_x_back ",
    "moe0":
        "moe0n_squared moe0n_summed moe0n_mean moe0n_rooted moe0n_inverse moe0n_scaled moe0n_stored "
        "moe0r_router_loaded moe0r_logits moe0r_logits_copied moe0r_logits_turned moe0r_max moe0r_shifted "
        "moe0r_exped moe0r_summed moe0r_inverse moe0r_affinity moe0r_affinity_turned moe0r_work moe0r_top "
        "moe0r_replaced moe0r_picked moe0r_counted moe0r_placed moe0r_slot_turned moe0r_h_turned0 moe0r_h_turned1 "
        "moe0r_h_copied0 moe0r_h_copied1 moe0x_w_ready0 moe0x_w_ready1 moe0x_w_ready2 moe0x_w_ready3 "
        "moe0x_w_ready4 moe0x_w_ready5 moe0x_selected moe0x_weighted moe0x_put_turned moe0x_put_copied "
        "moe0x_gathered0 moe0x_gathered1 moe0x_xs_copied0 moe0x_xs_copied1 moe0x_gated0 moe0x_gated1 moe0x_upped0 "
        "moe0x_upped1 moe0x_silued0 moe0x_silued1 moe0x_hidden0 moe0x_hidden1 moe0x_turned0 moe0x_turned1 "
        "moe0x_hid_copied0 moe0x_hid_copied1 moe0x_downed0 moe0x_downed1 moe0x_out_copied0 moe0x_out_copied1 "
        "moe0x_spread0 moe0x_spread1 moe0x_added0 moe0x_added1 moe0x_padded ",
    "rwkv1":
        "con_rwkv_loaded n1_squared n1_summed n1_mean n1_rooted n1_inverse n1_scaled n1_stored mp_w_ready0 "
        "mp_w_ready1 mp_product0 mp_product1 mp_copied0 mp_copied1 mp_stored0 mp_stored1 mp_x_stored "
        "mp_lora_ready mp_neighbours mp_mixed mp_lora rk_loaded rk_zeroed rk_heads_done rk_vec_steps rk_act_steps "
        "rk_pool_steps rk_kk_squared rk_kk_summed rk_kk_max rk_kk_root rk_v_turned rk_lora_out rk_sigmoids "
        "rk_cumsum rk_exps rk_b_and_kd rk_features rk_hats rk_tokens_turned rk_tok_copied_a rk_tok_copied_v "
        "rk_causal_products rk_masked rk_n_turned rk_a_copied rk_w_first rk_w_turned rk_t_copied rk_y_products "
        "rk_y_masked rk_w_products rk_w_added rk_av rk_av_copied rk_u_and_tk rk_u_copied rk_tk_copied "
        "rk_z_products rk_z_added rk_s_products rk_s_next rk_y_out rk_y_added rk_centred rk_gn_variance "
        "rk_gn_root rk_y_normed rk_y_turned rk_bonus_in rk_bonus rk_gate rk_s_zero out1_w_ready0 out1_w_ready1 "
        "out1_product0 out1_product1 out1_added0 out1_added1 out1_x_back ",
    "moe1":
        "moe1n_squared moe1n_summed moe1n_mean moe1n_rooted moe1n_inverse moe1n_scaled moe1n_stored "
        "moe1r_router_loaded moe1r_logits moe1r_logits_copied moe1r_logits_turned moe1r_max moe1r_shifted "
        "moe1r_exped moe1r_summed moe1r_inverse moe1r_affinity moe1r_affinity_turned moe1r_work moe1r_top "
        "moe1r_replaced moe1r_picked moe1r_counted moe1r_placed moe1r_slot_turned moe1r_h_turned0 moe1r_h_turned1 "
        "moe1r_h_copied0 moe1r_h_copied1 moe1x_w_ready0 moe1x_w_ready1 moe1x_w_ready2 moe1x_w_ready3 "
        "moe1x_w_ready4 moe1x_w_ready5 moe1x_selected moe1x_weighted moe1x_put_turned moe1x_put_copied "
        "moe1x_gathered0 moe1x_gathered1 moe1x_xs_copied0 moe1x_xs_copied1 moe1x_gated0 moe1x_gated1 moe1x_upped0 "
        "moe1x_upped1 moe1x_silued0 moe1x_silued1 moe1x_hidden0 moe1x_hidden1 moe1x_turned0 moe1x_turned1 "
        "moe1x_hid_copied0 moe1x_hid_copied1 moe1x_downed0 moe1x_downed1 moe1x_out_copied0 moe1x_out_copied1 "
        "moe1x_spread0 moe1x_spread1 moe1x_added0 moe1x_added1 moe1x_padded final_squared final_summed final_mean "
        "final_rooted final_inverse final_scaled final_stored ",
}

VEC = {}
_at = 0
for _name, _n in (("c", KD), ("c_ctx", KD), ("ada_b", DEPTH * 6 * KD), ("norm_g", DEPTH * 2 * KD),
                  ("final_g", KD), ("conv_w", 3 * KD), ("mu", 6 * KD), ("w0", 2 * KD), ("a0", 2 * KD),
                  ("k_k", KD), ("k_a", KD), ("r_k", KD), ("ln_w", KD), ("ln_b", KD), ("q_g", 1), ("k_g", 1)):
    VEC[_name] = _at
    _at += _n
NVEC = _at

LEVELS = (2, 4, 8, 16, 32)
GROUPS = {
    "base": (("ident", P), ("ones", P), ("iota", 64)),
    "attn": (("swap", P), ("cos", LAT), ("sin", LAT)),
    "rwkv": (("heads", P), ("causal", 2 * 4 * P), ("first", 2 * P), ("level", 2 * len(LEVELS) * P),
             ("half", 2), ("start", TOK), ("end", TOK)),
}
CON, NCON = {}, {}
for _group, _names in GROUPS.items():
    _at = 0
    for _name, _n in _names:
        CON[_name] = (_group, _at)
        _at += _n
    NCON[_group] = _at


def constants():
    c = {g: np.zeros((P, n), np.float32) for g, n in NCON.items()}

    def put(name, a, at=0):
        g, o = CON[name]
        c[g][:, o + at:o + at + a.shape[1]] = a

    i = np.arange(P)
    put("ident", np.eye(P))
    put("ones", np.ones((P, P)))
    put("heads", (i[:, None] // NH == i[None] // NH) * 1.0)
    swap = np.zeros((P, P))
    swap[i[:64] + 64, i[:64]] = -1.0
    swap[i[:64], i[:64] + 64] = 1.0
    put("swap", swap)
    t = np.arange(LAT)
    n = HD // 4
    inv = (10000.0 ** (-np.arange(n, dtype=np.float32) / n)).astype(np.float32)
    ang = np.concatenate([(t // GRID_W).astype(np.float32)[:, None] * inv,
                          (t % GRID_W).astype(np.float32)[:, None] * inv], -1).T
    put("cos", np.concatenate([np.cos(ang)] * 2))
    put("sin", np.concatenate([np.sin(ang)] * 2))
    put("iota", np.broadcast_to(np.arange(64.0), (P, 64)))
    s, tt = i[:, None], i[None]
    same = s // CH == tt // CH
    for d in range(2):
        before = (s < tt) if d == 0 else (s > tt)
        for m in range(4):
            put("causal", same & (before | ((s == tt) & (m >= 2))), (4 * d + m) * P)
        put("first", same & before & (s // 2 == tt // 2), d * P)
        for j, b in enumerate(LEVELS):
            put("level", (s // (2 * b) == tt // (2 * b)) & before & (s // b != tt // b), (d * len(LEVELS) + j) * P)
    put("half", (i[:, None] // NH == np.arange(2)[None]) * 1.0)
    tok = np.arange(TOK)
    put("start", np.broadcast_to((tok % CH != 0) * 1.0, (P, TOK)))
    put("end", np.broadcast_to((tok % CH != CH - 1) * 1.0, (P, TOK)))
    return {"con_" + g: a for g, a in c.items()}


class Core:

    def __init__(self, nc, ctx):
        self.nc, self.ctx = nc, ctx
        self.used, self.started, self.named, self.stage = [], {}, {}, None
        self.x = self.sb("x", [P, KD, TOK])
        self.h = self.sb("h", [P, KD, TOK])
        self.con = {"base": self.sb("con_base", [P, NCON["base"]])}
        self.vec = self.sb("vec", [P, NVEC])
        self.mod = self.sb("mod", [P, 2, DEPTH * 6 * KD])
        self.scale = self.sb("scale", [P, 2, DEPTH * 2 * KD])

    def sb(self, name, shape, ctx=None, dt=F32):
        return (ctx or self.ctx).enter_context(self.nc.sbuf_tensor(name, shape, dt))

    def hold(self, group, ctx):
        self.con[group] = self.sb("con_" + group, [P, NCON[group]], ctx)

    def ps(self, name, shape, ctx=None, dt=F32):
        return (ctx or self.ctx).enter_context(self.nc.psum_tensor(name, shape, dt))

    def sem(self, name):
        self.named.setdefault(self.stage, []).append(name)
        if name in self.started:
            return self.started[name]
        s = self.nc.alloc_semaphore(name=name)
        self.used.append(s)
        return s

    def begin_stage(self, stage):
        nc, used = self.nc, self.used
        by_dma = lambda name: name.rstrip("0123456789").endswith(("loaded", "w_ready", "lora_ready", "stored", "x_back"))
        names = SEMAPHORES.get(stage, "").split()
        self.stage = stage
        for s in used:
            nc.release_semaphore(s)
        self.started = {n: nc.alloc_semaphore(name=n) for n in names if not by_dma(n)}
        with nc.Block() as block:
            @block.gpsimd
            def _(pool):
                for s in used:
                    pool.sem_clear(s)
                for s in self.started.values():
                    pool.sem_inc(s, FROM)
        self.used = list(self.started.values())

    def c(self, name, n=P, at=0):
        g, o = CON[name]
        return self.con[g][:, o + at:o + at + n]

    def v(self, name, j=0, n=1):
        return self.vec[:, VEC[name] + j:VEC[name] + j + n]

    def m(self, src, layer, which, k):
        j = (layer * 6 + which) * KD + k
        return self.mod[:, src, j:j + 1]


def modulation(K, A, mod_dram):
    nc, vec, mod, scale = K.nc, K.vec, K.mod, K.scale
    NB = 4
    with ExitStack() as ctx:
        w = [K.sb(f"ada_w{j}", [P, KD, 512], ctx) for j in range(NB)]
        sc = K.sb("silu_c", [P, KD, 2], ctx)
        row = K.sb("mod_row", [2, DEPTH * NCOL, 512], ctx)
        rows = K.sb("mod_rows", [DEPTH * 6 * KD, 2, P], ctx)
        pr = [K.ps(f"mod_p{j}", [2, 512], ctx) for j in range(NB)]
        pt = K.ps("mod_t", [P, 2, DEPTH * 6 * KD], ctx)
        small = K.sem("mod_small_loaded")
        w_ready = [K.sem(f"mod_w_ready{j}") for j in range(NB)]
        silu = K.sem("mod_silu_done")
        prod = [K.sem(f"mod_product_done{j}") for j in range(NB)]
        copied = [K.sem(f"mod_row_copied{j}") for j in range(NB)]
        stored = K.sem("mod_row_stored")
        back = K.sem("mod_rows_loaded")
        turned = K.sem("mod_rows_turned")
        done = K.sem("mod_columns_done")
        n_it = DEPTH * NCOL // NB
        with nc.Block() as block:
            @block.sync
            def _(sp):
                sp.dma_start(vec[:], A["vecs"]).then_inc(small, 16)
                for g, t in K.con.items():
                    sp.dma_start(t[:], A["con_" + g]).then_inc(small, 16)
                for j in range(NB):
                    sp.dma_start(w[j][:], A["ada"][j]).then_inc(w_ready[j], 16)
                with sp.Fori(1, n_it) as i:
                    for j in range(NB):
                        sp.wait_ge(prod[j], FROM + i)
                        sp.dma_start(w[j][:], A["ada"][bass.ds(i * NB + j, 1)].rearrange("o p k n -> (o p) k n")
                                     ).then_inc(w_ready[j], 16)
                sp.dma_start(K.x[:], A["xT"]).then_inc(small, 16)
                for j in range(NB):
                    sp.wait_ge(copied[j], FROM + n_it)
                sp.dma_start(mod_dram, row[:]).then_inc(stored, 16)
                sp.wait_ge(stored, 16)
                for s in range(2):
                    sp.dma_start(rows[:, s, :], mod_dram[s].rearrange("c (b p) -> (c b) p", p=P)).then_inc(back, 16)
                sp.wait_ge(small, 16 * (2 + len(K.con)))

            @block.scalar
            def _(act):
                act.wait_ge(small, 16 * (1 + len(K.con)))
                for s, name in enumerate(("c", "c_ctx")):
                    nc.scalar.activation(sc[:, :, s], K.v(name, 0, KD), ACT.Silu).then_inc(silu, 1)

            @block.tensor
            def _(pe):
                pe.wait_ge(silu, FROM + 2)
                with pe.Fori(0, n_it) as i:
                    for j in range(NB):
                        pe.wait_ge(w_ready[j], 16 * i + 16)
                        pe.wait_ge(copied[j], FROM + i)
                        for k in range(KD):
                            last = nc.tensor.matmul(pr[j][:], sc[:, k, :], w[j][:, k, :], start=k == 0, stop=k == KD - 1)
                        last.then_inc(prod[j], 1)
                pe.wait_ge(back, 32)
                n = DEPTH * 6 * KD
                for s in range(2):
                    last = nc.tensor.transpose(pt[:, s, :], rows[:, s, :], K.c("ident")[0:n, 0:n])
                last.then_inc(turned, 1)

            @block.vector
            def _(dve):
                with dve.Fori(0, n_it) as i:
                    for j in range(NB):
                        dve.wait_ge(prod[j], FROM + i + 1)
                        nc.vector.tensor_copy(row[:, bass.ds(i * NB + j, 1), :].rearrange("s o n -> s (o n)"), pr[j][:]
                                              ).then_inc(copied[j], 1)
                dve.wait_ge(turned, FROM + 1)
                n = DEPTH * 6 * KD
                for s in range(2):
                    nc.vector.tensor_tensor(mod[:, s, :], pt[:, s, :], K.v("ada_b", 0, n), ALU.add).then_inc(done, 1)
                dve.wait_ge(done, FROM + 2)
                for s in range(2):
                    for l in range(DEPTH):
                        for j in range(2):
                            at = (l * 6 + 3 * j + 1) * KD
                            o = (l * 2 + j) * KD
                            last = nc.vector.scalar_tensor_tensor(out=scale[:, s, o:o + KD], in0=mod[:, s, at:at + KD],
                                                                  scalar=1.0, in1=K.v("norm_g", o, KD),
                                                                  op0=ALU.add, op1=ALU.mult)


def norm(K, tag, layer, sub, final=None):
    nc, x, h = K.nc, K.x, K.h
    with ExitStack() as ctx:
        sq = K.sb(f"{tag}_sq", [P, KD, TOK], ctx)
        ms = K.sb(f"{tag}_ms", [P, TOK], ctx)
        rstd = K.sb(f"{tag}_rstd", [P, TOK], ctx)
        ps = K.ps(f"{tag}_ps", [P, 1024], ctx)
        squared = K.sem(f"{tag}_squared")
        summed = K.sem(f"{tag}_summed")
        mean = K.sem(f"{tag}_mean")
        rooted = K.sem(f"{tag}_rooted")
        inv = K.sem(f"{tag}_inverse")
        scaled = K.sem(f"{tag}_scaled")
        stored = K.sem(f"{tag}_stored")
        spans = ((LATR, slice(0, LAT)), (CTXR, slice(512, 512 + CTX)))
        with nc.Block() as block:
            @block.scalar
            def _(act):
                for k in range(KD):
                    nc.scalar.activation(sq[:, k, :], x[:, k, :], ACT.Square).then_inc(squared, 1)
                act.wait_ge(mean, FROM + 2)
                nc.scalar.activation(rstd[:], ms[:], ACT.Sqrt).then_inc(rooted, 1)
                if final is None:
                    for k in range(KD):
                        act.wait_ge(scaled, FROM + 2 * k + 2)
                        for s, r in RANGES:
                            nc.scalar.activation(h[:, k, r], h[:, k, r], ACT.Identity,
                                                 bias=K.m(s, layer, 3 * sub, k))

            @block.tensor
            def _(pe):
                for k in range(KD):
                    pe.wait_ge(squared, FROM + k + 1)
                    for r, b in spans:
                        last = nc.tensor.matmul(ps[:, b], K.c("ones"), sq[:, k, r], start=k == 0, stop=k == KD - 1)
                last.then_inc(summed, 1)

            @block.vector
            def _(dve):
                dve.wait_ge(summed, FROM + 1)
                for r, b in spans:
                    nc.vector.tensor_scalar(ms[:, r], ps[:, b], 1.0 / D, EPS, ALU.mult, ALU.add).then_inc(mean, 1)
                dve.wait_ge(rooted, FROM + 1)
                nc.vector.reciprocal(ms[:], rstd[:]).then_inc(inv, 1)
                dve.wait_ge(inv, FROM + 1)
                for k in range(KD):
                    if final is not None:
                        nc.vector.scalar_tensor_tensor(out=h[:, k, LATR], in0=x[:, k, LATR], scalar=K.v("final_g", k),
                                                       in1=ms[:, LATR], op0=ALU.mult, op1=ALU.mult).then_inc(scaled, 1)
                        continue
                    for s, r in RANGES:
                        o = (layer * 2 + sub) * KD + k
                        nc.vector.scalar_tensor_tensor(out=h[:, k, r], in0=x[:, k, r], scalar=K.scale[:, s, o:o + 1],
                                                       in1=ms[:, r], op0=ALU.mult, op1=ALU.mult).then_inc(scaled, 1)

            if final is not None:
                @block.sync
                def _(sp):
                    for k in range(KD):
                        sp.wait_ge(scaled, FROM + k + 1)
                        sp.dma_start(final[:, k, :], h[:, k, LATR]).then_inc(stored, 16)
                    sp.wait_ge(stored, 16 * KD)


def project_qk(K, A, qk):
    nc, h = K.nc, K.h
    with ExitStack() as ctx:
        w = [K.sb(f"qk_w{j}", [P, KD, P], ctx) for j in range(2)]
        g = K.sb("qk_g", [P, NQ + NKV], ctx)
        sq = [K.sb(f"qk_sq{j}", [P, TOK], ctx) for j in range(2)]
        ms = [K.sb(f"qk_ms{j}", [P, TOK], ctx) for j in range(2)]
        rt = [K.sb(f"qk_rt{j}", [P, TOK], ctx) for j in range(2)]
        qn = [K.sb(f"qk_qn{j}", [P, TOK], ctx) for j in range(2)]
        qc = [K.sb(f"qk_cos{j}", [P, LAT], ctx) for j in range(2)]
        qs = [K.sb(f"qk_sin{j}", [P, LAT], ctx) for j in range(2)]
        raw = [K.ps(f"qk_raw{j}", [P, 1024], ctx) for j in range(2)]
        ss = K.ps("qk_ss", [P, 1024], ctx)
        rot = [K.ps(f"qk_rot{j}", [P, LAT], ctx) for j in range(2)]
        sems = {n: [K.sem(f"qk_{n}{j}") for j in range(2)] for n in
                ("w_ready", "proj_lat", "proj", "squared", "summed", "mean", "rooted", "inverse", "normed",
                 "swapped", "cosed", "sined", "written", "ctx_copied")}
        gains = K.sem("qk_gains")
        n_it = (NQ + NKV) // 2
        spans = ((LATR, slice(0, LAT)), (CTXR, slice(512, 512 + CTX)))
        S = lambda n, j: sems[n][j]
        with nc.Block() as block:
            @block.sync
            def _(sp):
                for j in range(2):
                    sp.dma_start(w[j][:], A["w_in"][j]).then_inc(S("w_ready", j), 16)
                with sp.Fori(1, n_it) as i:
                    for j in range(2):
                        sp.wait_ge(S("proj", j), FROM + i)
                        sp.dma_start(w[j][:], A["w_in"][bass.ds(2 * i + j, 1)].rearrange("o p k n -> (o p) k n")
                                     ).then_inc(S("w_ready", j), 16)

            @block.tensor
            def _(pe):
                def project(i, j):
                    pe.wait_ge(S("w_ready", j), 16 * i + 16)
                    pe.wait_ge(S("normed", j), FROM + 2 * i)
                    for r, b in spans:
                        for k in range(KD):
                            last = nc.tensor.matmul(raw[j][:, b], w[j][:, k, :], h[:, k, r], start=k == 0, stop=k == KD - 1)
                        last.then_inc(S("proj_lat" if r is LATR else "proj", j), 1)

                def sums(i, j):
                    pe.wait_ge(S("mean", 1 - j), FROM + 2 * i + 2 * j)
                    for n, (r, b) in enumerate(spans):
                        pe.wait_ge(S("squared", j), FROM + 2 * i + 1 + n)
                        last = nc.tensor.matmul(ss[:, b], K.c("ones"), sq[j][:, r], start=True, stop=True)
                    last.then_inc(S("summed", j), 1)

                def swap(i, j):
                    pe.wait_ge(S("normed", j), FROM + 2 * i + 2)
                    pe.wait_ge(S("sined", j), FROM + i)
                    nc.tensor.matmul(rot[j][:], K.c("swap"), qn[j][:, LATR], start=True, stop=True
                                     ).then_inc(S("swapped", j), 1)

                with pe.Fori(0, n_it) as i:
                    project(i, 0)
                    sums(i, 0)
                    project(i, 1)
                    swap(i, 0)
                    sums(i, 1)
                    swap(i, 1)

            @block.scalar
            def _(act):
                with act.Fori(0, n_it) as i:
                    for j in range(2):
                        act.wait_ge(S("summed", j), FROM + i)
                        for n, (r, b) in enumerate(spans):
                            act.wait_ge(S("proj_lat" if n == 0 else "proj", j), FROM + i + 1)
                            nc.scalar.activation(sq[j][:, r], raw[j][:, b], ACT.Square).then_inc(S("squared", j), 1)
                        act.wait_ge(S("mean", j), FROM + 2 * i + 2)
                        act.wait_ge(S("inverse", j), FROM + i)
                        nc.scalar.activation(rt[j][:], ms[j][:], ACT.Sqrt).then_inc(S("rooted", j), 1)

            @block.vector
            def _(dve):
                for n in range(NQ + NKV):
                    nc.vector.tensor_copy(g[:, n:n + 1], K.v("q_g" if n < NQ else "k_g")).then_inc(gains, 1)
                dve.wait_ge(gains, FROM + NQ + NKV)
                with dve.Fori(0, n_it) as i:
                    for j in range(2):
                        dve.wait_ge(S("summed", j), FROM + i + 1)
                        for r, b in spans:
                            nc.vector.tensor_scalar(ms[j][:, r], ss[:, b], 1.0 / HD, EPS, ALU.mult, ALU.add
                                                    ).then_inc(S("mean", j), 1)
                        dve.wait_ge(S("rooted", j), FROM + i + 1)
                        nc.vector.reciprocal(ms[j][:], rt[j][:]).then_inc(S("inverse", j), 1)
                        dve.wait_ge(S("inverse", j), FROM + i + 1)
                        dve.wait_ge(S("cosed", j), FROM + i)
                        dve.wait_ge(S("ctx_copied", j), FROM + i)
                        for r, b in spans:
                            nc.vector.scalar_tensor_tensor(out=qn[j][:, r], in0=raw[j][:, b], scalar=g[:, bass.ds(2 * i + j, 1)],
                                                           in1=ms[j][:, r], op0=ALU.mult, op1=ALU.mult
                                                           ).then_inc(S("normed", j), 1)
                        dve.wait_ge(S("swapped", j), FROM + i + 1)
                        dve.wait_ge(S("written", j), FROM + i)
                        nc.vector.tensor_tensor(qs[j][:], rot[j][:], K.c("sin", LAT), ALU.mult).then_inc(S("sined", j), 1)

            @block.gpsimd
            def _(pool):
                with pool.Fori(0, n_it) as i:
                    for j in range(2):
                        pool.wait_ge(S("normed", j), FROM + 2 * i + 2)
                        pool.wait_ge(S("written", j), FROM + i)
                        nc.gpsimd.tensor_tensor(qc[j][:], qn[j][:, LATR], K.c("cos", LAT), ALU.mult).then_inc(S("cosed", j), 1)
                        head = qk[:, bass.ds(2 * i + j, 1), :].rearrange("p o t -> p (o t)")
                        nc.gpsimd.tensor_copy(head[:, CTXR], qn[j][:, CTXR]).then_inc(S("ctx_copied", j), 1)
                        pool.wait_ge(S("cosed", j), FROM + i + 1)
                        pool.wait_ge(S("sined", j), FROM + i + 1)
                        nc.gpsimd.tensor_tensor(head[:, LATR], qc[j][:], qs[j][:], ALU.add).then_inc(S("written", j), 1)


def project_v_conv(K, A, v, o):
    nc, h = K.nc, K.h
    with ExitStack() as ctx:
        wv = K.sb("v_w", [P, NKV, KD, P], ctx)
        w = [[K.sb(f"conv_w{j}_{m}", [P, KD, P], ctx) for m in range(3)] for j in range(2)]
        PADC, PADL = 1, CTX + 3
        gc = [K.sb(f"conv_gc{j}", [P, TOK], ctx) for j in range(2)]
        u = [K.sb(f"conv_u{j}", [P, TOK + 4], ctx) for j in range(2)]
        y = [K.sb(f"conv_y{j}", [P, TOK], ctx) for j in range(2)]
        pv = [K.ps(f"v_p{j}", [P, 512], ctx) for j in range(2)]
        pg = [K.ps(f"conv_p{m}", [P, 1024], ctx) for m in range(3)]
        wv_ready, v_prod, v_out, zeroed = (K.sem(f"v_{n}") for n in ("w_ready", "product", "copied", "pads_zeroed"))
        sems = {n: [K.sem(f"conv_{n}{j}") for j in range(2)] for n in
                ("w_ready", "copied", "gated", "mid", "left", "right", "written")}
        prod = [K.sem(f"conv_product{m}") for m in range(3)]
        S = lambda n, j: sems[n][j]
        spans = ((LATR, slice(0, LAT)), (CTXR, slice(512, 512 + CTX)))
        segs = ((LATR, PADL, slice(0, LAT)), (CTXR, PADC, slice(512, 512 + CTX)))
        FIRST = (28, 20, 12)
        ORDER = (1, 0, 2)
        n_it = KD // 2
        VCH = NQ + NKV

        def col(name, c):
            return K.vec[:, bass.ds(c + VEC[name], 1)]

        with nc.Block() as block:
            @block.sync
            def _(sp):
                for m in range(NKV):
                    sp.dma_start(wv[:, m], A["w_in"][VCH + m]).then_inc(wv_ready, 16)
                with sp.Fori(0, n_it) as i:
                    for j in range(2):
                        sp.wait_ge(S("written", j), FROM + i)
                        for m in ORDER:
                            sp.dma_start(w[j][m][:], A["w_in"][bass.ds(2 * i + j + FIRST[m], 1)].rearrange("o p k n -> (o p) k n")
                                         ).then_inc(S("w_ready", j), 16)

            @block.tensor
            def _(pe):
                pe.wait_ge(wv_ready, 16 * NKV)
                for t in range(NT):
                    if t >= 2:
                        pe.wait_ge(v_out, FROM + t - 1)
                    for m in range(NKV):
                        for k in range(KD):
                            last = nc.tensor.matmul(pv[t % 2][:, m * P:(m + 1) * P], h[:, k, t * P:(t + 1) * P], wv[:, m, k, :],
                                                    start=k == 0, stop=k == KD - 1)
                    last.then_inc(v_prod, 1)
                with pe.Fori(0, n_it) as i:
                    for j in range(2):
                        pe.wait_ge(S("w_ready", j), 48 * i + 48)
                        for m in ORDER:
                            if j == 1:
                                pe.wait_ge(S(("gated", "copied", "written")[m], 0), FROM + (2, 2, 1)[m] * (i + 1))
                            else:
                                pe.wait_ge(S(("gated", "copied", "written")[m], 1), FROM + (2, 2, 1)[m] * i)
                            for r, b in spans:
                                for k in range(KD):
                                    last = nc.tensor.matmul(pg[m][:, b], w[j][m][:, k, :], h[:, k, r], start=k == 0, stop=k == KD - 1)
                            last.then_inc(prod[m], 1)

            @block.scalar
            def _(act):
                for t in range(NT):
                    act.wait_ge(v_prod, FROM + t + 1)
                    nc.scalar.activation(v[:, t, :], pv[t % 2][:, 0:NKV * P], ACT.Copy).then_inc(v_out, 1)
                with act.Fori(0, n_it) as i:
                    for j in range(2):
                        act.wait_ge(prod[1], FROM + 2 * i + j + 1)
                        act.wait_ge(S("gated", j), FROM + 2 * i)
                        for r, b in spans:
                            nc.scalar.activation(gc[j][:, r], pg[1][:, b], ACT.Copy).then_inc(S("copied", j), 1)

            @block.vector
            def _(dve):
                for j in range(2):
                    nc.vector.memset(u[j][:], 0.0).then_inc(zeroed, 1)
                dve.wait_ge(zeroed, FROM + 2)
                with dve.Fori(0, n_it) as i:
                    for j in range(2):
                        c = 2 * i + j
                        dve.wait_ge(prod[0], FROM + 2 * i + j + 1)
                        dve.wait_ge(S("copied", j), FROM + 2 * i + 2)
                        dve.wait_ge(S("written", j), FROM + i)
                        for r, at, b in segs:
                            n = r.stop - r.start
                            nc.vector.tensor_tensor(u[j][:, at:at + n], pg[0][:, b], gc[j][:, r], ALU.mult
                                                    ).then_inc(S("gated", j), 1)
                        dve.wait_ge(S("gated", j), FROM + 2 * i + 2)
                        for r, at, b in segs:
                            n = r.stop - r.start
                            nc.vector.tensor_scalar(y[j][:, r], u[j][:, at:at + n], col("conv_w", c + KD), None, ALU.mult
                                                    ).then_inc(S("mid", j), 1)
                        dve.wait_ge(S("mid", j), FROM + 2 * i + 2)
                        for r, at, b in segs:
                            n = r.stop - r.start
                            nc.vector.scalar_tensor_tensor(out=y[j][:, r], in0=u[j][:, at - 1:at - 1 + n], scalar=col("conv_w", c),
                                                           in1=y[j][:, r], op0=ALU.mult, op1=ALU.add).then_inc(S("left", j), 1)
                        dve.wait_ge(S("left", j), FROM + 2 * i + 2)
                        for r, at, b in segs:
                            n = r.stop - r.start
                            nc.vector.scalar_tensor_tensor(out=y[j][:, r], in0=u[j][:, at + 1:at + 1 + n], scalar=col("conv_w", c + 2 * KD),
                                                           in1=y[j][:, r], op0=ALU.mult, op1=ALU.add).then_inc(S("right", j), 1)
                        dve.wait_ge(S("right", j), FROM + 2 * i + 2)
                        dve.wait_ge(prod[2], FROM + 2 * i + j + 1)
                        dst = o[:, bass.ds(c + NQ, 1), :].rearrange("p o t -> p (o t)")
                        for r, at, b in segs:
                            op = nc.vector.tensor_tensor(dst[:, r], pg[2][:, b], y[j][:, r], ALU.mult)
                        op.then_inc(S("written", j), 1)


def attend(K, qk, v, o):
    nc = K.nc
    SCALE = HD ** -0.5
    TILES = [(kv, t, NT if t >= CT else CT) for kv in range(NKV) for t in list(range(CT, NT)) + list(range(CT))]
    n_tiles = len(TILES)
    half = n_tiles // 2
    with ExitStack() as ctx:
        qs = [K.sb(f"at_q{kv}", [P, TOK], ctx) for kv in range(NKV)]
        p = [K.sb(f"at_p{j}", [P, TOK], ctx) for j in range(2)]
        mx = [K.sb(f"at_max{j}", [P, 1], ctx) for j in range(2)]
        sm = [K.sb(f"at_sum{j}", [P, 1], ctx) for j in range(2)]
        rc = [K.sb(f"at_rec{j}", [P, 1], ctx) for j in range(2)]
        nb = [K.sb(f"at_bias{j}", [P, 1], ctx) for j in range(2)]
        ptl = [K.sb(f"at_ptl{kv}", [P, NT, LAT], ctx) for kv in range(NKV)]
        ptc = [K.sb(f"at_ptc{kv}", [P, CT, CTX], ctx) for kv in range(NKV)]
        sc = [K.ps(f"at_s{j}", [P, 1024], ctx) for j in range(2)]
        tr = K.ps("at_t", [P, 1024], ctx)
        po = K.ps("at_o", [P, 1024], ctx)
        per = {n: [K.sem(f"at_{n}{j}") for j in range(2)] for n in
               ("scored", "maxed", "biased", "exped", "summed", "scaled", "turned", "copied_a", "copied_v")}
        staged = [K.sem(f"at_staged{kv}") for kv in range(NKV)]
        summed_up = [K.sem(f"at_weighed{kv}") for kv in range(NKV)]
        out = [K.sem(f"at_out{kv}") for kv in range(NKV)]
        S = lambda n, j: per[n][j]
        with nc.Block() as block:
            @block.gpsimd
            def _(pool):
                with pool.Fori(0, QPK) as g:
                    for kv in range(NKV):
                        pool.wait_ge(summed_up[kv], FROM + g)
                        nc.gpsimd.tensor_copy(qs[kv][:], qk[:, bass.ds(g + kv * QPK, 1), :].rearrange("p o t -> p (o t)")
                                              ).then_inc(staged[kv], 1)

            @block.tensor
            def _(pe):
                def scores(g, n):
                    kv, t, keys = TILES[n]
                    j = n % 2
                    pe.wait_ge(staged[kv], FROM + g + 1)
                    pe.wait_ge(S("exped", j), FROM + half * g + n // 2)
                    last = nc.tensor.matmul(sc[j][:, 0:min(keys * P, 512)], qs[kv][:, t * P:(t + 1) * P],
                                            qk[:, NQ + kv, 0:min(keys * P, 512)], start=True, stop=True)
                    if keys > 4:
                        last = nc.tensor.matmul(sc[j][:, 512:keys * P], qs[kv][:, t * P:(t + 1) * P],
                                                qk[:, NQ + kv, 512:keys * P], start=True, stop=True)
                    last.then_inc(S("scored", j), 1)

                def turn(g, n):
                    kv, t, keys = TILES[n]
                    j = n % 2
                    pe.wait_ge(S("scaled", j), FROM + half * g + n // 2 + 1)
                    m = (half * g + n // 2 + (0 if j == 0 else 1))
                    pe.wait_ge(S("copied_a", 1 - j), FROM + m)
                    pe.wait_ge(S("copied_v", 1 - j), FROM + m)
                    for b in range(keys):
                        at = b * P if b < keys // 2 else 512 + (b - keys // 2) * P
                        last = nc.tensor.transpose(tr[:, at:at + P], p[j][:, b * P:(b + 1) * P], K.c("ident"))
                    last.then_inc(S("turned", j), 1)

                def weigh(g, kv):
                    for j in range(2):
                        m = half * g + (kv + 1) * half // 2
                        pe.wait_ge(S("copied_a", j), FROM + m)
                        pe.wait_ge(S("copied_v", j), FROM + m)
                    if kv == 1:
                        pe.wait_ge(out[0], FROM + 2 * g + 2)
                    else:
                        pe.wait_ge(out[1], FROM + 2 * g)
                    for b in range(NT):
                        nc.tensor.matmul(po[:, 0:LAT], v[:, b, kv * HD:(kv + 1) * HD], ptl[kv][:, b, :], start=b == 0, stop=b == NT - 1)
                    for b in range(CT):
                        last = nc.tensor.matmul(po[:, 512:512 + CTX], v[:, b, kv * HD:(kv + 1) * HD], ptc[kv][:, b, :],
                                                start=b == 0, stop=b == CT - 1)
                    last.then_inc(summed_up[kv], 1)

                with pe.Fori(0, QPK) as g:
                    scores(g, 0)
                    for n in range(n_tiles):
                        if n + 1 < n_tiles:
                            scores(g, n + 1)
                        turn(g, n)
                        if n == half:
                            weigh(g, 0)
                    weigh(g, 1)

            @block.vector
            def _(dve):
                def tile(g, n):
                    kv, t, keys = TILES[n]
                    j = n % 2
                    m = half * g + n // 2
                    dve.wait_ge(S("scored", j), FROM + m + 1)
                    dve.wait_ge(S("biased", j), FROM + m)
                    nc.vector.tensor_reduce(mx[j][:], sc[j][:, 0:keys * P], AX.X, ALU.max).then_inc(S("maxed", j), 1)

                def scale(g, n):
                    kv, t, keys = TILES[n]
                    j = n % 2
                    m = half * g + n // 2
                    dve.wait_ge(S("exped", j), FROM + m + 1)
                    nc.vector.reciprocal(rc[j][:], sm[j][:]).then_inc(S("summed", j), 1)
                    dve.wait_ge(S("summed", j), FROM + m + 1)
                    nc.vector.tensor_scalar(p[j][:, 0:keys * P], p[j][:, 0:keys * P], rc[j][:], None, ALU.mult
                                            ).then_inc(S("scaled", j), 1)

                def copy(g, n):
                    kv, t, keys = TILES[n]
                    j = n % 2
                    m = half * g + n // 2
                    dve.wait_ge(S("turned", j), FROM + m + 1)
                    dve.wait_ge(summed_up[kv], FROM + g)
                    lo = keys // 2
                    dst = ptl[kv][:, lo:keys, (t - CT) * P:(t - CT + 1) * P] if t >= CT else ptc[kv][:, lo:keys, t * P:(t + 1) * P]
                    nc.vector.tensor_copy(dst, tr[:, 512:512 + (keys - lo) * P].rearrange("p (b q) -> p b q", q=P)
                                          ).then_inc(S("copied_v", j), 1)

                def store(g, kv):
                    dve.wait_ge(summed_up[kv], FROM + g + 1)
                    dst = o[:, bass.ds(g + kv * QPK, 1), :].rearrange("p o t -> p (o t)")
                    nc.vector.tensor_copy(dst[:, LATR], po[:, 0:LAT]).then_inc(out[kv], 1)
                    nc.vector.tensor_copy(dst[:, CTXR], po[:, 512:512 + CTX]).then_inc(out[kv], 1)

                with dve.Fori(0, QPK) as g:
                    tile(g, 0)
                    for n in range(n_tiles):
                        scale(g, n)
                        if n + 1 < n_tiles:
                            tile(g, n + 1)
                        copy(g, n)
                        if n == half + 1:
                            store(g, 0)
                    store(g, 1)

            @block.scalar
            def _(act):
                def exps(g, n):
                    kv, t, keys = TILES[n]
                    j = n % 2
                    m = half * g + n // 2
                    act.wait_ge(S("maxed", j), FROM + m + 1)
                    act.wait_ge(S("exped", j), FROM + m)
                    nc.scalar.mul(nb[j][:], mx[j][:], -SCALE).then_inc(S("biased", j), 1)
                    act.wait_ge(S("biased", j), FROM + m + 1)
                    act.wait_ge(S("turned", j), FROM + m)
                    act.wait_ge(S("summed", j), FROM + m)
                    nc.scalar.activation(p[j][:, 0:keys * P], sc[j][:, 0:keys * P], ACT.Exp, bias=nb[j][:], scale=SCALE,
                                         accum_out=sm[j][:]).then_inc(S("exped", j), 1)

                def copy(g, n):
                    kv, t, keys = TILES[n]
                    j = n % 2
                    m = half * g + n // 2
                    act.wait_ge(S("turned", j), FROM + m + 1)
                    act.wait_ge(summed_up[kv], FROM + g)
                    hi = keys // 2
                    dst = ptl[kv][:, 0:hi, (t - CT) * P:(t - CT + 1) * P] if t >= CT else ptc[kv][:, 0:hi, t * P:(t + 1) * P]
                    nc.scalar.activation(dst, tr[:, 0:hi * P].rearrange("p (b q) -> p b q", q=P), ACT.Copy
                                         ).then_inc(S("copied_a", j), 1)

                with act.Fori(0, QPK) as g:
                    exps(g, 0)
                    for n in range(n_tiles):
                        if n + 1 < n_tiles:
                            exps(g, n + 1)
                        copy(g, n)


def project_out(K, tag, weights, o, chunks, layer, ranges, spilled=None):
    nc, x = K.nc, K.x
    with ExitStack() as ctx:
        w = [K.sb(f"{tag}_w{j}", [P, chunks, P], ctx) for j in range(2)]
        ps = [K.ps(f"{tag}_p{j}", [P, 1024], ctx) for j in range(2)]
        w_ready = [K.sem(f"{tag}_w_ready{j}") for j in range(2)]
        prod = [K.sem(f"{tag}_product{j}") for j in range(2)]
        added = [K.sem(f"{tag}_added{j}") for j in range(2)]
        x_back = K.sem(f"{tag}_x_back")
        bank = {0: slice(0, LAT), 1: slice(512, 512 + CTX)}
        n_it = KD // 2
        with nc.Block() as block:
            @block.sync
            def _(sp):
                if spilled is not None:
                    sp.dma_start(x[:], spilled).then_inc(x_back, 16)
                with sp.Fori(0, n_it) as i:
                    for j in range(2):
                        sp.wait_ge(prod[j], FROM + i)
                        sp.dma_start(w[j][:], weights[bass.ds(2 * i + j, 1)].rearrange("o p k n -> (o p) k n")
                                     ).then_inc(w_ready[j], 16)

            @block.tensor
            def _(pe):
                with pe.Fori(0, n_it) as i:
                    for j in range(2):
                        pe.wait_ge(w_ready[j], 16 * i + 16)
                        pe.wait_ge(added[j], FROM + len(ranges) * i)
                        for s, r in ranges:
                            ro = slice(r.start - TOK + o.shape[2], r.stop - TOK + o.shape[2])
                            for k in range(chunks):
                                last = nc.tensor.matmul(ps[j][:, bank[s]], w[j][:, k, :], o[:, k, ro], start=k == 0, stop=k == chunks - 1)
                        last.then_inc(prod[j], 1)

            @block.vector
            def _(dve):
                if spilled is not None:
                    dve.wait_ge(x_back, 16)
                with dve.Fori(0, n_it) as i:
                    for j in range(2):
                        dve.wait_ge(prod[j], FROM + i + 1)
                        xs = x[:, bass.ds(2 * i + j, 1), :].rearrange("p o t -> p (o t)")
                        for s, r in ranges:
                            gate = K.mod[:, s, bass.ds(2 * i + j + (layer * 6 + 2) * KD, 1)]
                            nc.vector.scalar_tensor_tensor(out=xs[:, r], in0=ps[j][:, bank[s]], scalar=gate, in1=xs[:, r],
                                                           op0=ALU.mult, op1=ALU.add).then_inc(added[j], 1)


def route(K, A, tag, layer, h2, slot, aff):
    nc, h = K.nc, K.h
    ctx_too = layer == 0
    tiles = list(range(0 if ctx_too else CT, NT))
    t0 = tiles[0]
    n = len(tiles)
    kinds = [(LATR, slice(0, LAT), CAP_L)] + ([(CTXR, slice(512, 512 + CTX), CAP_C)] if ctx_too else [])
    at = lambda t: (t - CT) * P if t >= CT else 512 + t * P
    with ExitStack() as ctx:
        rw = K.sb(f"{tag}_router", [P, KD, E], ctx)
        lg = K.sb(f"{tag}_logits", [E, TOK], ctx)
        ex = K.sb(f"{tag}_ex", [P, n, E], ctx)
        mx = K.sb(f"{tag}_mx", [P, n], ctx)
        rs = K.sb(f"{tag}_rs", [P, n], ctx)
        rr = K.sb(f"{tag}_rr", [P, n], ctx)
        work = K.sb(f"{tag}_work", [E, TOK], ctx)
        top = K.sb(f"{tag}_top", [E, 8], ctx)
        ones = K.sb(f"{tag}_ones", [E, TOK], ctx)
        cnt = K.sb(f"{tag}_cnt", [E, TOK], ctx)
        pl = K.ps(f"{tag}_pl", [E, 1024], ctx)
        pt = K.ps(f"{tag}_pt", [P, 512], ctx)
        pa = K.ps(f"{tag}_pa", [E, 1024], ctx)
        ph = [K.ps(f"{tag}_ph{j}", [P, 512], ctx) for j in range(2)]
        (loaded, logits, copied, turned, maxed, shifted, exped, summed, inv, affs, aff_turned, worked, found, replaced,
         picked, counted, placed, slot_turned) = (K.sem(f"{tag}_{x}") for x in (
             "router_loaded", "logits", "logits_copied", "logits_turned", "max", "shifted", "exped", "summed", "inverse",
             "affinity", "affinity_turned", "work", "top", "replaced", "picked", "counted", "placed", "slot_turned"))
        h_turned = [K.sem(f"{tag}_h_turned{j}") for j in range(2)]
        h_copied = [K.sem(f"{tag}_h_copied{j}") for j in range(2)]
        groups = [(t, g) for t in tiles for g in range(KD // 4)]
        with nc.Block() as block:
            @block.sync
            def _(sp):
                sp.dma_start(rw[:], A["router"][layer]).then_inc(loaded, 16)

            @block.tensor
            def _(pe):
                pe.wait_ge(loaded, 16)
                for r, b, _ in kinds:
                    for k in range(KD):
                        last = nc.tensor.matmul(pl[:, b], rw[:, k, :], h[:, k, r], start=k == 0, stop=k == KD - 1)
                last.then_inc(logits, 1)

                def turn_h(lo, hi):
                    for m in range(lo, hi):
                        t, g = groups[m]
                        if m >= 2:
                            pe.wait_ge(h_copied[m % 2], FROM + m // 2)
                        for k in range(4):
                            last = nc.tensor.transpose(ph[m % 2][:, k * P:(k + 1) * P], h[:, 4 * g + k, t * P:(t + 1) * P], K.c("ident"))
                        last.then_inc(h_turned[m % 2], 1)

                turn_h(0, 2)
                pe.wait_ge(copied, FROM + len(kinds))
                for m, t in enumerate(tiles):
                    last = nc.tensor.transpose(pt[:, m * E:(m + 1) * E], lg[:, t * P:(t + 1) * P], K.c("ident")[0:E, 0:E])
                last.then_inc(turned, 1)
                turn_h(2, len(groups) // 2)
                pe.wait_ge(affs, FROM + 1)
                for m, t in enumerate(tiles):
                    last = nc.tensor.transpose(pa[:, at(t):at(t) + P], aff[:, t, :], K.c("ident"))
                last.then_inc(aff_turned, 1)
                turn_h(len(groups) // 2, len(groups))
                pe.wait_ge(placed, FROM + len(kinds))
                pe.wait_ge(shifted, FROM + 1)
                for m, t in enumerate(tiles):
                    last = nc.tensor.transpose(pt[:, m * E:(m + 1) * E], cnt[:, t * P:(t + 1) * P], K.c("ident")[0:E, 0:E])
                last.then_inc(slot_turned, 1)

            @block.scalar
            def _(act):
                act.wait_ge(logits, FROM + 1)
                for r, b, _ in kinds:
                    nc.scalar.activation(lg[:, r], pl[:, b], ACT.Copy).then_inc(copied, 1)

                def copy_h(lo, hi):
                    for m in range(lo, hi):
                        t, g = groups[m]
                        act.wait_ge(h_turned[m % 2], FROM + m // 2 + 1)
                        nc.scalar.activation(h2[:, t, 4 * g * P:(4 * g + 4) * P], ph[m % 2][:], ACT.Copy).then_inc(h_copied[m % 2], 1)

                copy_h(0, 2)
                act.wait_ge(shifted, FROM + 1)
                nc.scalar.activation(ex[:], ex[:], ACT.Exp).then_inc(exped, 1)
                copy_h(2, len(groups))

            @block.vector
            def _(dve):
                nc.vector.memset(ones[:], 1.0).then_inc(worked, 1)
                logit = pt[:, 0:n * E].rearrange("p (t e) -> p t e", e=E)
                dve.wait_ge(turned, FROM + 1)
                nc.vector.tensor_reduce(mx[:], logit, AX.X, ALU.max).then_inc(maxed, 1)
                dve.wait_ge(maxed, FROM + 1)
                nc.vector.tensor_tensor(ex[:], logit, mx[:].unsqueeze(2).broadcast_to([P, n, E]), ALU.subtract).then_inc(shifted, 1)
                dve.wait_ge(exped, FROM + 1)
                nc.vector.tensor_reduce(rs[:], ex[:], AX.X, ALU.add).then_inc(summed, 1)
                dve.wait_ge(summed, FROM + 1)
                nc.vector.reciprocal(rr[:], rs[:]).then_inc(inv, 1)
                dve.wait_ge(inv, FROM + 1)
                nc.vector.tensor_tensor(aff[:, t0:NT, :], ex[:], rr[:].unsqueeze(2).broadcast_to([P, n, E]), ALU.mult).then_inc(affs, 1)
                dve.wait_ge(aff_turned, FROM + 1)
                for r, b, _ in kinds:
                    nc.vector.tensor_copy(work[:, r], pa[:, b]).then_inc(worked, 1)
                rounds = 0
                for r, b, cap in kinds:
                    dve.wait_ge(worked, FROM + 1 + len(kinds))
                    for _ in range(cap // 8):
                        dve.wait_ge(replaced, FROM + rounds) if rounds else None
                        nc.vector.max(top[:], work[:, r]).then_inc(found, 1)
                        rounds += 1
                        dve.wait_ge(found, FROM + rounds)
                        nc.vector.match_replace(work[:, r], top[:], work[:, r], -1.0).then_inc(replaced, 1)
                dve.wait_ge(replaced, FROM + rounds)
                for m, (r, b, _) in enumerate(kinds):
                    nc.vector.tensor_scalar(work[:, r], work[:, r], 0.0, None, ALU.is_lt).then_inc(picked, 1)
                    dve.wait_ge(picked, FROM + m + 1)
                    nc.vector.tensor_tensor_scan(cnt[:, r], ones[:, r], work[:, r], 0.0, ALU.mult, ALU.add).then_inc(counted, 1)
                    dve.wait_ge(counted, FROM + 2 * m + 1)
                    nc.vector.tensor_tensor(cnt[:, r], cnt[:, r], work[:, r], ALU.mult).then_inc(counted, 1)
                    dve.wait_ge(counted, FROM + 2 * m + 2)
                    nc.vector.tensor_scalar(cnt[:, r], cnt[:, r], -1.0, None, ALU.add).then_inc(placed, 1)
                dve.wait_ge(slot_turned, FROM + 1)
                nc.vector.tensor_copy(slot[:, t0:NT, :], logit)


def experts(K, A, tag, layer, h2, slot, aff):
    nc, x = K.nc, K.x
    ctx_too = layer == 0
    Q = 4
    NS = CAP_L + CAP_C if ctx_too else CAP_L
    NR = CAP_L + CAP_C
    with ExitStack() as ctx:
        hm_ = K.h[:].rearrange("p k t -> p (k t)")
        XS, SL, SCX = KD * Q * NS, NT - CT, CT
        xs = hm_[:, 0:XS].rearrange("p (k e j) -> p k e j", k=KD, e=Q)
        o = XS
        sel_l = hm_[:, o:o + SL * Q * CAP_L].rearrange("p (t e j) -> p t e j", t=SL, e=Q)
        o += SL * Q * CAP_L
        sw_l = hm_[:, o:o + SL * Q * CAP_L].rearrange("p (t e j) -> p t e j", t=SL, e=Q)
        o += SL * Q * CAP_L
        sel_c = hm_[:, o:o + SCX * Q * CAP_C].rearrange("p (t e j) -> p t e j", t=SCX, e=Q)
        o += SCX * Q * CAP_C
        sw_c = hm_[:, o:o + SCX * Q * CAP_C].rearrange("p (t e j) -> p t e j", t=SCX, e=Q)
        w = [K.sb(f"{tag}_w{s}", [P, 4096], ctx) for s in range(6)]
        put_l = K.sb(f"{tag}_put_l", [P, 2, LAT], ctx)
        put_c = K.sb(f"{tag}_put_c", [P, CTX], ctx)
        sg = [K.sb(f"{tag}_sg{f}", [NS, 512], ctx) for f in range(2)]
        hid = [K.sb(f"{tag}_hid{f}", [NR, 512], ctx) for f in range(2)]
        hidT = [K.sb(f"{tag}_hidT{f}", [P, 4, NS], ctx) for f in range(2)]
        out_l = K.sb(f"{tag}_out_l", [P, D], ctx)
        out_c = K.sb(f"{tag}_out_c", [P, D], ctx)
        pg = [K.ps(f"{tag}_pg{f}", [P, 512], ctx) for f in range(2)]
        pu = [K.ps(f"{tag}_pu{f}", [P, 512], ctx) for f in range(2)]
        pt = [K.ps(f"{tag}_pt{f}", [P, 512], ctx) for f in range(2)]
        pd = [K.ps(f"{tag}_pd{f}", [P, 512], ctx) for f in range(2)]
        sem = lambda n: K.sem(f"{tag}_{n}")
        two = lambda n: [sem(f"{n}{f}") for f in range(2)]
        w_ready = [sem(f"w_ready{s}") for s in range(6)]
        selected, weighted, put_turned, put_copied = (sem(n) for n in ("selected", "weighted", "put_turned", "put_copied"))
        gathered, xs_copied = two("gathered"), two("xs_copied")
        gated, upped, silued, hidden, turned, hid_copied, downed = (two(n) for n in (
            "gated", "upped", "silued", "hidden", "turned", "hid_copied", "downed"))
        out_copied = two("out_copied")
        spread, added = two("spread"), two("added")
        NB = KD // 2 * (3 if ctx_too else 2)
        padded = sem("padded")
        NPUT = 3 if ctx_too else 2
        views = [w[s][:].rearrange("p (k n) -> p k n", n=512) for s in range(4)] + \
                [w[s][:].rearrange("p (k n) -> p k n", n=D) for s in (4, 5)]
        gate_w, up_w, down_w = (A["moe_" + n][layer] for n in ("gate", "up", "down"))
        with nc.Block() as block:
            @block.sync
            def _(sp):
                with sp.Fori(0, E // Q) as q:
                    for e in range(Q):
                        for s in range(6):
                            sp.wait_ge((gated[0], upped[0], gated[1], upped[1], downed[0], downed[1])[s], FROM + Q * q + e)
                            if s < 4:
                                m = (gate_w, up_w)[s % 2][bass.ds(Q * q + e, 1)]
                                src = m.rearrange("o (k p) f -> (o p) k f", p=P)[:, :, 512 * (s // 2):512 * (s // 2) + 512]
                            else:
                                m = down_w[bass.ds(Q * q + e, 1)]
                                src = m.rearrange("o (k p) f -> (o p) k f", p=P)[:, 4 * (s - 4):4 * (s - 4) + 4, :]
                            sp.dma_start(views[s], src).then_inc(w_ready[s], 16)

            @block.tensor
            def _(pe):
                def gather(q):
                    pe.wait_ge(selected, FROM + q + 1)
                    for k in range(KD):
                        b = k % 2
                        pe.wait_ge(xs_copied[b], FROM + 4 * q + k // 2)
                        if k < 2:
                            pe.wait_ge(hid_copied[b], FROM + Q * q)
                        for t in range(SL):
                            last = nc.tensor.matmul(pt[b][:, 0:Q * CAP_L], h2[:, CT + t, k * P:(k + 1) * P], sel_l[:, t].rearrange("p e j -> p (e j)"),
                                                    start=t == 0, stop=t == SL - 1)
                        if ctx_too:
                            for t in range(CT):
                                last = nc.tensor.matmul(pt[b][:, 256:256 + Q * CAP_C], h2[:, t, k * P:(k + 1) * P], sel_c[:, t].rearrange("p e j -> p (e j)"),
                                                        start=t == 0, stop=t == CT - 1)
                        last.then_inc(gathered[b], 1)

                def turn_put(q):
                    pe.wait_ge(weighted, FROM + q + 1)
                    for f in range(2):
                        pe.wait_ge(silued[f], FROM + Q * q)
                    for pr in range(2):
                        for t in range(SL):
                            last = nc.tensor.transpose(pg[pr][:, t * P:(t + 1) * P], sw_l[:, t, 2 * pr:2 * pr + 2, :].rearrange("p e j -> p (e j)"), K.c("ident"))
                        last.then_inc(put_turned, 1)
                    if ctx_too:
                        pe.wait_ge(hidden[0], FROM + Q * q)
                        for t in range(CT):
                            last = nc.tensor.transpose(pu[0][:, t * P:(t + 1) * P], sw_c[:, t].rearrange("p e j -> p (e j)"), K.c("ident"))
                        last.then_inc(put_turned, 1)

                def gate_up(q, e):
                    n = Q * q + e
                    if e == 0:
                        for b in range(2):
                            pe.wait_ge(xs_copied[b], FROM + 4 * q + 4)
                        pe.wait_ge(put_copied, FROM + NPUT * q + NPUT)
                    for f in range(2):
                        for m, (bank, done, used) in enumerate(((pg, gated, silued), (pu, upped, hidden))):
                            s = 2 * f + m
                            pe.wait_ge(w_ready[s], 16 * n + 16)
                            pe.wait_ge(used[f], FROM + n)
                            for k in range(KD):
                                last = nc.tensor.matmul(bank[f][0:NS, :], xs[:, k, e, :], views[s][:, k, :], start=k == 0, stop=k == KD - 1)
                            last.then_inc(done[f], 1)

                def down(q, e):
                    n = Q * q + e
                    for f in range(2):
                        pe.wait_ge(hidden[f], FROM + n + 1)
                        if not (e == 0):
                            pe.wait_ge(hid_copied[f], FROM + n)
                        else:
                            pe.wait_ge(xs_copied[f], FROM + 4 * q + 4)
                        for c in range(4):
                            last = nc.tensor.transpose(pt[f][:, c * NR:(c + 1) * NR], hid[f][:, c * P:(c + 1) * P], K.c("ident")[0:NR, 0:NR])
                        last.then_inc(turned[f], 1)
                        pe.wait_ge(hid_copied[f], FROM + n + 1)
                        pe.wait_ge(w_ready[4 + f], 16 * n + 16)
                        if f == 0:
                            for b in range(2):
                                pe.wait_ge(out_copied[b], FROM + n)
                                pe.wait_ge(added[b], FROM + (NB * q + (4 if e >= 2 else 0)))
                        for b in range(2):
                            for c in range(4):
                                last = nc.tensor.matmul(pd[b][0:NS, :], hidT[f][:, c, :], views[4 + f][:, c, b * 512:(b + 1) * 512],
                                                        start=f == 0 and c == 0, stop=f == 1 and c == 3)
                        last.then_inc(downed[f], 1)

                def spread_out(q, part):
                    n = Q * q + (2, 4, 4)[part]
                    for b in range(2):
                        pe.wait_ge(out_copied[b], FROM + n)
                    for k in range(KD):
                        b = k % 2
                        pe.wait_ge(added[b], FROM + NB * q + 4 * part + k // 2)
                        if part < 2:
                            last = nc.tensor.matmul(pd[b][:], out_l[:, k * P:(k + 1) * P], put_l[:, part, :], start=True, stop=True)
                        else:
                            last = nc.tensor.matmul(pd[b][:, 0:CTX], out_c[:, k * P:(k + 1) * P], put_c[:], start=True, stop=True)
                        last.then_inc(spread[b], 1)

                with pe.Fori(0, E // Q) as q:
                    gather(q)
                    turn_put(q)
                    for e in range(Q):
                        gate_up(q, e)
                        if e == 2:
                            spread_out(q, 0)
                        down(q, e)
                    spread_out(q, 1)
                    if ctx_too:
                        spread_out(q, 2)

            @block.scalar
            def _(act):
                def copy_xs(q):
                    for k in range(0, KD, 2):
                        act.wait_ge(gathered[0], FROM + 4 * q + k // 2 + 1)
                        if k == 0:
                            act.wait_ge(upped[1], FROM + Q * q)
                        last = nc.scalar.activation(xs[:, k, :, 0:CAP_L], pt[0][:, 0:Q * CAP_L].rearrange("p (e j) -> p e j", e=Q), ACT.Copy)
                        if ctx_too:
                            last = nc.scalar.activation(xs[:, k, :, CAP_L:NS], pt[0][:, 256:256 + Q * CAP_C].rearrange("p (e j) -> p e j", e=Q), ACT.Copy)
                        last.then_inc(xs_copied[0], 1)

                def copy_out(q, e):
                    n = Q * q + e
                    act.wait_ge(downed[1], FROM + n + 1)
                    act.wait_ge(spread[1], FROM + (NB * q + (4 if e >= 2 else 0)))
                    row = CAP_L * (e % 2)
                    last = nc.scalar.activation(out_l[row:row + CAP_L, 0:512], pd[0][0:CAP_L, :], ACT.Copy)
                    if ctx_too:
                        last = nc.scalar.activation(out_c[CAP_C * e:CAP_C * e + CAP_C, 0:512], pd[0][CAP_L:NS, :], ACT.Copy)
                    last.then_inc(out_copied[0], 1)

                with act.Fori(0, E // Q) as q:
                    copy_xs(q)
                    for pr in range(2):
                        act.wait_ge(put_turned, FROM + NPUT * q + pr + 1)
                        act.wait_ge(spread[1], FROM + NB * q)
                        nc.scalar.activation(put_l[:, pr, :], pg[pr][:], ACT.Copy).then_inc(put_copied, 1)
                    if ctx_too:
                        act.wait_ge(put_turned, FROM + NPUT * q + 3)
                        nc.scalar.activation(put_c[:], pu[0][:, 0:CTX], ACT.Copy).then_inc(put_copied, 1)
                    for e in range(Q):
                        n = Q * q + e
                        for f in range(2):
                            act.wait_ge(gated[f], FROM + n + 1)
                            act.wait_ge(hidden[f], FROM + n)
                            nc.scalar.activation(sg[f][:], pg[f][0:NS, :], ACT.Silu).then_inc(silued[f], 1)
                        act.wait_ge(turned[0], FROM + n + 1)
                        act.wait_ge(downed[0], FROM + n)
                        nc.scalar.activation(hidT[0][:], pt[0][:, 0:4 * NR].rearrange("p (c j) -> p c j", c=4)[:, :, 0:NS], ACT.Copy).then_inc(hid_copied[0], 1)
                        copy_out(q, e)

            @block.vector
            def _(dve):
                def select(q):
                    dve.wait_ge(gathered[1], FROM + 4 * q)
                    kinds = [(sel_l, sw_l, CT, SL, CAP_L)] + ([(sel_c, sw_c, 0, CT, CAP_C)] if ctx_too else [])
                    for sel, sw, t0, nt, cap in kinds:
                        for t in range(nt):
                            place = slot[:, t0 + t, bass.ds(Q * q, Q)].unsqueeze(2).broadcast_to([P, Q, cap])
                            last = nc.vector.tensor_tensor(sel[:, t], K.c("iota", cap).unsqueeze(1).broadcast_to([P, Q, cap]), place, ALU.is_equal)
                    last.then_inc(selected, 1)
                    dve.wait_ge(selected, FROM + q + 1)
                    dve.wait_ge(put_turned, FROM + NPUT * q)
                    for sel, sw, t0, nt, cap in kinds:
                        for t in range(nt):
                            a = aff[:, t0 + t, bass.ds(Q * q, Q)].unsqueeze(2).broadcast_to([P, Q, cap])
                            last = nc.vector.tensor_tensor(sw[:, t], sel[:, t], a, ALU.mult)
                    last.then_inc(weighted, 1)

                def copy_xs(q):
                    for k in range(1, KD, 2):
                        dve.wait_ge(gathered[1], FROM + 4 * q + k // 2 + 1)
                        if k == 1:
                            dve.wait_ge(upped[1], FROM + Q * q)
                        last = nc.vector.tensor_copy(xs[:, k, :, 0:CAP_L], pt[1][:, 0:Q * CAP_L].rearrange("p (e j) -> p e j", e=Q))
                        if ctx_too:
                            last = nc.vector.tensor_copy(xs[:, k, :, CAP_L:NS], pt[1][:, 256:256 + Q * CAP_C].rearrange("p (e j) -> p e j", e=Q))
                        last.then_inc(xs_copied[1], 1)

                def add(q, part):
                    for k in range(KD):
                        b = k % 2
                        dve.wait_ge(spread[b], FROM + NB * q + 4 * part + k // 2 + 1)
                        dve.wait_ge(added[b], FROM + NB * q + 4 * part + k // 2)
                        s, r, n = (0, LATR, LAT) if part < 2 else (1, CTXR, CTX)
                        nc.vector.scalar_tensor_tensor(out=x[:, k, r], in0=pd[b][:, 0:n], scalar=K.m(s, layer, 5, k), in1=x[:, k, r],
                                                       op0=ALU.mult, op1=ALU.add).then_inc(added[b], 1)

                def multiply(q, e):
                    n = Q * q + e
                    for f in range(2):
                        dve.wait_ge(silued[f], FROM + n + 1)
                        dve.wait_ge(upped[f], FROM + n + 1)
                        dve.wait_ge(turned[f], FROM + n)
                        nc.vector.tensor_tensor(hid[f][0:NS, :], sg[f][:], pu[f][0:NS, :], ALU.mult).then_inc(hidden[f], 1)

                def finish(q, e):
                    n = Q * q + e
                    dve.wait_ge(turned[1], FROM + n + 1)
                    dve.wait_ge(downed[1], FROM + n)
                    nc.vector.tensor_copy(hidT[1][:], pt[1][:, 0:4 * NR].rearrange("p (c j) -> p c j", c=4)[:, :, 0:NS]).then_inc(hid_copied[1], 1)
                    dve.wait_ge(downed[1], FROM + n + 1)
                    row = CAP_L * (e % 2)
                    dve.wait_ge(spread[1], FROM + (NB * q + (4 if e >= 2 else 0)))
                    last = nc.vector.tensor_copy(out_l[row:row + CAP_L, 512:D], pd[1][0:CAP_L, :])
                    if ctx_too:
                        last = nc.vector.tensor_copy(out_c[CAP_C * e:CAP_C * e + CAP_C, 512:D], pd[1][CAP_L:NS, :])
                    last.then_inc(out_copied[1], 1)

                if NR > NS:
                    for f in range(2):
                        nc.vector.memset(hid[f][NS:NR, :], 0.0).then_inc(padded, 1)
                    dve.wait_ge(padded, FROM + 2)
                with dve.Fori(0, E // Q) as q:
                    select(q)
                    copy_xs(q)
                    for e in range(Q):
                        multiply(q, e)
                        if e == 2:
                            add(q, 0)
                        finish(q, e)
                    add(q, 1)
                    if ctx_too:
                        add(q, 2)


def mixture(K, A, layer):
    with ExitStack() as ctx:
        tag = f"moe{layer}"
        norm(K, tag + "n", layer, 1)
        h2 = K.sb(f"{tag}_h2", [P, NT, D], ctx)
        slot = K.sb(f"{tag}_slot", [P, NT, E], ctx)
        aff = K.sb(f"{tag}_aff", [P, NT, E], ctx)
        route(K, A, tag + "r", layer, h2, slot, aff)
        experts(K, A, tag + "x", layer, h2, slot, aff)


def mix_and_project(K, A, scr, hid):
    nc, h = K.nc, K.h
    JOBS = (("k", 2), ("v", 3), ("r", 0), ("w1", 1), ("a1", 4), ("g1", 5))
    LORA_F = {"w1": ACT.Tanh, "a1": ACT.Copy, "g1": ACT.Sigmoid}
    with ExitStack() as ctx:
        xx = K.sb("mp_xx", [P, KD, TOK], ctx)
        mix = [K.sb(f"mp_mix{j}", [P, KD, TOK], ctx) for j in range(2)]
        w = [K.sb(f"mp_w{j}", [P, KD, P], ctx) for j in range(2)]
        lw = [K.sb(f"mp_lw{n}", [P, KD, P], ctx) for n in range(3)]
        st = [K.sb(f"mp_st{j}", [P, TOK], ctx) for j in range(2)]
        ps = [K.ps(f"mp_p{j}", [P, 1024], ctx) for j in range(2)]
        w_ready = [K.sem(f"mp_w_ready{j}") for j in range(2)]
        prod = [K.sem(f"mp_product{j}") for j in range(2)]
        copied = [K.sem(f"mp_copied{j}") for j in range(2)]
        stored = [K.sem(f"mp_stored{j}") for j in range(2)]
        spilled = K.sem("mp_x_stored")
        lora_ready, neighbours, mixed, lora = (K.sem(f"mp_{n}") for n in ("lora_ready", "neighbours", "mixed", "lora"))
        spans = ((LATR, slice(0, LAT)), (CTXR, slice(512, 512 + CTX)))
        n_it = KD // 2
        with nc.Block() as block:
            @block.sync
            def _(sp):
                for n, (name, _) in enumerate(JOBS[3:]):
                    sp.dma_start(lw[n][:], A[name]).then_inc(lora_ready, 16)
                sp.dma_start(scr["x"], K.x[:]).then_inc(spilled, 16)
                for m, (name, _) in enumerate(JOBS[:3]):
                    with sp.Fori(0, n_it) as i:
                        for j in range(2):
                            sp.wait_ge(prod[j], FROM + i + m * n_it)
                            sp.dma_start(w[j][:], A["rw_" + name][bass.ds(2 * i + j, 1)].rearrange("o p k n -> (o p) k n")
                                         ).then_inc(w_ready[j], 16)

            @block.vector
            def _(dve):
                for r in (CTXR, LATR):
                    lo, hi = r.start, r.stop
                    nc.vector.tensor_tensor(xx[:, :, lo + 1:hi - 1], h[:, :, lo:hi - 2], h[:, :, lo + 2:hi], ALU.add).then_inc(neighbours, 1)
                    nc.vector.tensor_copy(xx[:, :, lo:lo + 1], h[:, :, lo + 1:lo + 2]).then_inc(neighbours, 1)
                    nc.vector.tensor_copy(xx[:, :, hi - 1:hi], h[:, :, hi - 2:hi - 1]).then_inc(neighbours, 1)
                dve.wait_ge(neighbours, FROM + 6)
                for k in range(KD):
                    nc.vector.scalar_tensor_tensor(out=xx[:, k, :], in0=xx[:, k, :], scalar=0.5, in1=h[:, k, :],
                                                   op0=ALU.mult, op1=ALU.subtract).then_inc(neighbours, 1)
                for m, (name, row) in enumerate(JOBS):
                    if m == 0:
                        dve.wait_ge(neighbours, FROM + 6 + KD)
                    elif m >= 2 and m <= 4:
                        for j in range(2):
                            dve.wait_ge(prod[j], FROM + (m - 1) * n_it)
                    elif m == 5:
                        dve.wait_ge(lora, FROM + 1)
                    for k in range(KD):
                        nc.vector.scalar_tensor_tensor(out=mix[m % 2][:, k, :], in0=xx[:, k, :], scalar=K.v("mu", row * KD + k),
                                                       in1=h[:, k, :], op0=ALU.mult, op1=ALU.add).then_inc(mixed, 1)

            @block.tensor
            def _(pe):
                for m, (name, _) in enumerate(JOBS[:3]):
                    pe.wait_ge(mixed, FROM + KD * (m + 1))
                    with pe.Fori(0, n_it) as i:
                        for j in range(2):
                            pe.wait_ge(w_ready[j], 16 * i + 16 * (m * n_it + 1))
                            pe.wait_ge(copied[j], FROM + i + m * n_it)
                            for r, b in spans:
                                for k in range(KD):
                                    last = nc.tensor.matmul(ps[j][:, b], w[j][:, k, :], mix[m % 2][:, k, r], start=k == 0, stop=k == KD - 1)
                            last.then_inc(prod[j], 1)
                pe.wait_ge(lora_ready, 48)
                for n, (name, _) in enumerate(JOBS[3:]):
                    m = 3 + n
                    pe.wait_ge(mixed, FROM + KD * (m + 1))
                    pe.wait_ge(copied[n % 2], FROM + 3 * n_it + n // 2)
                    for r, b in spans:
                        for k in range(KD):
                            last = nc.tensor.matmul(ps[n % 2][:, b], lw[n][:, k, :], mix[m % 2][:, k, r], start=k == 0, stop=k == KD - 1)
                    last.then_inc(lora, 1)

            @block.scalar
            def _(act):
                for m, (name, _) in enumerate(JOBS[:3]):
                    with act.Fori(0, n_it) as i:
                        for j in range(2):
                            act.wait_ge(prod[j], FROM + i + (m * n_it + 1))
                            for r, b in spans:
                                last = nc.scalar.activation(st[j][:, r], ps[j][:, b], ACT.Copy)
                            last.then_inc(copied[j], 1)
                            act.wait_ge(copied[j], FROM + i + (m * n_it + 1))
                            act.dma_start(scr[name][bass.ds(2 * i + j, 1)].rearrange("o p t -> (o p) t"), st[j][:]
                                          ).then_inc(stored[j], 16)
                        for j in range(2):
                            act.wait_ge(stored[j], 16 * i + 16 * (m * n_it + 1))
                for n, (name, _) in enumerate(JOBS[3:]):
                    act.wait_ge(lora, FROM + n + 1)
                    for r, b in spans:
                        last = nc.scalar.activation(hid[name][:, r], ps[n % 2][:, b], LORA_F[name])
                    last.then_inc(copied[n % 2], 1)
                for j in range(2):
                    act.wait_ge(stored[j], 16 * 3 * n_it)
                act.wait_ge(spilled, 16)


class Chain:

    def __init__(self, eng, sem, i, per):
        self.eng, self.sem, self.i, self.per, self.n = eng, sem, i, per, 0

    def step(self, ins):
        self.n += 1
        ins.then_inc(self.sem, 1)

    def wait(self):
        self.eng.wait_ge(self.sem, FROM + self.i * self.per + self.n)

    def end(self):
        assert self.n == self.per, (self.n, self.per)


def rwkv(K, A, scr, hid, o):
    nc = K.nc
    NEG = -float(np.exp(np.float32(-0.5)))
    NC = TOK // CH
    LV = len(LEVELS)
    T3 = [0, 1, 2]
    with ExitStack() as ctx:
        sb = lambda n, s: K.sb("rk_" + n, s, ctx)
        kT, vT, rT = sb("k", [P, TOK]), sb("v", [P, TOK]), sb("r", [P, TOK])
        w2z = [sb(f"w2z{d}", [P, P]) for d in range(2)]
        a2z = [sb(f"a2z{d}", [P, P]) for d in range(2)]
        g2c = sb("g2c", [P, P])
        kk, sq, ms = sb("kk", [P, TOK]), sb("sq", [P, TOK]), sb("ms", [P, TOK])
        lw, L, aa, kd = sb("lw", [P, TOK]), sb("L", [P, TOK]), sb("a", [P, TOK]), sb("kd", [P, TOK])
        Lx = ms
        eL, eLx, emL = sb("eL", [P, TOK]), sb("eLx", [P, TOK]), sb("emL", [P, TOK])
        b = sq
        Bh, kh = lw, aa
        kds = sb("kds", [P, LAT])
        xm = K.x[:].rearrange("p k t -> p (k t)")
        zr = xm[:, 0:4 * TOK].rearrange("p (m t) -> p m t", m=4)
        Zz = xm[:, 4 * TOK:6 * TOK].rearrange("p (t h c) -> p t h c", t=NT, h=2)
        S = xm[:, 6 * TOK:6 * TOK + NC * P].rearrange("p (n c) -> p n c", c=P)
        spare = K.h[:].rearrange("p k t -> p (k t)")[:, KD * LAT:KD * TOK]
        U = spare[:, 0:TOK].rearrange("p (t c) -> p t c", c=P)
        TKT = spare[:, TOK:2 * TOK]
        Y = spare[:, 2 * TOK:2 * TOK + LAT].rearrange("p (t c) -> p t c", c=P)
        Rt, Bt, kt = sb("Rt", [P, LAT]), sb("Bt", [P, TOK]), sb("kt", [P, TOK])
        Kz = sb("Kz", [P, NT, 2, P])
        BKz = sb("BKz", [P, NT, 2, 2, P])
        Vz = sb("Vz", [P, NT, 2, P])
        xy = sb("xy", [P, NT, 2, 4, P])
        A4 = [sb(f"A4_{q}", [P, 4, P]) for q in T3]
        W4 = [sb(f"W4_{q}", [P, 4, P]) for q in T3]
        TT4 = [sb(f"T4_{q}", [P, 4, P]) for q in T3]
        Y4 = [sb(f"Y4_{q}", [P, 4, P]) for q in T3]
        AVz = Kz
        tmpS = sb("tmpS", [P, P])
        stat = sb("stat", [P, 4, 8])
        yT, bon, gg = eL[:, 0:LAT], eLx[:, 0:LAT], emL[:, 0:LAT]
        prod3 = lw[:, 0:LAT]
        bank = [K.ps(f"rk_b{n}", [P, 512], ctx) for n in range(8)]
        sem = lambda n: K.sem("rk_" + n)
        loaded, zeroed, hp_done = sem("loaded"), sem("zeroed"), sem("heads_done")
        d_vec, d_act, d_pool = sem("vec_steps"), sem("act_steps"), sem("pool_steps")
        raw_sq, sq_sum, sq_max, sq_root, v_turned = (sem(n) for n in ("kk_squared", "kk_summed", "kk_max", "kk_root", "v_turned"))
        uw, sig, cum, exps, ready_b, feat, hats, turned_tok, tok_a, tok_v = (sem(n) for n in (
            "lora_out", "sigmoids", "cumsum", "exps", "b_and_kd", "features", "hats", "tokens_turned", "tok_copied_a", "tok_copied_v"))
        aq, masked, n_turned, a_copied, w_first, w_turned, t_copied, y_prod, y_masked, w_prod, w_added = (sem(n) for n in (
            "causal_products", "masked", "n_turned", "a_copied", "w_first", "w_turned", "t_copied", "y_products", "y_masked",
            "w_products", "w_added"))
        av, av_copied, utk, u_copied, tk_copied = (sem(n) for n in ("av", "av_copied", "u_and_tk", "u_copied", "tk_copied"))
        z_prod, z_added, s_prod, s_next, y_out, y_added = (sem(n) for n in ("z_products", "z_added", "s_products", "s_next", "y_out", "y_added"))
        centred, gn_var, gn_root, y_normed, y_back, bonus_in, bonus, gate = (sem(n) for n in (
            "centred", "gn_variance", "gn_root", "y_normed", "y_turned", "bonus_in", "bonus", "gate"))
        s_zero = sem("s_zero")
        diag = lambda ap: ap.rearrange("p h (a j) -> p (h a) j", j=NH)[:, 0:4:3, :]
        spans = ((LATR, 0), (CTXR, 1))
        order = [list(range(NC)), list(range(CTX // CH))[::-1] + list(range(CTX // CH, NC))[::-1]]
        n_it = KD

        def col(name, i, at=0):
            return K.vec[:, bass.ds(i + (VEC[name] + at), 1)]

        with nc.Block() as block:
            @block.sync
            def _(sp):
                sp.wait_ge(zeroed, FROM + 4)
                with sp.Fori(0, n_it) as i:
                    sp.wait_ge(hp_done, FROM + i)
                    one = lambda t: t[bass.ds(i, 1)].rearrange("o p t -> (o p) t")
                    sp.dma_start(kT[:], one(scr["k"])).then_inc(loaded, 16)
                    sp.dma_start(vT[:], one(scr["v"])).then_inc(loaded, 16)
                    sp.dma_start(rT[:], one(scr["r"])).then_inc(loaded, 16)
                    for d in range(2):
                        sp.dma_start(w2z[d][64 * d:64 * d + 64, :], one(A["w2"])[64 * d:64 * d + 64, :]).then_inc(loaded, 16)
                        sp.dma_start(a2z[d][64 * d:64 * d + 64, :], one(A["a2"])[64 * d:64 * d + 64, :]).then_inc(loaded, 16)
                    sp.dma_start(g2c[:], one(A["g2"])).then_inc(loaded, 16)

            @block.gpsimd
            def _(pool):
                for d in range(2):
                    nc.gpsimd.memset(w2z[d][:], 0.0).then_inc(zeroed, 1)
                    nc.gpsimd.memset(a2z[d][:], 0.0).then_inc(zeroed, 1)
                nc.gpsimd.memset(Vz[:], 0.0).then_inc(zeroed, 1)
                nc.gpsimd.memset(Zz, 0.0).then_inc(zeroed, 1)
                nc.gpsimd.memset(S, 0.0).then_inc(zeroed, 1)
                with pool.Fori(0, n_it) as i:
                    for d in range(2):
                        u = 2 * i + d
                        pool.wait_ge(exps, FROM + 3 * u + 3)
                        pool.wait_ge(ready_b, FROM + 2 * u + 2)
                        nc.gpsimd.tensor_tensor(Bt[:], b[:], emL[:], ALU.mult).then_inc(hats, 1)
                        nc.gpsimd.tensor_tensor(kt[:], kd[:], emL[:], ALU.mult).then_inc(hats, 1)
                        pool.wait_ge(hats, FROM + 4 * u + 2)
                        end = CH - 1 if d == 0 else 0
                        pc = eL[:].rearrange("p (c j) -> p c j", j=CH)[:, :, end:end + 1].broadcast_to([P, NC, CH])
                        cj = lambda t: t[:].rearrange("p (c j) -> p c j", j=CH)
                        nc.gpsimd.tensor_tensor(cj(Bh), cj(Bt), pc, ALU.mult).then_inc(hats, 1)
                        nc.gpsimd.tensor_tensor(cj(kh), cj(kt), pc, ALU.mult).then_inc(hats, 1)

            @block.scalar
            def _(act):
                with act.Fori(0, n_it) as i:
                    act.wait_ge(raw_sq, FROM + 2 * i + 1)
                    nc.scalar.activation(sq[:], kk[:], ACT.Square).then_inc(raw_sq, 1)
                    act.wait_ge(sq_max, FROM + 2 * i + 2)
                    nc.scalar.activation(ms[:], ms[:], ACT.Sqrt).then_inc(sq_root, 1)
                    for d in range(2):
                        u = 2 * i + d
                        act.wait_ge(uw, FROM + 2 * u + 1)
                        for r, n in spans:
                            nc.scalar.activation(lw[:, r], bank[n][:, 0:r.stop - r.start], ACT.Sigmoid, bias=col("w0", i, KD * d)).then_inc(sig, 1)
                        act.wait_ge(uw, FROM + 2 * u + 2)
                        for r, n in spans:
                            nc.scalar.activation(aa[:, r], bank[2 + n][:, 0:r.stop - r.start], ACT.Sigmoid, bias=col("a0", i, KD * d)).then_inc(sig, 1)
                        act.wait_ge(cum, FROM + 3 * u + 3)
                        nc.scalar.activation(eL[:], L[:], ACT.Exp).then_inc(exps, 1)
                        nc.scalar.activation(eLx[:], Lx[:], ACT.Exp).then_inc(exps, 1)
                        nc.scalar.activation(emL[:], L[:], ACT.Exp, scale=-1.0).then_inc(exps, 1)
                        for t in range(NT):
                            act.wait_ge(turned_tok, FROM + NT * u + t + 1)
                            nc.scalar.activation(Kz[:, t, :, :], bank[2 * (t % 2)][:, 0:2 * P].rearrange("p (h c) -> p h c", h=2), ACT.Copy).then_inc(tok_a, 1)
                        for q in T3:
                            act.wait_ge(n_turned, FROM + 3 * u + q + 1)
                            nc.scalar.activation(A4[q][:], bank[q][:].rearrange("p (m c) -> p m c", m=4), ACT.Copy).then_inc(a_copied, 1)
                        for lv in range(LV):
                            for q in T3:
                                act.wait_ge(w_turned, FROM + 3 * (LV * u + lv) + q + 1)
                                nc.scalar.activation(TT4[q][:], bank[q][:].rearrange("p (m c) -> p m c", m=4), ACT.Copy).then_inc(t_copied, 1)
                        act.wait_ge(utk, FROM + 2 * u + 1)
                        for n in range(2):
                            w = (4, 2)[n] * P
                            nc.scalar.activation(TKT[:, 4 * P * n:4 * P * n + w], bank[2 + n][:, 0:w], ACT.Copy).then_inc(tk_copied, 1)
                        act.wait_ge(utk, FROM + 2 * u + 2)
                        for n in range(2):
                            w = (4, 2)[n]
                            nc.scalar.activation(U[:, 4 * n:4 * n + w, :], bank[4 + n][:, 0:w * P].rearrange("p (t c) -> p t c", c=P), ACT.Copy).then_inc(u_copied, 1)
                    act.wait_ge(gn_var, FROM + i + 1)
                    nc.scalar.activation(stat[:, 3, :], stat[:, 2, :], ACT.Sqrt).then_inc(gn_root, 1)

            @block.tensor
            def _(pe):
                tile = lambda t: slice(t * P, (t + 1) * P)
                at = lambda q, m: (2 * q + m // 2, m % 2)

                def lora_out(u, d):
                    pe.wait_ge(zeroed, FROM + 7)
                    for n, (z, hname) in enumerate(((w2z, "w1"), (a2z, "a1"))):
                        for r, bn in spans:
                            last = nc.tensor.matmul(bank[2 * n + bn][:, 0:r.stop - r.start], z[d][:], hid[hname][:, r], start=True, stop=True)
                        last.then_inc(uw, 1)

                def direction(i, d):
                    u = 2 * i + d
                    if d == 1:
                        pe.wait_ge(y_added, FROM + u)
                    lora_out(u, d)
                    pe.wait_ge(feat, FROM + 5 * u + 5)
                    pe.wait_ge(hats, FROM + 4 * u + 4)
                    pe.wait_ge(sig, FROM + 4 * u + 4)
                    for t in range(NT):
                        if t >= 2:
                            pe.wait_ge(tok_a, FROM + NT * u + t - 1)
                            pe.wait_ge(tok_v, FROM + NT * u + t - 1)
                        j = 2 * (t % 2)
                        for hh in range(2):
                            nc.tensor.transpose(bank[j][:, hh * P:(hh + 1) * P], zr[:, hh, tile(t)], K.c("ident"))
                        nc.tensor.transpose(bank[j + 1][:, 0:P], Bh[:, tile(t)], K.c("ident"))
                        nc.tensor.transpose(bank[j + 1][:, P:2 * P], kh[:, tile(t)], K.c("ident")).then_inc(turned_tok, 1)
                    for t in range(NT):
                        w = 4 if t >= CT else 2
                        j = 4 + 2 * (t % 2)
                        if t >= 2:
                            pe.wait_ge(masked, FROM + 2 * (NT * u + t - 1))
                        for n, m in enumerate((Bt, kt)):
                            last = nc.tensor.matmul(bank[j + n][:, 0:w * P], m[:, tile(t)], zr[:, 0:w, tile(t)], start=True, stop=True)
                            last.then_inc(aq, 1)
                    pe.wait_ge(tok_a, FROM + NT * (u + 1))
                    pe.wait_ge(tok_v, FROM + NT * (u + 1))
                    for q in T3:
                        pe.wait_ge(masked, FROM + 2 * (NT * u + 2 * q + 2))
                        for m in range(4):
                            t, hh = at(q, m)
                            last = nc.tensor.transpose(bank[q][:, m * P:(m + 1) * P], xy[:, t, 0, hh, :], K.c("ident"))
                        last.then_inc(n_turned, 1)
                    pe.wait_ge(masked, FROM + 2 * NT * (u + 1))
                    for lv in range(LV):
                        for q in T3:
                            if lv == 0:
                                pe.wait_ge(w_first, FROM + 2 * (3 * u + q + 1))
                                pe.wait_ge(a_copied, FROM + 3 * u + q + 1)
                            else:
                                pe.wait_ge(w_added, FROM + 3 * ((LV * u) + lv - 1) + q + 1)
                            for m in range(4):
                                last = nc.tensor.transpose(bank[q][:, m * P:(m + 1) * P], W4[q][:, m, :], K.c("ident"))
                            last.then_inc(w_turned, 1)
                        for q in T3:
                            pe.wait_ge(t_copied, FROM + 3 * (LV * u + lv) + q + 1)
                            for m in range(4):
                                last = nc.tensor.matmul(bank[q][:, m * P:(m + 1) * P], A4[q][:, m, :], W4[q][:, m, :], start=True, stop=True)
                            last.then_inc(y_prod, 1)
                        for q in T3:
                            pe.wait_ge(y_masked, FROM + 3 * (LV * u + lv) + q + 1)
                            for m in range(4):
                                last = nc.tensor.matmul(bank[3 + q][:, m * P:(m + 1) * P], TT4[q][:, m, :], Y4[q][:, m, :], start=True, stop=True)
                            last.then_inc(w_prod, 1)
                    pe.wait_ge(w_added, FROM + 3 * LV * (u + 1))
                    for t in range(NT):
                        for hh in range(2):
                            last = nc.tensor.matmul(bank[2 + t // 4][:, (t % 4) * P:(t % 4 + 1) * P], Kz[:, t, hh, :],
                                                    W4[t // 2][:, 2 * (t % 2) + hh, :], start=hh == 0, stop=hh == 1)
                    last.then_inc(utk, 1)
                    for t in range(NT):
                        for hh in range(2):
                            last = nc.tensor.matmul(bank[t // 4][:, (t % 4) * P:(t % 4 + 1) * P], xy[:, t, 1, hh, :], Vz[:, t, hh, :],
                                                    start=hh == 0, stop=hh == 1)
                    last.then_inc(av, 1)
                    pe.wait_ge(av_copied, FROM + 2 * u + 2)
                    for t in range(NT):
                        for hh in range(2):
                            last = nc.tensor.matmul(bank[4 + t // 4][:, (t % 4) * P:(t % 4 + 1) * P], W4[t // 2][:, 2 * (t % 2) + hh, :],
                                                    AVz[:, t, hh, :], start=hh == 0, stop=hh == 1)
                    last.then_inc(utk, 1)
                    pe.wait_ge(tk_copied, FROM + 2 * u + 2)
                    pe.wait_ge(u_copied, FROM + 2 * u + 2)
                    pe.wait_ge(s_zero, FROM + u + 1)
                    for n, c in enumerate(order[d][:-1] + order[d][-1:]):
                        t, half = c // 2, c % 2
                        rows = slice(CH * half, CH * half + CH)
                        last_chunk = n == NC - 1
                        if n:
                            pe.wait_ge(s_next, FROM + (NC - 1) * u + n)
                        nc.tensor.matmul(bank[4 + n % 2][rows, 0:P], TKT[:, c * CH:(c + 1) * CH], S[:, n, :], start=True, stop=True).then_inc(z_prod, 1)
                        if last_chunk:
                            break
                        nc.tensor.matmul(bank[6 + n % 2][:, 0:P], BKz[:, t, half, 1, :], diag(Vz[:, t]), start=True, stop=False)
                        pe.wait_ge(z_added, FROM + NC * u + n + 1)
                        nc.tensor.matmul(bank[6 + n % 2][:, 0:P], BKz[:, t, half, 0, :], diag(Zz[:, t]), start=False, stop=True).then_inc(s_prod, 1)
                    pe.wait_ge(z_added, FROM + NC * (u + 1))
                    for t in range(CT, NT):
                        oc = slice((t - CT) * P, (t - CT + 1) * P)
                        for half in range(2):
                            c = 2 * t + half
                            n = order[d].index(c)
                            rows = slice(CH * half, CH * half + CH)
                            nc.tensor.matmul(bank[0][rows, oc], Rt[:, c * CH - CTX:(c + 1) * CH - CTX], S[:, n, :], start=True, stop=False,
                                             skip_group_check=True)
                        for hh in range(2):
                            nc.tensor.matmul(bank[0][:, oc], xy[:, t, 0, 2 + hh, :], Zz[:, t, hh, :], start=False, stop=False, skip_group_check=True)
                            last = nc.tensor.matmul(bank[0][:, oc], xy[:, t, 1, 2 + hh, :], Vz[:, t, hh, :], start=False, stop=hh == 1, skip_group_check=True)
                    last.then_inc(y_out, 1)

                with pe.Fori(0, n_it) as i:
                    pe.wait_ge(loaded, 128 * i + 128)
                    pe.wait_ge(raw_sq, FROM + 2 * i + 2)
                    pe.wait_ge(hp_done, FROM + i)
                    for r, bn in spans:
                        last = nc.tensor.matmul(bank[bn][:, 0:r.stop - r.start], K.c("heads"), sq[:, r], start=True, stop=True)
                    last.then_inc(sq_sum, 1)
                    for t in range(NT):
                        last = nc.tensor.transpose(bank[4 + t // 4][:, (t % 4) * P:(t % 4 + 1) * P], vT[:, tile(t)], K.c("ident"))
                    last.then_inc(v_turned, 1)
                    pe.wait_ge(sq_max, FROM + 2 * i + 2)
                    direction(i, 0)
                    direction(i, 1)
                    nc.tensor.matmul(bank[1][:], g2c[:], hid["g1"][:, LATR], start=True, stop=True).then_inc(gate, 1)
                    pe.wait_ge(bonus_in, FROM + i + 1)
                    nc.tensor.matmul(bank[2][:], K.c("heads"), prod3, start=True, stop=True).then_inc(bonus, 1)
                    pe.wait_ge(y_normed, FROM + i + 1)
                    for t in range(4):
                        last = nc.tensor.transpose(bank[3][:, t * P:(t + 1) * P], Y[:, t, :], K.c("ident"))
                    last.then_inc(y_back, 1)

            @block.vector
            def _(dve):
                PER = RWKV_VEC_STEPS
                with dve.Fori(0, n_it) as i:
                    ch = Chain(dve, d_vec, i, PER)

                    def step(ins):
                        ch.step(ins)
                        ch.wait()

                    dve.wait_ge(loaded, 128 * i + 128)
                    dve.wait_ge(hp_done, FROM + i)
                    nc.vector.tensor_scalar(kk[:], kT[:], col("k_k", i), None, ALU.mult).then_inc(raw_sq, 1)
                    dve.wait_ge(sq_sum, FROM + i + 1)
                    for r, bn in spans:
                        nc.vector.tensor_scalar(ms[:, r], bank[bn][:, 0:r.stop - r.start], 1e-24, None, ALU.max).then_inc(sq_max, 1)
                    dve.wait_ge(v_turned, FROM + i + 1)
                    dve.wait_ge(zeroed, FROM + 7)
                    for n in range(2):
                        w = (4, 2)[n]
                        for hh in range(2):
                            ch.step(nc.vector.tensor_copy(Vz[:, 4 * n:4 * n + w, hh, NH * hh:NH * hh + NH],
                                                          bank[4 + n][:, 0:w * P].rearrange("p (t c) -> p t c", c=P)[:, :, NH * hh:NH * hh + NH]))
                    dve.wait_ge(sq_root, FROM + i + 1)
                    step(nc.vector.reciprocal(eL[:], ms[:]))
                    step(nc.vector.tensor_tensor(kk[:], kk[:], eL[:], ALU.mult))
                    for d in range(2):
                        u = 2 * i + d
                        dve.wait_ge(sig, FROM + 4 * u + 2)
                        step(nc.vector.tensor_scalar(lw[:], lw[:], NEG, None, ALU.mult))
                        if d == 0:
                            ins = nc.vector.tensor_tensor_scan(L[:], K.c("start", TOK), lw[:], 0.0, ALU.mult, ALU.add)
                        else:
                            ins = nc.vector.tensor_tensor_scan(L[:, ::-1], K.c("end", TOK)[:, ::-1], lw[:, ::-1], 0.0, ALU.mult, ALU.add)
                        ins.then_inc(cum, 1)
                        dve.wait_ge(cum, FROM + 3 * u + 1)
                        nc.vector.tensor_tensor(Lx[:], L[:], lw[:], ALU.subtract).then_inc(cum, 1)
                        dve.wait_ge(sig, FROM + 4 * u + 4)
                        nc.vector.scalar_tensor_tensor(out=b[:], in0=kk[:], scalar=-1.0, in1=aa[:], op0=ALU.mult, op1=ALU.mult).then_inc(ready_b, 1)
                        step(nc.vector.tensor_scalar(kd[:], aa[:], -1.0, col("k_a", i), ALU.add, ALU.mult))
                        nc.vector.scalar_tensor_tensor(out=kd[:], in0=kd[:], scalar=1.0, in1=kT[:], op0=ALU.add, op1=ALU.mult).then_inc(ready_b, 1)
                        dve.wait_ge(ready_b, FROM + 2 * u + 2)
                        if d == 0:
                            nc.vector.tensor_copy(kds[:], kd[:, LATR]).then_inc(cum, 1)
                        else:
                            nc.vector.tensor_tensor(kds[:], kds[:], kd[:, LATR], ALU.add).then_inc(cum, 1)
                        dve.wait_ge(cum, FROM + 3 * u + 3)
                        dve.wait_ge(exps, FROM + 3 * u + 2)
                        for hh in range(2):
                            nc.vector.scalar_tensor_tensor(out=zr[:, hh, :], in0=kk[:], scalar=K.c("half", 1, hh), in1=eLx[:],
                                                           op0=ALU.mult, op1=ALU.mult).then_inc(feat, 1)
                            nc.vector.scalar_tensor_tensor(out=zr[:, 2 + hh, LATR], in0=rT[:, LATR], scalar=K.c("half", 1, hh), in1=eL[:, LATR],
                                                           op0=ALU.mult, op1=ALU.mult).then_inc(feat, 1)
                        nc.vector.tensor_tensor(Rt[:], rT[:, LATR], eL[:, LATR], ALU.mult).then_inc(feat, 1)
                        ch.step(nc.vector.memset(S[:, 0, :], 0.0))
                        ch.wait()
                        nc.vector.memset(tmpS[:], 0.0).then_inc(s_zero, 1)
                        dve.wait_ge(s_zero, FROM + u + 1)
                        for t in range(NT):
                            dve.wait_ge(turned_tok, FROM + NT * u + t + 1)
                            for half in range(2):
                                last = nc.vector.tensor_scalar(BKz[:, t, half, :, :], bank[2 * (t % 2) + 1][:, 0:2 * P].rearrange("p (m c) -> p m c", m=2),
                                                               K.c("half", 1, half), None, ALU.mult)
                            last.then_inc(tok_v, 1)
                        for t in range(NT):
                            w = 4 if t >= CT else 2
                            for n in range(2):
                                dve.wait_ge(aq, FROM + 2 * (NT * u + t) + n + 1)
                                nc.vector.tensor_tensor(xy[:, t, n, 0:w, :], bank[4 + 2 * (t % 2) + n][:, 0:w * P].rearrange("p (m c) -> p m c", m=w),
                                                        K.c("causal", w * P, 4 * P * d).rearrange("p (m c) -> p m c", m=w), ALU.mult).then_inc(masked, 1)
                        dve.wait_ge(masked, FROM + 2 * NT * (u + 1))
                        for q in T3:
                            n4 = xy[:, 2 * q:2 * q + 2, 0, 0:2, :]
                            for x in range(2):
                                last = nc.vector.tensor_tensor(Y4[q][:, 2 * x:2 * x + 2, :], xy[:, 2 * q + x, 0, 0:2, :],
                                                               K.c("first", P, P * d).unsqueeze(1).broadcast_to([P, 2, P]), ALU.mult)
                            last.then_inc(w_first, 1)
                            dve.wait_ge(w_first, FROM + 2 * (3 * u + q) + 1)
                            nc.vector.tensor_tensor(W4[q][:], Y4[q][:], K.c("ident").unsqueeze(1).broadcast_to([P, 4, P]), ALU.add).then_inc(w_first, 1)
                        for lv in range(LV):
                            for q in T3:
                                dve.wait_ge(y_prod, FROM + 3 * (LV * u + lv) + q + 1)
                                nc.vector.tensor_tensor(Y4[q][:], bank[q][:].rearrange("p (m c) -> p m c", m=4),
                                                        K.c("level", P, (d * LV + lv) * P).unsqueeze(1).broadcast_to([P, 4, P]), ALU.mult).then_inc(y_masked, 1)
                            for q in T3:
                                dve.wait_ge(w_prod, FROM + 3 * (LV * u + lv) + q + 1)
                                nc.vector.tensor_tensor(W4[q][:], W4[q][:], bank[3 + q][:].rearrange("p (m c) -> p m c", m=4), ALU.add).then_inc(w_added, 1)
                        dve.wait_ge(w_added, FROM + 3 * LV * (u + 1))
                        dve.wait_ge(utk, FROM + 2 * u + 1)
                        step(nc.vector.memset(AVz[:], 0.0))
                        dve.wait_ge(av, FROM + u + 1)
                        for n in range(2):
                            w = (4, 2)[n]
                            for hh in range(2):
                                last = nc.vector.tensor_copy(AVz[:, 4 * n:4 * n + w, hh, NH * hh:NH * hh + NH],
                                                             bank[n][:, 0:w * P].rearrange("p (t c) -> p t c", c=P)[:, :, NH * hh:NH * hh + NH])
                            last.then_inc(av_copied, 1)
                        end = CH - 1 if d == 0 else 0
                        dve.wait_ge(u_copied, FROM + 2 * u + 2)
                        for n, c in enumerate(order[d]):
                            t, half = c // 2, c % 2
                            rows = slice(CH * half, CH * half + CH)
                            dve.wait_ge(z_prod, FROM + NC * u + n + 1)
                            nc.vector.tensor_tensor(diag(Zz[rows, t]), bank[4 + n % 2][rows, 0:P].rearrange("p (h j) -> p h j", h=2),
                                                    U[rows, t, :].rearrange("p (h j) -> p h j", h=2), ALU.add).then_inc(z_added, 1)
                            if n == NC - 1:
                                break
                            dve.wait_ge(s_prod, FROM + (NC - 1) * u + n + 1)
                            if n:
                                dve.wait_ge(s_next, FROM + (NC - 1) * u + n)
                            step(nc.vector.tensor_tensor(tmpS[:], bank[6 + n % 2][:, 0:P], K.c("heads"), ALU.mult))
                            nc.vector.scalar_tensor_tensor(out=S[:, n + 1, :], in0=S[:, n, :], scalar=eL[:, c * CH + end:c * CH + end + 1],
                                                           in1=tmpS[:], op0=ALU.mult, op1=ALU.add).then_inc(s_next, 1)
                            dve.wait_ge(s_next, FROM + (NC - 1) * u + n + 1)
                        dve.wait_ge(y_out, FROM + u + 1)
                        pb = bank[0][:].rearrange("p (t c) -> p t c", c=P)
                        if d == 0:
                            nc.vector.tensor_copy(Y, pb).then_inc(y_added, 1)
                        else:
                            nc.vector.tensor_tensor(Y, Y, pb, ALU.add).then_inc(y_added, 1)
                        dve.wait_ge(y_added, FROM + u + 1)
                    step(nc.vector.tensor_scalar(prod3, rT[:, LATR], col("r_k", i), None, ALU.mult))
                    nc.vector.tensor_tensor(prod3, prod3, kds[:], ALU.mult).then_inc(bonus_in, 1)
                    y8 = Y.rearrange("p t (h j) -> p (t h) j", h=2)
                    bc = lambda n: stat[:, n, :].unsqueeze(2).broadcast_to([P, 8, NH])
                    step(nc.vector.tensor_reduce(stat[:, 0, :], y8, AX.X, ALU.add))
                    step(nc.vector.tensor_scalar(stat[:, 0, :], stat[:, 0, :], 1.0 / NH, None, ALU.mult))
                    step(nc.vector.tensor_tensor(y8, y8, bc(0), ALU.subtract))
                    sqv = Y4[0][:].rearrange("p m (h j) -> p (m h) j", h=2)
                    step(nc.vector.tensor_tensor(sqv, y8, y8, ALU.mult))
                    step(nc.vector.tensor_reduce(stat[:, 1, :], sqv, AX.X, ALU.add))
                    nc.vector.tensor_scalar(stat[:, 2, :], stat[:, 1, :], 1.0 / NH, GN_EPS, ALU.mult, ALU.add).then_inc(gn_var, 1)
                    dve.wait_ge(gn_root, FROM + i + 1)
                    step(nc.vector.reciprocal(stat[:, 1, :], stat[:, 3, :]))
                    nc.vector.tensor_tensor(y8, y8, bc(1), ALU.mult).then_inc(y_normed, 1)
                    dve.wait_ge(bonus, FROM + i + 1)
                    step(nc.vector.tensor_tensor(bon, bank[2][:], vT[:, LATR], ALU.mult))
                    dve.wait_ge(y_back, FROM + i + 1)
                    step(nc.vector.tensor_scalar(yT, bank[3][:], col("ln_w", i), col("ln_b", i), ALU.mult, ALU.add))
                    step(nc.vector.tensor_tensor(bon, bon, yT, ALU.add))
                    dve.wait_ge(gate, FROM + i + 1)
                    nc.vector.tensor_tensor(o[:, bass.ds(i, 1), :].rearrange("p o t -> p (o t)"), bon, bank[1][:], ALU.mult).then_inc(hp_done, 1)
                    ch.end()


def rwkv_layer(K, A, scr, layer):
    nc, x = K.nc, K.x
    norm(K, "n1", layer, 0)
    with ExitStack() as ctx:
        hid = {n: K.sb("hid_" + n, [P, TOK], ctx) for n in ("w1", "a1", "g1")}
        mix_and_project(K, A, scr, hid)
        o = K.h[:].rearrange("p k t -> p (k t)")[:, 0:KD * LAT].rearrange("p (k t) -> p k t", k=KD)
        rwkv(K, A, scr, hid, o)
    project_out(K, "out1", A["rw_o"], o, KD, layer, ((0, LATR),), spilled=scr["x"])


RWKV_VEC_STEPS = 46


def build(nc, A, out):
    with ExitStack() as ctx:
        K = Core(nc, ctx)
        K.begin_stage("mixer0")
        mod_dram = nc.dram_tensor("mod_rows_scratch", (2, DEPTH * NCOL, 512), F32, kind="Internal").ap()
        scr = {n: nc.dram_tensor(f"rw_{n}_scratch", (KD, P, TOK), F32, kind="Internal").ap() for n in ("k", "v", "r")}
        scr["x"] = nc.dram_tensor("x_scratch", (P, KD, TOK), F32, kind="Internal").ap()
        with ExitStack() as first:
            K.hold("attn", first)
            modulation(K, A, mod_dram)
            norm(K, "n0", 0, 0)
            qk = K.sb("qk", [P, NQ + NKV, TOK], first)
            v = K.sb("v", [P, NT, NKV * HD], first)
            o = K.sb("o", [P, NQ + KD, TOK], first)
            project_qk(K, A, qk)
            project_v_conv(K, A, v, o)
            attend(K, qk, v, o)
            project_out(K, "out0", A["w_out"], o, NQ + KD, 0, RANGES)
        del K.con["attn"]
        K.begin_stage("moe0")
        mixture(K, A, 0)
        K.begin_stage("rwkv1")
        with ExitStack() as second:
            K.hold("rwkv", second)
            load_constants(K, A, "rwkv")
            rwkv_layer(K, A, scr, 1)
        K.begin_stage("moe1")
        mixture(K, A, 1)
        norm(K, "final", None, None, final=out)
    return K.named


def load_constants(K, A, group):
    nc = K.nc
    loaded = K.sem(f"con_{group}_loaded")
    with nc.Block() as block:
        @block.sync
        def _(sp):
            sp.dma_start(K.con[group][:], A["con_" + group]).then_inc(loaded, 16)
            sp.wait_ge(loaded, 16)


def lay_out(a):
    f = lambda n: np.asarray(a[n])
    cols = lambda *names: [f(n).reshape(-1, P) for n in names]
    w = {}
    rows = cols("c", "c_ctx", "ada_b", "norm_g", "final_g", "conv_w", "rw_mu", "rw_w0", "rw_a0", "rw_k_k", "rw_k_a",
                "rw_r_k", "rw_ln_w", "rw_ln_b", "q_norm_g", "k_norm_g")
    w["vecs"] = np.ascontiguousarray(np.concatenate(rows, 0).T)
    x = np.concatenate([f("ctx")[0], f("x")[0]], 0)
    w["xT"] = np.ascontiguousarray(x.T.reshape(KD, P, TOK).transpose(1, 0, 2))

    def by_columns(m, n=P):
        k, c = m.shape
        return np.ascontiguousarray(m.reshape(k // P, P, c // n, n).transpose(2, 1, 0, 3))

    w["ada"] = np.concatenate([by_columns(f("ada_w")[l], 512) for l in range(DEPTH)], 0)
    w["w_in"] = by_columns(f("mix_w_in")[0])
    w["w_out"] = by_columns(f("mix_w_out")[0])
    for n in ("r", "k", "v", "o"):
        w["rw_" + n] = by_columns(f("rw_w_" + n)[0])
    for n in ("w1", "a1"):
        m = f("rw_" + n)[0]
        w[n] = by_columns(np.concatenate([m[0], m[1]], 1))[0]
    w["g1"] = by_columns(f("rw_g1")[0])[0]
    for n in ("w2", "a2"):
        w[n] = np.ascontiguousarray(f("rw_" + n)[0].reshape(2 * 64, KD, P).transpose(1, 0, 2))
    w["g2"] = np.ascontiguousarray(f("rw_g2")[0].reshape(P, KD, P).transpose(1, 0, 2))
    w["router"] = np.ascontiguousarray(f("moe_router").reshape(DEPTH, KD, P, E).transpose(0, 2, 1, 3))
    for n in ("gate", "up", "down"):
        w["moe_" + n] = np.ascontiguousarray(f("moe_w_" + n))
    return w


def kernel(**inputs):
    import concourse.bacc as _bacc
    from concourse.bass_utils import run_bass_kernel_spmd as _run

    arrays = {**lay_out(inputs), **constants()}
    nc = _bacc.Bacc("TRN2", target_bir_lowering=False, num_devices=1)
    A = {n: nc.dram_tensor("in_" + n, a.shape, mybir.dt.from_np(a.dtype), kind="ExternalInput").ap() for n, a in arrays.items()}
    out = nc.dram_tensor("outT", (P, KD, LAT), F32, kind="ExternalOutput").ap()
    build(nc, A, out)
    r = _run(nc, [{"in_" + n: a for n, a in arrays.items()}], core_ids=[0]).results[0]["outT"]
    return np.ascontiguousarray(r.transpose(2, 1, 0).reshape(1, LAT, D))
```

```python
from contextlib import ExitStack

import numpy as np

import concourse.bass as bass
from concourse import mybir

ALU = mybir.AluOpType
ACT = mybir.ActivationFunctionType
AX = mybir.AxisListType
F32 = mybir.dt.float32
F32R, U32 = mybir.dt.float32r, mybir.dt.uint32

P = 128
D = 1024
KD = D // P
CTX, LAT = 256, 512
TOK = CTX + LAT
NT = TOK // P
CT = CTX // P
DEPTH = 2
HD = 128
NQ, NKV = 8, 2
QPK = NQ // NKV
GRID_W = 64
E = 16
CAP_L, CAP_C = 2 * LAT // E, 2 * CTX // E
EPS = 1e-6
GN_EPS = 64e-5
NH = 64
CH = 64
NCOL = 6 * D // 512

LATR, CTXR = slice(CTX, TOK), slice(0, CTX)
RANGES = ((1, CTXR), (0, LATR))

FROM = 1

LEADING = 0xFFFFF000

SEMAPHORES = {
    "mixer0":
        "mod_small_loaded mod_w_ready0 mod_w_ready1 mod_w_ready2 mod_w_ready3 mod_silu_done mod_product_done0 "
        "mod_product_done1 mod_product_done2 mod_product_done3 mod_row_copied0 mod_row_copied1 mod_row_copied2 "
        "mod_row_copied3 mod_row_stored mod_rows_loaded mod_rows_turned mod_columns_done n0_squared n0_summed "
        "n0_mean n0_rooted n0_inverse n0_scaled n0_stored conv_h_lead conv_h_rest conv_h_split conv_weights_lead "
        "conv_weights_rest conv_weights_split v_w_ready v_product v_copied v_pads_zeroed conv_w_ready0 "
        "conv_w_ready1 conv_copied0 conv_copied1 conv_gated0 conv_gated1 conv_mid0 conv_mid1 conv_left0 "
        "conv_left1 conv_right0 conv_right1 conv_written0 conv_written1 conv_product0 conv_product1 conv_product2 "
        "qk_w_ready0 qk_w_ready1 qk_proj_lat0 qk_proj_lat1 qk_proj0 qk_proj1 qk_squared0 qk_squared1 qk_summed0 "
        "qk_summed1 qk_mean0 qk_mean1 qk_rooted0 qk_rooted1 qk_inverse0 qk_inverse1 qk_normed0 qk_normed1 "
        "qk_swapped0 qk_swapped1 qk_cosed0 qk_cosed1 qk_sined0 qk_sined1 qk_written0 qk_written1 qk_ctx_copied0 "
        "qk_ctx_copied1 qk_gains at_scored0 at_scored1 at_maxed0 at_maxed1 at_biased0 at_biased1 at_exped0 "
        "at_exped1 at_summed0 at_summed1 at_scaled0 at_scaled1 at_turned0 at_turned1 at_copied_a0 at_copied_a1 "
        "at_copied_v0 at_copied_v1 at_staged0 at_staged1 at_weighed0 at_weighed1 at_out0 at_out1 out0_w_ready0 "
        "out0_w_ready1 out0_product0 out0_product1 out0_added0 out0_added1 out0_x_back ",
    "moe0":
        "moe0x_w_ready0 moe0x_w_ready1 moe0x_w_ready2 moe0x_w_ready3 moe0x_w_ready4 moe0x_w_ready5 moe0n_squared "
        "moe0n_summed moe0n_mean moe0n_rooted moe0n_inverse moe0n_scaled moe0n_stored moe0r_router_loaded "
        "moe0r_logits moe0r_logits_copied moe0r_logits_turned moe0r_max moe0r_shifted moe0r_exped moe0r_summed "
        "moe0r_inverse moe0r_affinity moe0r_affinity_turned moe0r_work moe0r_top moe0r_replaced moe0r_picked "
        "moe0r_counted moe0r_placed moe0r_slot_turned moe0r_h_turned0 moe0r_h_turned1 moe0r_h_copied0 "
        "moe0r_h_copied1 moe0x_selected moe0x_weighted moe0x_put_turned moe0x_put_copied moe0x_gathered0 "
        "moe0x_gathered1 moe0x_xs_copied0 moe0x_xs_copied1 moe0x_gated0 moe0x_gated1 moe0x_upped0 moe0x_upped1 "
        "moe0x_silued0 moe0x_silued1 moe0x_hidden0 moe0x_hidden1 moe0x_turned0 moe0x_turned1 moe0x_hid_copied0 "
        "moe0x_hid_copied1 moe0x_downed0 moe0x_downed1 moe0x_out_copied0 moe0x_out_copied1 moe0x_spread0 "
        "moe0x_spread1 moe0x_added0 moe0x_added1 moe0x_padded ",
    "rwkv1":
        "con_rwkv_loaded n1_squared n1_summed n1_mean n1_rooted n1_inverse n1_scaled n1_stored mp_w_ready0 "
        "mp_w_ready1 mp_product0 mp_product1 mp_copied0 mp_copied1 mp_stored0 mp_stored1 mp_x_stored "
        "mp_lora_ready mp_edges mp_neighbours mp_mixed mp_lora rk_loaded rk_v_loaded rk_g_loaded rk_kk_made "
        "rk_kk_raw rk_kk_square rk_kk_sum rk_kk_max rk_kk_root rk_kk_rec rk_v_turned rk_vz_made rk_vt_loaded "
        "rk_bonus_kept rk_bonus rk_bonus_v rk_centred rk_gn_sum rk_gn_var rk_gn_root rk_normed rk_y_turned "
        "rk_y_scaled rk_gate rk_out_made rk_gn_steps rk_zeroed rk_kds_half rk_low_rank rk_sigmoids rk_log_decay "
        "rk_cumsum rk_exclusive rk_kd_half rk_kd_made rk_b_made rk_exps rk_zr_made rk_kds_made rk_hats "
        "rk_unit_kept rk_tokens_turned rk_tokens_copied rk_causal_products rk_masked rk_n_turned rk_a_copied "
        "rk_w_first rk_w_turned rk_t_copied rk_aw_product rk_aw_masked rk_w_product rk_w_added rk_av rk_av_copied "
        "rk_u_and_tk rk_u_copied rk_tk_copied rk_z_product rk_z_added rk_s_product rk_s_next rk_y_out rk_y_added "
        "out1_w_ready0 out1_w_ready1 out1_product0 out1_product1 out1_added0 out1_added1 out1_x_back ",
    "moe1":
        "moe1x_w_ready0 moe1x_w_ready1 moe1x_w_ready2 moe1x_w_ready3 moe1x_w_ready4 moe1x_w_ready5 moe1n_squared "
        "moe1n_summed moe1n_mean moe1n_rooted moe1n_inverse moe1n_scaled moe1n_stored moe1r_router_loaded "
        "moe1r_logits moe1r_logits_copied moe1r_logits_turned moe1r_max moe1r_shifted moe1r_exped moe1r_summed "
        "moe1r_inverse moe1r_affinity moe1r_affinity_turned moe1r_work moe1r_top moe1r_replaced moe1r_picked "
        "moe1r_counted moe1r_placed moe1r_slot_turned moe1r_h_turned0 moe1r_h_turned1 moe1r_h_copied0 "
        "moe1r_h_copied1 moe1x_selected moe1x_weighted moe1x_put_turned moe1x_put_copied moe1x_gathered0 "
        "moe1x_gathered1 moe1x_xs_copied0 moe1x_xs_copied1 moe1x_gated0 moe1x_gated1 moe1x_upped0 moe1x_upped1 "
        "moe1x_silued0 moe1x_silued1 moe1x_hidden0 moe1x_hidden1 moe1x_turned0 moe1x_turned1 moe1x_hid_copied0 "
        "moe1x_hid_copied1 moe1x_downed0 moe1x_downed1 moe1x_out_copied0 moe1x_out_copied1 moe1x_spread0 "
        "moe1x_spread1 moe1x_added0 moe1x_added1 moe1x_padded final_squared final_summed final_mean final_rooted "
        "final_inverse final_scaled final_stored ",
}

VEC = {}
_at = 0
for _name, _n in (("c", KD), ("c_ctx", KD), ("ada_b", DEPTH * 6 * KD), ("norm_g", DEPTH * 2 * KD),
                  ("final_g", KD), ("conv_w", 3 * KD), ("mu", 6 * KD), ("w0", 2 * KD), ("a0", 2 * KD),
                  ("k_k", KD), ("k_a", KD), ("r_k", KD), ("ln_w", KD), ("ln_b", KD), ("q_g", 1), ("k_g", 1)):
    VEC[_name] = _at
    _at += _n
NVEC = _at

LEVELS = (2, 4, 8, 16, 32)
GROUPS = {
    "base": (("ident", P), ("ones", P), ("iota", 64)),
    "attn": (("swap", P), ("cos", LAT), ("sin", LAT)),
    "rwkv": (("heads", P), ("causal", 2 * 2 * P), ("first", 2 * P), ("level", 2 * len(LEVELS) * P),
             ("half", 2), ("start", TOK)),
}
CON, NCON = {}, {}
for _group, _names in GROUPS.items():
    _at = 0
    for _name, _n in _names:
        CON[_name] = (_group, _at)
        _at += _n
    NCON[_group] = _at


def constants():
    c = {g: np.zeros((P, n), np.float32) for g, n in NCON.items()}

    def put(name, a, at=0):
        g, o = CON[name]
        c[g][:, o + at:o + at + a.shape[1]] = a

    i = np.arange(P)
    put("ident", np.eye(P))
    put("ones", np.ones((P, P)))
    put("heads", (i[:, None] // NH == i[None] // NH) * 1.0)
    swap = np.zeros((P, P))
    swap[i[:64] + 64, i[:64]] = -1.0
    swap[i[:64], i[:64] + 64] = 1.0
    put("swap", swap)
    t = np.arange(LAT)
    n = HD // 4
    inv = (10000.0 ** (-np.arange(n, dtype=np.float32) / n)).astype(np.float32)
    ang = np.concatenate([(t // GRID_W).astype(np.float32)[:, None] * inv,
                          (t % GRID_W).astype(np.float32)[:, None] * inv], -1).T
    put("cos", np.concatenate([np.cos(ang)] * 2))
    put("sin", np.concatenate([np.sin(ang)] * 2))
    put("iota", np.broadcast_to(np.arange(64.0), (P, 64)))
    s, tt = i[:, None], i[None]
    same = s // CH == tt // CH
    for d in range(2):
        before = (s < tt) if d == 0 else (s > tt)
        for m in range(2):
            put("causal", same & (before | ((s == tt) & (m == 1))), (2 * d + m) * P)
        put("first", same & before & (s // 2 == tt // 2), d * P)
        for j, b in enumerate(LEVELS):
            put("level", (s // (2 * b) == tt // (2 * b)) & before & (s // b != tt // b), (d * len(LEVELS) + j) * P)
    put("half", (i[:, None] // NH == np.arange(2)[None]) * 1.0)
    tok = np.arange(TOK)
    put("start", np.broadcast_to((tok % CH != 0) * 1.0, (P, TOK)))
    return {"con_" + g: a for g, a in c.items()}


class Core:

    def __init__(self, nc, ctx):
        self.nc, self.ctx = nc, ctx
        self.used, self.started, self.named, self.stage = [], {}, {}, None
        self.x = self.sb("x", [P, KD, TOK])
        self.h = self.sb("h", [P, KD, TOK])
        self.con = {"base": self.sb("con_base", [P, NCON["base"]])}
        self.vec = self.sb("vec", [P, NVEC])
        self.mod = self.sb("mod", [P, 2, DEPTH * 6 * KD])
        self.scale = self.sb("scale", [P, 2, DEPTH * 2 * KD])

    def sb(self, name, shape, ctx=None, dt=F32):
        return (ctx or self.ctx).enter_context(self.nc.sbuf_tensor(name, shape, dt))

    def hold(self, group, ctx):
        self.con[group] = self.sb("con_" + group, [P, NCON[group]], ctx)

    def ps(self, name, shape, ctx=None, dt=F32):
        return (ctx or self.ctx).enter_context(self.nc.psum_tensor(name, shape, dt))

    def sem(self, name):
        self.named.setdefault(self.stage, []).append(name)
        if name in self.started:
            return self.started[name]
        s = self.nc.alloc_semaphore(name=name)
        self.used.append(s)
        return s

    def begin_stage(self, stage):
        nc, used = self.nc, self.used
        by_dma = lambda name: name.rstrip("0123456789").endswith(("loaded", "w_ready", "lora_ready", "stored", "x_back"))
        names = SEMAPHORES.get(stage, "").split()
        self.stage = stage
        for s in used:
            nc.release_semaphore(s)
        self.started = {n: nc.alloc_semaphore(name=n) for n in names if not by_dma(n)}
        with nc.Block() as block:
            @block.gpsimd
            def _(pool):
                for s in used:
                    pool.sem_clear(s)
                for s in self.started.values():
                    pool.sem_inc(s, FROM)
        self.used = list(self.started.values())

    def c(self, name, n=P, at=0):
        g, o = CON[name]
        return self.con[g][:, o + at:o + at + n]

    def v(self, name, j=0, n=1):
        return self.vec[:, VEC[name] + j:VEC[name] + j + n]

    def m(self, src, layer, which, k):
        j = (layer * 6 + which) * KD + k
        return self.mod[:, src, j:j + 1]


def modulation(K, A, mod_dram):
    nc, vec, mod, scale = K.nc, K.vec, K.mod, K.scale
    NB = 4
    with ExitStack() as ctx:
        w = [K.sb(f"ada_w{j}", [P, KD, 512], ctx) for j in range(NB)]
        sc = K.sb("silu_c", [P, KD, 2], ctx)
        row = K.sb("mod_row", [2, DEPTH * NCOL, 512], ctx)
        rows = K.sb("mod_rows", [DEPTH * 6 * KD, 2, P], ctx)
        pr = [K.ps(f"mod_p{j}", [2, 512], ctx) for j in range(NB)]
        pt = K.ps("mod_t", [P, 2, DEPTH * 6 * KD], ctx)
        small = K.sem("mod_small_loaded")
        w_ready = [K.sem(f"mod_w_ready{j}") for j in range(NB)]
        silu = K.sem("mod_silu_done")
        prod = [K.sem(f"mod_product_done{j}") for j in range(NB)]
        copied = [K.sem(f"mod_row_copied{j}") for j in range(NB)]
        stored = K.sem("mod_row_stored")
        back = K.sem("mod_rows_loaded")
        turned = K.sem("mod_rows_turned")
        done = K.sem("mod_columns_done")
        n_it = DEPTH * NCOL // NB
        with nc.Block() as block:
            @block.sync
            def _(sp):
                sp.dma_start(vec[:], A["vecs"]).then_inc(small, 16)
                for g, t in K.con.items():
                    sp.dma_start(t[:], A["con_" + g]).then_inc(small, 16)
                for j in range(NB):
                    sp.dma_start(w[j][:], A["ada"][j]).then_inc(w_ready[j], 16)
                with sp.Fori(1, n_it) as i:
                    for j in range(NB):
                        sp.wait_ge(prod[j], FROM + i)
                        sp.dma_start(w[j][:], A["ada"][bass.ds(i * NB + j, 1)].rearrange("o p k n -> (o p) k n")
                                     ).then_inc(w_ready[j], 16)
                sp.dma_start(K.x[:], A["xT"]).then_inc(small, 16)
                for j in range(NB):
                    sp.wait_ge(copied[j], FROM + n_it)
                sp.dma_start(mod_dram, row[:]).then_inc(stored, 16)
                sp.wait_ge(stored, 16)
                for s in range(2):
                    sp.dma_start(rows[:, s, :], mod_dram[s].rearrange("c (b p) -> (c b) p", p=P)).then_inc(back, 16)
                sp.wait_ge(small, 16 * (2 + len(K.con)))

            @block.scalar
            def _(act):
                act.wait_ge(small, 16 * (1 + len(K.con)))
                for s, name in enumerate(("c", "c_ctx")):
                    nc.scalar.activation(sc[:, :, s], K.v(name, 0, KD), ACT.Silu).then_inc(silu, 1)

            @block.tensor
            def _(pe):
                pe.wait_ge(silu, FROM + 2)
                with pe.Fori(0, n_it) as i:
                    for j in range(NB):
                        pe.wait_ge(w_ready[j], 16 * i + 16)
                        pe.wait_ge(copied[j], FROM + i)
                        for k in range(KD):
                            last = nc.tensor.matmul(pr[j][:], sc[:, k, :], w[j][:, k, :], start=k == 0, stop=k == KD - 1)
                        last.then_inc(prod[j], 1)
                pe.wait_ge(back, 32)
                n = DEPTH * 6 * KD
                for s in range(2):
                    last = nc.tensor.transpose(pt[:, s, :], rows[:, s, :], K.c("ident")[0:n, 0:n])
                last.then_inc(turned, 1)

            @block.vector
            def _(dve):
                with dve.Fori(0, n_it) as i:
                    for j in range(NB):
                        dve.wait_ge(prod[j], FROM + i + 1)
                        nc.vector.tensor_copy(row[:, bass.ds(i * NB + j, 1), :].rearrange("s o n -> s (o n)"), pr[j][:]
                                              ).then_inc(copied[j], 1)
                dve.wait_ge(turned, FROM + 1)
                n = DEPTH * 6 * KD
                for s in range(2):
                    nc.vector.tensor_tensor(mod[:, s, :], pt[:, s, :], K.v("ada_b", 0, n), ALU.add).then_inc(done, 1)
                dve.wait_ge(done, FROM + 2)
                for s in range(2):
                    for l in range(DEPTH):
                        for j in range(2):
                            at = (l * 6 + 3 * j + 1) * KD
                            o = (l * 2 + j) * KD
                            last = nc.vector.scalar_tensor_tensor(out=scale[:, s, o:o + KD], in0=mod[:, s, at:at + KD],
                                                                  scalar=1.0, in1=K.v("norm_g", o, KD),
                                                                  op0=ALU.add, op1=ALU.mult)


def norm(K, tag, layer, sub, final=None, ahead=None):
    nc, x, h = K.nc, K.x, K.h
    with ExitStack() as ctx:
        sq = K.sb(f"{tag}_sq", [P, KD, TOK], ctx)
        ms = K.sb(f"{tag}_ms", [P, TOK], ctx)
        rstd = K.sb(f"{tag}_rstd", [P, TOK], ctx)
        ps = K.ps(f"{tag}_ps", [P, 1024], ctx)
        squared = K.sem(f"{tag}_squared")
        summed = K.sem(f"{tag}_summed")
        mean = K.sem(f"{tag}_mean")
        rooted = K.sem(f"{tag}_rooted")
        inv = K.sem(f"{tag}_inverse")
        scaled = K.sem(f"{tag}_scaled")
        stored = K.sem(f"{tag}_stored")
        spans = ((LATR, slice(0, LAT)), (CTXR, slice(512, 512 + CTX)))
        with nc.Block() as block:
            @block.scalar
            def _(act):
                for k in range(KD):
                    nc.scalar.activation(sq[:, k, :], x[:, k, :], ACT.Square).then_inc(squared, 1)
                act.wait_ge(mean, FROM + 2)
                nc.scalar.activation(rstd[:], ms[:], ACT.Sqrt).then_inc(rooted, 1)
                if final is None:
                    for k in range(KD):
                        act.wait_ge(scaled, FROM + 2 * k + 2)
                        for s, r in RANGES:
                            nc.scalar.activation(h[:, k, r], h[:, k, r], ACT.Identity,
                                                 bias=K.m(s, layer, 3 * sub, k))

            @block.tensor
            def _(pe):
                for k in range(KD):
                    pe.wait_ge(squared, FROM + k + 1)
                    for r, b in spans:
                        last = nc.tensor.matmul(ps[:, b], K.c("ones"), sq[:, k, r], start=k == 0, stop=k == KD - 1)
                last.then_inc(summed, 1)

            @block.vector
            def _(dve):
                dve.wait_ge(summed, FROM + 1)
                for r, b in spans:
                    nc.vector.tensor_scalar(ms[:, r], ps[:, b], 1.0 / D, EPS, ALU.mult, ALU.add).then_inc(mean, 1)
                dve.wait_ge(rooted, FROM + 1)
                nc.vector.reciprocal(ms[:], rstd[:]).then_inc(inv, 1)
                dve.wait_ge(inv, FROM + 1)
                for k in range(KD):
                    if final is not None:
                        nc.vector.scalar_tensor_tensor(out=h[:, k, LATR], in0=x[:, k, LATR], scalar=K.v("final_g", k),
                                                       in1=ms[:, LATR], op0=ALU.mult, op1=ALU.mult).then_inc(scaled, 1)
                        continue
                    for s, r in RANGES:
                        o = (layer * 2 + sub) * KD + k
                        nc.vector.scalar_tensor_tensor(out=h[:, k, r], in0=x[:, k, r], scalar=K.scale[:, s, o:o + 1],
                                                       in1=ms[:, r], op0=ALU.mult, op1=ALU.mult).then_inc(scaled, 1)

            if ahead is not None:
                @block.sync
                def _(sp):
                    ahead(sp)

            if final is not None:
                @block.sync
                def _(sp):
                    for k in range(KD):
                        sp.wait_ge(scaled, FROM + k + 1)
                        sp.dma_start(final[:, k, :], h[:, k, LATR]).then_inc(stored, 16)
                    sp.wait_ge(stored, 16 * KD)


def project_qk(K, A, qk):
    nc, h = K.nc, K.h
    with ExitStack() as ctx:
        w = [K.sb(f"qk_w{j}", [P, KD, P], ctx) for j in range(2)]
        g = K.sb("qk_g", [P, NQ + NKV], ctx)
        sq = [K.sb(f"qk_sq{j}", [P, TOK], ctx) for j in range(2)]
        ms = [K.sb(f"qk_ms{j}", [P, TOK], ctx) for j in range(2)]
        rt = [K.sb(f"qk_rt{j}", [P, TOK], ctx) for j in range(2)]
        qn = [K.sb(f"qk_qn{j}", [P, TOK], ctx) for j in range(2)]
        qc = [K.sb(f"qk_cos{j}", [P, LAT], ctx) for j in range(2)]
        qs = [K.sb(f"qk_sin{j}", [P, LAT], ctx) for j in range(2)]
        raw = [K.ps(f"qk_raw{j}", [P, 1024], ctx) for j in range(2)]
        ss = K.ps("qk_ss", [P, 1024], ctx)
        rot = [K.ps(f"qk_rot{j}", [P, LAT], ctx) for j in range(2)]
        sems = {n: [K.sem(f"qk_{n}{j}") for j in range(2)] for n in
                ("w_ready", "proj_lat", "proj", "squared", "summed", "mean", "rooted", "inverse", "normed",
                 "swapped", "cosed", "sined", "written", "ctx_copied")}
        gains = K.sem("qk_gains")
        n_it = (NQ + NKV) // 2
        spans = ((LATR, slice(0, LAT)), (CTXR, slice(512, 512 + CTX)))
        S = lambda n, j: sems[n][j]
        with nc.Block() as block:
            @block.sync
            def _(sp):
                for j in range(2):
                    sp.dma_start(w[j][:], A["w_in"][j]).then_inc(S("w_ready", j), 16)
                with sp.Fori(1, n_it) as i:
                    for j in range(2):
                        sp.wait_ge(S("proj", j), FROM + i)
                        sp.dma_start(w[j][:], A["w_in"][bass.ds(2 * i + j, 1)].rearrange("o p k n -> (o p) k n")
                                     ).then_inc(S("w_ready", j), 16)

            @block.tensor
            def _(pe):
                def project(i, j):
                    pe.wait_ge(S("w_ready", j), 16 * i + 16)
                    pe.wait_ge(S("normed", j), FROM + 2 * i)
                    for r, b in spans:
                        for k in range(KD):
                            last = nc.tensor.matmul(raw[j][:, b], w[j][:, k, :], h[:, k, r], start=k == 0, stop=k == KD - 1)
                        last.then_inc(S("proj_lat" if r is LATR else "proj", j), 1)

                def sums(i, j):
                    pe.wait_ge(S("mean", 1 - j), FROM + 2 * i + 2 * j)
                    for n, (r, b) in enumerate(spans):
                        pe.wait_ge(S("squared", j), FROM + 2 * i + 1 + n)
                        last = nc.tensor.matmul(ss[:, b], K.c("ones"), sq[j][:, r], start=True, stop=True)
                    last.then_inc(S("summed", j), 1)

                def swap(i, j):
                    pe.wait_ge(S("normed", j), FROM + 2 * i + 2)
                    pe.wait_ge(S("sined", j), FROM + i)
                    nc.tensor.matmul(rot[j][:], K.c("swap"), qn[j][:, LATR], start=True, stop=True
                                     ).then_inc(S("swapped", j), 1)

                def two_heads(i, more):
                    sums(i, 0)
                    project(i, 1)
                    swap(i, 0)
                    sums(i, 1)
                    if more:
                        project(i + 1, 0)
                    swap(i, 1)

                project(0, 0)
                with pe.Fori(0, n_it - 1) as i:
                    two_heads(i, True)
                two_heads(n_it - 1, False)

            @block.scalar
            def _(act):
                with act.Fori(0, n_it) as i:
                    for j in range(2):
                        act.wait_ge(S("summed", j), FROM + i)
                        for n, (r, b) in enumerate(spans):
                            act.wait_ge(S("proj_lat" if n == 0 else "proj", j), FROM + i + 1)
                            nc.scalar.activation(sq[j][:, r], raw[j][:, b], ACT.Square).then_inc(S("squared", j), 1)
                        act.wait_ge(S("mean", j), FROM + 2 * i + 2)
                        act.wait_ge(S("inverse", j), FROM + i)
                        nc.scalar.activation(rt[j][:], ms[j][:], ACT.Sqrt).then_inc(S("rooted", j), 1)

            @block.vector
            def _(dve):
                for n in range(NQ + NKV):
                    nc.vector.tensor_copy(g[:, n:n + 1], K.v("q_g" if n < NQ else "k_g")).then_inc(gains, 1)
                dve.wait_ge(gains, FROM + NQ + NKV)
                with dve.Fori(0, n_it) as i:
                    for j in range(2):
                        dve.wait_ge(S("summed", j), FROM + i + 1)
                        for r, b in spans:
                            nc.vector.tensor_scalar(ms[j][:, r], ss[:, b], 1.0 / HD, EPS, ALU.mult, ALU.add
                                                    ).then_inc(S("mean", j), 1)
                        dve.wait_ge(S("rooted", j), FROM + i + 1)
                        nc.vector.reciprocal(ms[j][:], rt[j][:]).then_inc(S("inverse", j), 1)
                        dve.wait_ge(S("inverse", j), FROM + i + 1)
                        dve.wait_ge(S("cosed", j), FROM + i)
                        dve.wait_ge(S("ctx_copied", j), FROM + i)
                        for r, b in spans:
                            nc.vector.scalar_tensor_tensor(out=qn[j][:, r], in0=raw[j][:, b], scalar=g[:, bass.ds(2 * i + j, 1)],
                                                           in1=ms[j][:, r], op0=ALU.mult, op1=ALU.mult
                                                           ).then_inc(S("normed", j), 1)
                        dve.wait_ge(S("swapped", j), FROM + i + 1)
                        dve.wait_ge(S("written", j), FROM + i)
                        nc.vector.tensor_tensor(qs[j][:], rot[j][:], K.c("sin", LAT), ALU.mult).then_inc(S("sined", j), 1)

            @block.gpsimd
            def _(pool):
                with pool.Fori(0, n_it) as i:
                    for j in range(2):
                        pool.wait_ge(S("normed", j), FROM + 2 * i + 2)
                        pool.wait_ge(S("written", j), FROM + i)
                        nc.gpsimd.tensor_tensor(qc[j][:], qn[j][:, LATR], K.c("cos", LAT), ALU.mult).then_inc(S("cosed", j), 1)
                        head = qk[:, bass.ds(2 * i + j, 1), :].rearrange("p o t -> p (o t)")
                        nc.gpsimd.tensor_copy(head[:, CTXR], qn[j][:, CTXR]).then_inc(S("ctx_copied", j), 1)
                        pool.wait_ge(S("cosed", j), FROM + i + 1)
                        pool.wait_ge(S("sined", j), FROM + i + 1)
                        nc.gpsimd.tensor_tensor(head[:, LATR], qc[j][:], qs[j][:], ALU.add).then_inc(S("written", j), 1)


def split_product(nc, out, w, x, start, stop):
    nc.tensor.matmul(out, w[0], x[0], start=start, stop=False)
    nc.tensor.matmul(out, w[0], x[1], start=False, stop=False)
    return nc.tensor.matmul(out, w[1], x[0], start=False, stop=stop)


def project_v_conv(K, A, v, o):
    nc, h = K.nc, K.h
    with ExitStack() as ctx:
        wv = K.sb("v_w", [P, NKV, KD, P], ctx)
        w = [[K.sb(f"conv_w{j}_{m}", [P, KD, P], ctx) for m in range(3)] for j in range(2)]
        PADC, PADL = 1, CTX + 3
        gc = [K.sb(f"conv_gc{j}", [P, TOK], ctx) for j in range(2)]
        u = [K.sb(f"conv_u{j}", [P, TOK + 4], ctx) for j in range(2)]
        y = [K.sb(f"conv_y{j}", [P, TOK], ctx) for j in range(2)]
        lead = wv[:, 0]
        ws = [[K.sb(f"conv_ws{j}_{n}", [P, KD, P], ctx, F32R) for n in range(2)] for j in range(2)]
        hs = [K.sb(f"conv_h{n}", [P, KD, TOK], ctx, F32R) for n in range(2)]
        h_lead, h_rest, h_split = (K.sem(f"conv_{n}") for n in ("h_lead", "h_rest", "h_split"))
        w_lead, w_rest, w_split = (K.sem(f"conv_{n}") for n in ("weights_lead", "weights_rest", "weights_split"))
        pv = [K.ps(f"v_p{j}", [P, 512], ctx) for j in range(2)]
        pg = [K.ps(f"conv_p{m}", [P, 1024], ctx) for m in range(3)]
        wv_ready, v_prod, v_out, zeroed = (K.sem(f"v_{n}") for n in ("w_ready", "product", "copied", "pads_zeroed"))
        sems = {n: [K.sem(f"conv_{n}{j}") for j in range(2)] for n in
                ("w_ready", "copied", "gated", "mid", "left", "right", "written")}
        prod = [K.sem(f"conv_product{m}") for m in range(3)]
        S = lambda n, j: sems[n][j]
        spans = ((LATR, slice(0, LAT)), (CTXR, slice(512, 512 + CTX)))
        segs = ((LATR, PADL, slice(0, LAT)), (CTXR, PADC, slice(512, 512 + CTX)))
        FIRST = (28, 20, 12)
        ORDER = (1, 0, 2)
        n_it = KD // 2
        def steps(eng, step):
            with eng.Fori(0, n_it - 1) as i:
                for j in range(2):
                    step(i, j, True)
            step(n_it - 1, 0, True)
            step(n_it - 1, 1, False)

        VCH = NQ + NKV

        def col(name, c):
            return K.vec[:, bass.ds(c + VEC[name], 1)]

        with nc.Block() as block:
            @block.sync
            def _(sp):
                for m in range(NKV):
                    sp.dma_start(wv[:, m], A["w_in"][VCH + m]).then_inc(wv_ready, 16)
                with sp.Fori(0, n_it) as i:
                    for j in range(2):
                        sp.wait_ge(S("written", j), FROM + i)
                        for m in ORDER:
                            sp.dma_start(w[j][m][:], A["w_in"][bass.ds(2 * i + j + FIRST[m], 1)].rearrange("o p k n -> (o p) k n")
                                         ).then_inc(S("w_ready", j), 16)

            @block.tensor
            def _(pe):
                pe.wait_ge(wv_ready, 16 * NKV)
                for t in range(NT):
                    if t >= 2:
                        pe.wait_ge(v_out, FROM + t - 1)
                    for m in range(NKV):
                        for k in range(KD):
                            last = nc.tensor.matmul(pv[t % 2][:, m * P:(m + 1) * P], h[:, k, t * P:(t + 1) * P], wv[:, m, k, :],
                                                    start=k == 0, stop=k == KD - 1)
                    last.then_inc(v_prod, 1)

                def step(i, j, more):
                    for x, m in enumerate(ORDER):
                        n = 6 * i + 3 * j + x
                        pe.wait_ge(w_rest, FROM + n + 1)
                        pe.wait_ge(w_split, FROM + n + 1)
                        if j == 1:
                            pe.wait_ge(S(("gated", "copied", "written")[m], 0), FROM + (2, 2, 1)[m] * (i + 1))
                        else:
                            pe.wait_ge(S(("gated", "copied", "written")[m], 1), FROM + (2, 2, 1)[m] * i)
                        for r, b in spans:
                            for k in range(KD):
                                pe.wait_ge(h_split, FROM + k + 1)
                                wk = [t[:, k, :] for t in ws[(3 * j + x) % 2]]
                                last = split_product(nc, pg[m][:, b], wk, [t[:, k, r] for t in hs], k == 0, k == KD - 1)
                        last.then_inc(prod[m], 1)

                steps(pe, step)

            @block.scalar
            def _(act):
                for t in range(NT):
                    act.wait_ge(v_prod, FROM + t + 1)
                    nc.scalar.activation(v[:, t, :], pv[t % 2][:, 0:NKV * P], ACT.Copy).then_inc(v_out, 1)

                for k in range(KD):
                    act.wait_ge(h_rest, FROM + k + 1)
                    nc.scalar.activation(hs[0][:, k, :], y[k % 2][:], ACT.Copy).then_inc(h_split, 1)

                def split(i, j, x):
                    act.wait_ge(w_lead, FROM + (6 * i + 3 * j + x) + 1)
                    nc.scalar.activation(ws[(3 * j + x) % 2][0][:], lead, ACT.Copy).then_inc(w_split, 1)

                def step(i, j, more):
                    split(i, j, 1)
                    split(i, j, 2)
                    if more:
                        split(i + j, 1 - j, 0)
                    act.wait_ge(prod[1], FROM + 2 * i + j + 1)
                    act.wait_ge(S("gated", j), FROM + 2 * i)
                    for r, b in spans:
                        nc.scalar.activation(gc[j][:, r], pg[1][:, b], ACT.Copy).then_inc(S("copied", j), 1)

                split(0, 0, 0)
                steps(act, step)

            @block.vector
            def _(dve):
                for j in range(2):
                    nc.vector.memset(u[j][:], 0.0).then_inc(zeroed, 1)
                dve.wait_ge(zeroed, FROM + 2)
                for k in range(KD):
                    if k >= 2:
                        dve.wait_ge(h_split, FROM + k - 1)
                    nc.vector.tensor_scalar(y[k % 2][:].bitcast(U32), h[:, k, :].bitcast(U32), LEADING, None, ALU.bitwise_and
                                            ).then_inc(h_lead, 1)
                    dve.wait_ge(h_lead, FROM + k + 1)
                    nc.vector.tensor_tensor(hs[1][:, k, :], h[:, k, :], y[k % 2][:], ALU.subtract).then_inc(h_rest, 1)
                dve.wait_ge(h_split, FROM + KD)

                def split(i, j, x):
                    n = 6 * i + 3 * j + x
                    m = ORDER[x]
                    first = isinstance(i, int) and i == 0 and j == 0
                    dve.wait_ge(S("w_ready", j), 48 * i + 48)
                    if not (first and x == 0):
                        dve.wait_ge(w_split, FROM + n)
                        dve.wait_ge(w_rest, FROM + n)
                    if x == 2:
                        dve.wait_ge(prod[ORDER[0]], FROM + 2 * i + j + 1)
                    elif not first:
                        dve.wait_ge(prod[ORDER[x + 1]], FROM + 2 * i + j)
                    nc.vector.tensor_scalar(lead.bitcast(U32), w[j][m][:].bitcast(U32), LEADING, None, ALU.bitwise_and).then_inc(w_lead, 1)
                    dve.wait_ge(w_lead, FROM + n + 1)
                    nc.vector.tensor_tensor(ws[(3 * j + x) % 2][1][:], w[j][m][:], lead, ALU.subtract).then_inc(w_rest, 1)

                def step(i, j, more):
                    split(i, j, 1)
                    split(i, j, 2)
                    if more:
                        split(i + j, 1 - j, 0)
                    c = 2 * i + j
                    dve.wait_ge(prod[0], FROM + 2 * i + j + 1)
                    dve.wait_ge(S("copied", j), FROM + 2 * i + 2)
                    dve.wait_ge(S("written", j), FROM + i)
                    for r, at, b in segs:
                        n = r.stop - r.start
                        nc.vector.tensor_tensor(u[j][:, at:at + n], pg[0][:, b], gc[j][:, r], ALU.mult
                                                ).then_inc(S("gated", j), 1)
                    dve.wait_ge(S("gated", j), FROM + 2 * i + 2)
                    for r, at, b in segs:
                        n = r.stop - r.start
                        nc.vector.tensor_scalar(y[j][:, r], u[j][:, at:at + n], col("conv_w", c + KD), None, ALU.mult
                                                ).then_inc(S("mid", j), 1)
                    dve.wait_ge(S("mid", j), FROM + 2 * i + 2)
                    for r, at, b in segs:
                        n = r.stop - r.start
                        nc.vector.scalar_tensor_tensor(out=y[j][:, r], in0=u[j][:, at - 1:at - 1 + n], scalar=col("conv_w", c),
                                                       in1=y[j][:, r], op0=ALU.mult, op1=ALU.add).then_inc(S("left", j), 1)
                    dve.wait_ge(S("left", j), FROM + 2 * i + 2)
                    for r, at, b in segs:
                        n = r.stop - r.start
                        nc.vector.scalar_tensor_tensor(out=y[j][:, r], in0=u[j][:, at + 1:at + 1 + n], scalar=col("conv_w", c + 2 * KD),
                                                       in1=y[j][:, r], op0=ALU.mult, op1=ALU.add).then_inc(S("right", j), 1)
                    dve.wait_ge(S("right", j), FROM + 2 * i + 2)
                    dve.wait_ge(prod[2], FROM + 2 * i + j + 1)
                    dst = o[:, bass.ds(c, 1), :].rearrange("p o t -> p (o t)")
                    for r, at, b in segs:
                        op = nc.vector.tensor_tensor(dst[:, r], pg[2][:, b], y[j][:, r], ALU.mult)
                    op.then_inc(S("written", j), 1)

                dve.wait_ge(v_prod, FROM + NT)
                split(0, 0, 0)
                steps(dve, step)


def attend(K, qk, v, o):
    nc = K.nc
    SCALE = HD ** -0.5
    TILES = [(kv, t, NT if t >= CT else CT) for kv in range(NKV) for t in list(range(CT, NT)) + list(range(CT))]
    n_tiles = len(TILES)
    half = n_tiles // 2
    with ExitStack() as ctx:
        qs = [K.sb(f"at_q{kv}", [P, TOK], ctx) for kv in range(NKV)]
        p = [K.sb(f"at_p{j}", [P, TOK], ctx) for j in range(2)]
        mx = [K.sb(f"at_max{j}", [P, 1], ctx) for j in range(2)]
        sm = [K.sb(f"at_sum{j}", [P, 1], ctx) for j in range(2)]
        rc = [K.sb(f"at_rec{j}", [P, 1], ctx) for j in range(2)]
        nb = [K.sb(f"at_bias{j}", [P, 1], ctx) for j in range(2)]
        ptl = [K.sb(f"at_ptl{kv}", [P, NT, LAT], ctx) for kv in range(NKV)]
        ptc = [K.sb(f"at_ptc{kv}", [P, CT, CTX], ctx) for kv in range(NKV)]
        sc = [K.ps(f"at_s{j}", [P, 1024], ctx) for j in range(2)]
        tr = K.ps("at_t", [P, 1024], ctx)
        po = K.ps("at_o", [P, 1024], ctx)
        per = {n: [K.sem(f"at_{n}{j}") for j in range(2)] for n in
               ("scored", "maxed", "biased", "exped", "summed", "scaled", "turned", "copied_a", "copied_v")}
        staged = [K.sem(f"at_staged{kv}") for kv in range(NKV)]
        summed_up = [K.sem(f"at_weighed{kv}") for kv in range(NKV)]
        out = [K.sem(f"at_out{kv}") for kv in range(NKV)]
        S = lambda n, j: per[n][j]
        with nc.Block() as block:
            @block.gpsimd
            def _(pool):
                with pool.Fori(0, QPK) as g:
                    for kv in range(NKV):
                        pool.wait_ge(summed_up[kv], FROM + g)
                        nc.gpsimd.tensor_copy(qs[kv][:], qk[:, bass.ds(g + kv * QPK, 1), :].rearrange("p o t -> p (o t)")
                                              ).then_inc(staged[kv], 1)

            @block.tensor
            def _(pe):
                def scores(g, n):
                    kv, t, keys = TILES[n]
                    j = n % 2
                    pe.wait_ge(staged[kv], FROM + g + 1)
                    pe.wait_ge(S("exped", j), FROM + half * g + n // 2)
                    last = nc.tensor.matmul(sc[j][:, 0:min(keys * P, 512)], qs[kv][:, t * P:(t + 1) * P],
                                            qk[:, NQ + kv, 0:min(keys * P, 512)], start=True, stop=True)
                    if keys > 4:
                        last = nc.tensor.matmul(sc[j][:, 512:keys * P], qs[kv][:, t * P:(t + 1) * P],
                                                qk[:, NQ + kv, 512:keys * P], start=True, stop=True)
                    last.then_inc(S("scored", j), 1)

                def turn(g, n):
                    kv, t, keys = TILES[n]
                    j = n % 2
                    pe.wait_ge(S("scaled", j), FROM + half * g + n // 2 + 1)
                    m = (half * g + n // 2 + (0 if j == 0 else 1))
                    pe.wait_ge(S("copied_a", 1 - j), FROM + m)
                    pe.wait_ge(S("copied_v", 1 - j), FROM + m)
                    for b in range(keys):
                        at = b * P if b < keys // 2 else 512 + (b - keys // 2) * P
                        last = nc.tensor.transpose(tr[:, at:at + P], p[j][:, b * P:(b + 1) * P], K.c("ident"))
                    last.then_inc(S("turned", j), 1)

                def weigh(g, kv):
                    for j in range(2):
                        m = half * g + (kv + 1) * half // 2
                        pe.wait_ge(S("copied_a", j), FROM + m)
                        pe.wait_ge(S("copied_v", j), FROM + m)
                    if kv == 1:
                        pe.wait_ge(out[0], FROM + 2 * g + 2)
                    else:
                        pe.wait_ge(out[1], FROM + 2 * g)
                    for b in range(NT):
                        nc.tensor.matmul(po[:, 0:LAT], v[:, b, kv * HD:(kv + 1) * HD], ptl[kv][:, b, :], start=b == 0, stop=b == NT - 1)
                    for b in range(CT):
                        last = nc.tensor.matmul(po[:, 512:512 + CTX], v[:, b, kv * HD:(kv + 1) * HD], ptc[kv][:, b, :],
                                                start=b == 0, stop=b == CT - 1)
                    last.then_inc(summed_up[kv], 1)

                with pe.Fori(0, QPK) as g:
                    scores(g, 0)
                    for n in range(n_tiles):
                        if n + 1 < n_tiles:
                            scores(g, n + 1)
                        turn(g, n)
                        if n == half:
                            weigh(g, 0)
                    weigh(g, 1)

            @block.vector
            def _(dve):
                def tile(g, n):
                    kv, t, keys = TILES[n]
                    j = n % 2
                    m = half * g + n // 2
                    dve.wait_ge(S("scored", j), FROM + m + 1)
                    dve.wait_ge(S("biased", j), FROM + m)
                    nc.vector.tensor_reduce(mx[j][:], sc[j][:, 0:keys * P], AX.X, ALU.max).then_inc(S("maxed", j), 1)

                def scale(g, n):
                    kv, t, keys = TILES[n]
                    j = n % 2
                    m = half * g + n // 2
                    dve.wait_ge(S("exped", j), FROM + m + 1)
                    nc.vector.reciprocal(rc[j][:], sm[j][:]).then_inc(S("summed", j), 1)
                    dve.wait_ge(S("summed", j), FROM + m + 1)
                    nc.vector.tensor_scalar(p[j][:, 0:keys * P], p[j][:, 0:keys * P], rc[j][:], None, ALU.mult
                                            ).then_inc(S("scaled", j), 1)

                def copy(g, n):
                    kv, t, keys = TILES[n]
                    j = n % 2
                    m = half * g + n // 2
                    dve.wait_ge(S("turned", j), FROM + m + 1)
                    dve.wait_ge(summed_up[kv], FROM + g)
                    lo = keys // 2
                    dst = ptl[kv][:, lo:keys, (t - CT) * P:(t - CT + 1) * P] if t >= CT else ptc[kv][:, lo:keys, t * P:(t + 1) * P]
                    nc.vector.tensor_copy(dst, tr[:, 512:512 + (keys - lo) * P].rearrange("p (b q) -> p b q", q=P)
                                          ).then_inc(S("copied_v", j), 1)

                def store(g, kv):
                    dve.wait_ge(summed_up[kv], FROM + g + 1)
                    dst = o[:, bass.ds(g + kv * QPK, 1), :].rearrange("p o t -> p (o t)")
                    nc.vector.tensor_copy(dst[:, LATR], po[:, 0:LAT]).then_inc(out[kv], 1)
                    nc.vector.tensor_copy(dst[:, CTXR], po[:, 512:512 + CTX]).then_inc(out[kv], 1)

                with dve.Fori(0, QPK) as g:
                    tile(g, 0)
                    for n in range(n_tiles):
                        scale(g, n)
                        if n + 1 < n_tiles:
                            tile(g, n + 1)
                        copy(g, n)
                        if n == half + 1:
                            store(g, 0)
                    store(g, 1)

            @block.scalar
            def _(act):
                def exps(g, n):
                    kv, t, keys = TILES[n]
                    j = n % 2
                    m = half * g + n // 2
                    act.wait_ge(S("maxed", j), FROM + m + 1)
                    act.wait_ge(S("exped", j), FROM + m)
                    nc.scalar.mul(nb[j][:], mx[j][:], -SCALE).then_inc(S("biased", j), 1)
                    act.wait_ge(S("biased", j), FROM + m + 1)
                    act.wait_ge(S("turned", j), FROM + m)
                    act.wait_ge(S("summed", j), FROM + m)
                    nc.scalar.activation(p[j][:, 0:keys * P], sc[j][:, 0:keys * P], ACT.Exp, bias=nb[j][:], scale=SCALE,
                                         accum_out=sm[j][:]).then_inc(S("exped", j), 1)

                def copy(g, n):
                    kv, t, keys = TILES[n]
                    j = n % 2
                    m = half * g + n // 2
                    act.wait_ge(S("turned", j), FROM + m + 1)
                    act.wait_ge(summed_up[kv], FROM + g)
                    hi = keys // 2
                    dst = ptl[kv][:, 0:hi, (t - CT) * P:(t - CT + 1) * P] if t >= CT else ptc[kv][:, 0:hi, t * P:(t + 1) * P]
                    nc.scalar.activation(dst, tr[:, 0:hi * P].rearrange("p (b q) -> p b q", q=P), ACT.Copy
                                         ).then_inc(S("copied_a", j), 1)

                with act.Fori(0, QPK) as g:
                    exps(g, 0)
                    for n in range(n_tiles):
                        if n + 1 < n_tiles:
                            exps(g, n + 1)
                        copy(g, n)


def project_out(K, tag, weights, o, chunks, layer, ranges, spilled=None):
    nc, x = K.nc, K.x
    with ExitStack() as ctx:
        w = [K.sb(f"{tag}_w{j}", [P, chunks, P], ctx) for j in range(2)]
        ps = [K.ps(f"{tag}_p{j}", [P, 1024], ctx) for j in range(2)]
        w_ready = [K.sem(f"{tag}_w_ready{j}") for j in range(2)]
        prod = [K.sem(f"{tag}_product{j}") for j in range(2)]
        added = [K.sem(f"{tag}_added{j}") for j in range(2)]
        x_back = K.sem(f"{tag}_x_back")
        bank = {0: slice(0, LAT), 1: slice(512, 512 + CTX)}
        n_it = KD // 2
        with nc.Block() as block:
            @block.sync
            def _(sp):
                for j in range(2):
                    sp.dma_start(w[j][:], weights[j]).then_inc(w_ready[j], 16)
                if spilled is not None:
                    sp.dma_start(x[:], spilled).then_inc(x_back, 16)
                with sp.Fori(1, n_it) as i:
                    for j in range(2):
                        sp.wait_ge(prod[j], FROM + i)
                        sp.dma_start(w[j][:], weights[bass.ds(2 * i + j, 1)].rearrange("o p k n -> (o p) k n")).then_inc(w_ready[j], 16)

            @block.tensor
            def _(pe):
                with pe.Fori(0, n_it) as i:
                    for j in range(2):
                        pe.wait_ge(w_ready[j], 16 * i + 16)
                        pe.wait_ge(added[j], FROM + len(ranges) * i)
                        for s, r in ranges:
                            ro = slice(r.start - TOK + o[0].shape[2], r.stop - TOK + o[0].shape[2])
                            for k in range(chunks):
                                last = nc.tensor.matmul(ps[j][:, bank[s]], w[j][:, k, :], o[k // KD][:, k % KD, ro], start=k == 0, stop=k == chunks - 1)
                        last.then_inc(prod[j], 1)

            @block.vector
            def _(dve):
                if spilled is not None:
                    dve.wait_ge(x_back, 16)
                with dve.Fori(0, n_it) as i:
                    for j in range(2):
                        dve.wait_ge(prod[j], FROM + i + 1)
                        xs = x[:, bass.ds(2 * i + j, 1), :].rearrange("p o t -> p (o t)")
                        for s, r in ranges:
                            gate = K.mod[:, s, bass.ds(2 * i + j + (layer * 6 + 2) * KD, 1)]
                            nc.vector.scalar_tensor_tensor(out=xs[:, r], in0=ps[j][:, bank[s]], scalar=gate, in1=xs[:, r],
                                                           op0=ALU.mult, op1=ALU.add).then_inc(added[j], 1)


def route(K, A, tag, layer, h2, slot, aff, ahead):
    nc, h = K.nc, K.h
    ctx_too = layer == 0
    tiles = list(range(0 if ctx_too else CT, NT))
    t0 = tiles[0]
    n = len(tiles)
    kinds = [(LATR, slice(0, LAT), CAP_L)] + ([(CTXR, slice(512, 512 + CTX), CAP_C)] if ctx_too else [])
    at = lambda t: (t - CT) * P if t >= CT else 512 + t * P
    with ExitStack() as ctx:
        rw = K.sb(f"{tag}_router", [P, KD, E], ctx)
        lg = K.sb(f"{tag}_logits", [E, TOK], ctx)
        ex = K.sb(f"{tag}_ex", [P, n, E], ctx)
        mx = K.sb(f"{tag}_mx", [P, n], ctx)
        rs = K.sb(f"{tag}_rs", [P, n], ctx)
        rr = K.sb(f"{tag}_rr", [P, n], ctx)
        work = K.sb(f"{tag}_work", [E, TOK], ctx)
        top = K.sb(f"{tag}_top", [E, 8], ctx)
        ones = K.sb(f"{tag}_ones", [E, TOK], ctx)
        cnt = K.sb(f"{tag}_cnt", [E, TOK], ctx)
        pl = K.ps(f"{tag}_pl", [E, 1024], ctx)
        pt = K.ps(f"{tag}_pt", [P, 512], ctx)
        pa = K.ps(f"{tag}_pa", [E, 1024], ctx)
        ph = [K.ps(f"{tag}_ph{j}", [P, 512], ctx) for j in range(2)]
        (loaded, logits, copied, turned, maxed, shifted, exped, summed, inv, affs, aff_turned, worked, found, replaced,
         picked, counted, placed, slot_turned) = (K.sem(f"{tag}_{x}") for x in (
             "router_loaded", "logits", "logits_copied", "logits_turned", "max", "shifted", "exped", "summed", "inverse",
             "affinity", "affinity_turned", "work", "top", "replaced", "picked", "counted", "placed", "slot_turned"))
        h_turned = [K.sem(f"{tag}_h_turned{j}") for j in range(2)]
        h_copied = [K.sem(f"{tag}_h_copied{j}") for j in range(2)]
        groups = [(t, g) for t in tiles for g in range(KD // 4)]
        with nc.Block() as block:
            @block.sync
            def _(sp):
                sp.dma_start(rw[:], A["router"][layer]).then_inc(loaded, 16)
                ahead(sp)

            @block.tensor
            def _(pe):
                pe.wait_ge(loaded, 16)
                for r, b, _ in kinds:
                    for k in range(KD):
                        last = nc.tensor.matmul(pl[:, b], rw[:, k, :], h[:, k, r], start=k == 0, stop=k == KD - 1)
                last.then_inc(logits, 1)

                def turn_h(lo, hi):
                    for m in range(lo, hi):
                        t, g = groups[m]
                        if m >= 2:
                            pe.wait_ge(h_copied[m % 2], FROM + m // 2)
                        for k in range(4):
                            last = nc.tensor.transpose(ph[m % 2][:, k * P:(k + 1) * P], h[:, 4 * g + k, t * P:(t + 1) * P], K.c("ident"))
                        last.then_inc(h_turned[m % 2], 1)

                turn_h(0, 2)
                pe.wait_ge(copied, FROM + len(kinds))
                for m, t in enumerate(tiles):
                    last = nc.tensor.transpose(pt[:, m * E:(m + 1) * E], lg[:, t * P:(t + 1) * P], K.c("ident")[0:E, 0:E])
                last.then_inc(turned, 1)
                turn_h(2, len(groups) // 2)
                pe.wait_ge(affs, FROM + 1)
                for m, t in enumerate(tiles):
                    last = nc.tensor.transpose(pa[:, at(t):at(t) + P], aff[:, t, :], K.c("ident"))
                last.then_inc(aff_turned, 1)
                turn_h(len(groups) // 2, len(groups))
                pe.wait_ge(placed, FROM + len(kinds))
                pe.wait_ge(shifted, FROM + 1)
                for m, t in enumerate(tiles):
                    last = nc.tensor.transpose(pt[:, m * E:(m + 1) * E], cnt[:, t * P:(t + 1) * P], K.c("ident")[0:E, 0:E])
                last.then_inc(slot_turned, 1)

            @block.scalar
            def _(act):
                act.wait_ge(logits, FROM + 1)
                for r, b, _ in kinds:
                    nc.scalar.activation(lg[:, r], pl[:, b], ACT.Copy).then_inc(copied, 1)

                def copy_h(lo, hi):
                    for m in range(lo, hi):
                        t, g = groups[m]
                        act.wait_ge(h_turned[m % 2], FROM + m // 2 + 1)
                        nc.scalar.activation(h2[:, t, 4 * g * P:(4 * g + 4) * P], ph[m % 2][:], ACT.Copy).then_inc(h_copied[m % 2], 1)

                copy_h(0, 2)
                act.wait_ge(shifted, FROM + 1)
                nc.scalar.activation(ex[:], ex[:], ACT.Exp).then_inc(exped, 1)
                copy_h(2, len(groups))

            @block.vector
            def _(dve):
                nc.vector.memset(ones[:], 1.0).then_inc(worked, 1)
                logit = pt[:, 0:n * E].rearrange("p (t e) -> p t e", e=E)
                dve.wait_ge(turned, FROM + 1)
                nc.vector.tensor_reduce(mx[:], logit, AX.X, ALU.max).then_inc(maxed, 1)
                dve.wait_ge(maxed, FROM + 1)
                nc.vector.tensor_tensor(ex[:], logit, mx[:].unsqueeze(2).broadcast_to([P, n, E]), ALU.subtract).then_inc(shifted, 1)
                dve.wait_ge(exped, FROM + 1)
                nc.vector.tensor_reduce(rs[:], ex[:], AX.X, ALU.add).then_inc(summed, 1)
                dve.wait_ge(summed, FROM + 1)
                nc.vector.reciprocal(rr[:], rs[:]).then_inc(inv, 1)
                dve.wait_ge(inv, FROM + 1)
                nc.vector.tensor_tensor(aff[:, t0:NT, :], ex[:], rr[:].unsqueeze(2).broadcast_to([P, n, E]), ALU.mult).then_inc(affs, 1)
                dve.wait_ge(aff_turned, FROM + 1)
                for r, b, _ in kinds:
                    nc.vector.tensor_copy(work[:, r], pa[:, b]).then_inc(worked, 1)
                rounds = 0
                for r, b, cap in kinds:
                    dve.wait_ge(worked, FROM + 1 + len(kinds))
                    for _ in range(cap // 8):
                        dve.wait_ge(replaced, FROM + rounds) if rounds else None
                        nc.vector.max(top[:], work[:, r]).then_inc(found, 1)
                        rounds += 1
                        dve.wait_ge(found, FROM + rounds)
                        nc.vector.match_replace(work[:, r], top[:], work[:, r], -1.0).then_inc(replaced, 1)
                dve.wait_ge(replaced, FROM + rounds)
                for m, (r, b, _) in enumerate(kinds):
                    nc.vector.tensor_scalar(work[:, r], work[:, r], 0.0, None, ALU.is_lt).then_inc(picked, 1)
                    dve.wait_ge(picked, FROM + m + 1)
                    nc.vector.tensor_tensor_scan(cnt[:, r], ones[:, r], work[:, r], 0.0, ALU.mult, ALU.add).then_inc(counted, 1)
                    dve.wait_ge(counted, FROM + 2 * m + 1)
                    nc.vector.tensor_tensor(cnt[:, r], cnt[:, r], work[:, r], ALU.mult).then_inc(counted, 1)
                    dve.wait_ge(counted, FROM + 2 * m + 2)
                    nc.vector.tensor_scalar(cnt[:, r], cnt[:, r], -1.0, None, ALU.add).then_inc(placed, 1)
                dve.wait_ge(slot_turned, FROM + 1)
                nc.vector.tensor_copy(slot[:, t0:NT, :], logit)


def experts(K, A, tag, layer, h2, slot, aff, load, views, w_ready):
    nc, x = K.nc, K.x
    ctx_too = layer == 0
    Q = 4
    NS = CAP_L + CAP_C if ctx_too else CAP_L
    NR = CAP_L + CAP_C
    with ExitStack() as ctx:
        hm_ = K.h[:].rearrange("p k t -> p (k t)")
        XS, SL, SCX = KD * Q * NS, NT - CT, CT
        xs = hm_[:, 0:XS].rearrange("p (k e j) -> p k e j", k=KD, e=Q)
        o = XS
        sel_l = hm_[:, o:o + SL * Q * CAP_L].rearrange("p (t e j) -> p t e j", t=SL, e=Q)
        o += SL * Q * CAP_L
        sw_l = hm_[:, o:o + SL * Q * CAP_L].rearrange("p (t e j) -> p t e j", t=SL, e=Q)
        o += SL * Q * CAP_L
        sel_c = hm_[:, o:o + SCX * Q * CAP_C].rearrange("p (t e j) -> p t e j", t=SCX, e=Q)
        o += SCX * Q * CAP_C
        sw_c = hm_[:, o:o + SCX * Q * CAP_C].rearrange("p (t e j) -> p t e j", t=SCX, e=Q)
        put_l = K.sb(f"{tag}_put_l", [P, 2, LAT], ctx)
        put_c = K.sb(f"{tag}_put_c", [P, CTX], ctx)
        sg = [K.sb(f"{tag}_sg{f}", [NS, 512], ctx) for f in range(2)]
        hid = [K.sb(f"{tag}_hid{f}", [NR, 512], ctx) for f in range(2)]
        hidT = [K.sb(f"{tag}_hidT{f}", [P, 4, NS], ctx) for f in range(2)]
        out_l = K.sb(f"{tag}_out_l", [P, D], ctx)
        out_c = K.sb(f"{tag}_out_c", [P, D], ctx)
        pg = [K.ps(f"{tag}_pg{f}", [P, 512], ctx) for f in range(2)]
        pu = [K.ps(f"{tag}_pu{f}", [P, 512], ctx) for f in range(2)]
        pt = [K.ps(f"{tag}_pt{f}", [P, 512], ctx) for f in range(2)]
        pd = [K.ps(f"{tag}_pd{f}", [P, 512], ctx) for f in range(2)]
        sem = lambda n: K.sem(f"{tag}_{n}")
        two = lambda n: [sem(f"{n}{f}") for f in range(2)]
        selected, weighted, put_turned, put_copied = (sem(n) for n in ("selected", "weighted", "put_turned", "put_copied"))
        gathered, xs_copied = two("gathered"), two("xs_copied")
        gated, upped, silued, hidden, turned, hid_copied, downed = (two(n) for n in (
            "gated", "upped", "silued", "hidden", "turned", "hid_copied", "downed"))
        out_copied = two("out_copied")
        spread, added = two("spread"), two("added")
        NB = KD // 2 * (3 if ctx_too else 2)
        padded = sem("padded")
        NPUT = 3 if ctx_too else 2

        def fours(eng, four):
            with eng.Fori(0, E // Q - 1) as q:
                four(q, True)
            four(E // Q - 1, False)

        with nc.Block() as block:
            @block.sync
            def _(sp):
                def load_next(n):
                    for s in range(6):
                        sp.wait_ge((gated[0], upped[0], gated[1], upped[1], downed[0], downed[1])[s], FROM + n)
                        load(sp, n, s)

                for e in range(1, Q):
                    load_next(e)
                with sp.Fori(1, E // Q) as q:
                    for e in range(Q):
                        load_next(Q * q + e)

            @block.tensor
            def _(pe):
                def gather(q):
                    pe.wait_ge(selected, FROM + q + 1)
                    for k in range(KD):
                        b = k % 2
                        pe.wait_ge(xs_copied[b], FROM + 4 * q + k // 2)
                        if k < 2:
                            pe.wait_ge(hid_copied[b], FROM + Q * q)
                        for t in range(SL):
                            last = nc.tensor.matmul(pt[b][:, 0:Q * CAP_L], h2[:, CT + t, k * P:(k + 1) * P], sel_l[:, t].rearrange("p e j -> p (e j)"),
                                                    start=t == 0, stop=t == SL - 1)
                        if ctx_too:
                            for t in range(CT):
                                last = nc.tensor.matmul(pt[b][:, 256:256 + Q * CAP_C], h2[:, t, k * P:(k + 1) * P], sel_c[:, t].rearrange("p e j -> p (e j)"),
                                                        start=t == 0, stop=t == CT - 1)
                        last.then_inc(gathered[b], 1)

                def turn_put(q):
                    pe.wait_ge(weighted, FROM + q + 1)
                    for f in range(2):
                        pe.wait_ge(silued[f], FROM + Q * q)
                    for pr in range(2):
                        for t in range(SL):
                            last = nc.tensor.transpose(pg[pr][:, t * P:(t + 1) * P], sw_l[:, t, 2 * pr:2 * pr + 2, :].rearrange("p e j -> p (e j)"), K.c("ident"))
                        last.then_inc(put_turned, 1)
                    if ctx_too:
                        pe.wait_ge(hidden[0], FROM + Q * q)
                        for t in range(CT):
                            last = nc.tensor.transpose(pu[0][:, t * P:(t + 1) * P], sw_c[:, t].rearrange("p e j -> p (e j)"), K.c("ident"))
                        last.then_inc(put_turned, 1)

                def gate_up(q, e):
                    n = Q * q + e
                    if e == 0:
                        for b in range(2):
                            pe.wait_ge(xs_copied[b], FROM + 4 * q + 4)
                        pe.wait_ge(put_copied, FROM + NPUT * q + NPUT)
                    for f in range(2):
                        for m, (bank, done, used) in enumerate(((pg, gated, silued), (pu, upped, hidden))):
                            s = 2 * f + m
                            pe.wait_ge(w_ready[s], 16 * n + 16)
                            pe.wait_ge(used[f], FROM + n)
                            for k in range(KD):
                                last = nc.tensor.matmul(bank[f][0:NS, :], xs[:, k, e, :], views[s][:, k, :], start=k == 0, stop=k == KD - 1)
                            last.then_inc(done[f], 1)
                            if s == 2:
                                turn_hidden(q, e, 0)

                def turn_hidden(q, e, f):
                    n = Q * q + e
                    pe.wait_ge(hidden[f], FROM + n + 1)
                    if not (e == 0):
                        pe.wait_ge(hid_copied[f], FROM + n)
                    else:
                        pe.wait_ge(xs_copied[f], FROM + 4 * q + 4)
                    for c in range(4):
                        last = nc.tensor.transpose(pt[f][:, c * NR:(c + 1) * NR], hid[f][:, c * P:(c + 1) * P], K.c("ident")[0:NR, 0:NR])
                    last.then_inc(turned[f], 1)

                def down(q, e):
                    n = Q * q + e
                    for f in range(2):
                        pe.wait_ge(hid_copied[f], FROM + n + 1)
                        pe.wait_ge(w_ready[4 + f], 16 * n + 16)
                        if f == 0:
                            for b in range(2):
                                pe.wait_ge(out_copied[b], FROM + n)
                                pe.wait_ge(added[b], FROM + (NB * q + (4 if e >= 2 else 0)))
                        for b in range(2):
                            for c in range(4):
                                last = nc.tensor.matmul(pd[b][0:NS, :], hidT[f][:, c, :], views[4 + f][:, c, b * 512:(b + 1) * 512],
                                                        start=f == 0 and c == 0, stop=f == 1 and c == 3)
                            if f == 0 and b == 0:
                                turn_hidden(q, e, 1)
                        last.then_inc(downed[f], 1)

                def spread_out(q, part):
                    n = Q * q + (2, 4, 4)[part]
                    for b in range(2):
                        pe.wait_ge(out_copied[b], FROM + n)
                    for k in range(KD):
                        b = k % 2
                        pe.wait_ge(added[b], FROM + NB * q + 4 * part + k // 2)
                        if part < 2:
                            last = nc.tensor.matmul(pd[b][:], out_l[:, k * P:(k + 1) * P], put_l[:, part, :], start=True, stop=True)
                        else:
                            last = nc.tensor.matmul(pd[b][:, 0:CTX], out_c[:, k * P:(k + 1) * P], put_c[:], start=True, stop=True)
                        last.then_inc(spread[b], 1)

                def four(q, more):
                    turn_put(q)
                    for e in range(Q):
                        gate_up(q, e)
                        if e == 2:
                            spread_out(q, 0)
                        down(q, e)
                    if more:
                        gather(q + 1)
                    spread_out(q, 1)
                    if ctx_too:
                        spread_out(q, 2)

                gather(0)
                fours(pe, four)

            @block.scalar
            def _(act):
                def copy_xs(q):
                    for k in range(0, KD, 2):
                        act.wait_ge(gathered[0], FROM + 4 * q + k // 2 + 1)
                        if k == 0:
                            act.wait_ge(upped[1], FROM + Q * q)
                        last = nc.scalar.activation(xs[:, k, :, 0:CAP_L], pt[0][:, 0:Q * CAP_L].rearrange("p (e j) -> p e j", e=Q), ACT.Copy)
                        if ctx_too:
                            last = nc.scalar.activation(xs[:, k, :, CAP_L:NS], pt[0][:, 256:256 + Q * CAP_C].rearrange("p (e j) -> p e j", e=Q), ACT.Copy)
                        last.then_inc(xs_copied[0], 1)

                def copy_out(q, e):
                    n = Q * q + e
                    act.wait_ge(downed[1], FROM + n + 1)
                    act.wait_ge(spread[1], FROM + (NB * q + (4 if e >= 2 else 0)))
                    row = CAP_L * (e % 2)
                    last = nc.scalar.activation(out_l[row:row + CAP_L, 0:512], pd[0][0:CAP_L, :], ACT.Copy)
                    if ctx_too:
                        last = nc.scalar.activation(out_c[CAP_C * e:CAP_C * e + CAP_C, 0:512], pd[0][CAP_L:NS, :], ACT.Copy)
                    last.then_inc(out_copied[0], 1)

                def four(q, more):
                    for pr in range(2):
                        act.wait_ge(put_turned, FROM + NPUT * q + pr + 1)
                        act.wait_ge(spread[1], FROM + NB * q)
                        nc.scalar.activation(put_l[:, pr, :], pg[pr][:], ACT.Copy).then_inc(put_copied, 1)
                    if ctx_too:
                        act.wait_ge(put_turned, FROM + NPUT * q + 3)
                        nc.scalar.activation(put_c[:], pu[0][:, 0:CTX], ACT.Copy).then_inc(put_copied, 1)
                    for e in range(Q):
                        n = Q * q + e
                        for f in range(2):
                            act.wait_ge(gated[f], FROM + n + 1)
                            act.wait_ge(hidden[f], FROM + n)
                            nc.scalar.activation(sg[f][:], pg[f][0:NS, :], ACT.Silu).then_inc(silued[f], 1)
                        act.wait_ge(turned[0], FROM + n + 1)
                        act.wait_ge(downed[0], FROM + n)
                        nc.scalar.activation(hidT[0][:], pt[0][:, 0:4 * NR].rearrange("p (c j) -> p c j", c=4)[:, :, 0:NS], ACT.Copy).then_inc(hid_copied[0], 1)
                        copy_out(q, e)
                    if more:
                        copy_xs(q + 1)

                copy_xs(0)
                fours(act, four)

            @block.vector
            def _(dve):
                def select(q):
                    dve.wait_ge(gathered[1], FROM + 4 * q)
                    kinds = [(sel_l, sw_l, CT, SL, CAP_L)] + ([(sel_c, sw_c, 0, CT, CAP_C)] if ctx_too else [])
                    for sel, sw, t0, nt, cap in kinds:
                        for t in range(nt):
                            place = slot[:, t0 + t, bass.ds(Q * q, Q)].unsqueeze(2).broadcast_to([P, Q, cap])
                            last = nc.vector.tensor_tensor(sel[:, t], K.c("iota", cap).unsqueeze(1).broadcast_to([P, Q, cap]), place, ALU.is_equal)
                    last.then_inc(selected, 1)
                    dve.wait_ge(selected, FROM + q + 1)
                    dve.wait_ge(put_turned, FROM + NPUT * q)
                    for sel, sw, t0, nt, cap in kinds:
                        for t in range(nt):
                            a = aff[:, t0 + t, bass.ds(Q * q, Q)].unsqueeze(2).broadcast_to([P, Q, cap])
                            last = nc.vector.tensor_tensor(sw[:, t], sel[:, t], a, ALU.mult)
                    last.then_inc(weighted, 1)

                def copy_xs(q):
                    for k in range(1, KD, 2):
                        dve.wait_ge(gathered[1], FROM + 4 * q + k // 2 + 1)
                        if k == 1:
                            dve.wait_ge(upped[1], FROM + Q * q)
                        last = nc.vector.tensor_copy(xs[:, k, :, 0:CAP_L], pt[1][:, 0:Q * CAP_L].rearrange("p (e j) -> p e j", e=Q))
                        if ctx_too:
                            last = nc.vector.tensor_copy(xs[:, k, :, CAP_L:NS], pt[1][:, 256:256 + Q * CAP_C].rearrange("p (e j) -> p e j", e=Q))
                        last.then_inc(xs_copied[1], 1)

                def add(q, part):
                    for k in range(KD):
                        b = k % 2
                        dve.wait_ge(spread[b], FROM + NB * q + 4 * part + k // 2 + 1)
                        dve.wait_ge(added[b], FROM + NB * q + 4 * part + k // 2)
                        s, r, n = (0, LATR, LAT) if part < 2 else (1, CTXR, CTX)
                        nc.vector.scalar_tensor_tensor(out=x[:, k, r], in0=pd[b][:, 0:n], scalar=K.m(s, layer, 5, k), in1=x[:, k, r],
                                                       op0=ALU.mult, op1=ALU.add).then_inc(added[b], 1)

                def multiply(q, e):
                    n = Q * q + e
                    for f in range(2):
                        dve.wait_ge(silued[f], FROM + n + 1)
                        dve.wait_ge(upped[f], FROM + n + 1)
                        dve.wait_ge(turned[f], FROM + n)
                        nc.vector.tensor_tensor(hid[f][0:NS, :], sg[f][:], pu[f][0:NS, :], ALU.mult).then_inc(hidden[f], 1)

                def finish(q, e):
                    n = Q * q + e
                    dve.wait_ge(turned[1], FROM + n + 1)
                    dve.wait_ge(downed[1], FROM + n)
                    nc.vector.tensor_copy(hidT[1][:], pt[1][:, 0:4 * NR].rearrange("p (c j) -> p c j", c=4)[:, :, 0:NS]).then_inc(hid_copied[1], 1)
                    dve.wait_ge(downed[1], FROM + n + 1)
                    row = CAP_L * (e % 2)
                    dve.wait_ge(spread[1], FROM + (NB * q + (4 if e >= 2 else 0)))
                    last = nc.vector.tensor_copy(out_l[row:row + CAP_L, 512:D], pd[1][0:CAP_L, :])
                    if ctx_too:
                        last = nc.vector.tensor_copy(out_c[CAP_C * e:CAP_C * e + CAP_C, 512:D], pd[1][CAP_L:NS, :])
                    last.then_inc(out_copied[1], 1)

                if NR > NS:
                    for f in range(2):
                        nc.vector.memset(hid[f][NS:NR, :], 0.0).then_inc(padded, 1)
                    dve.wait_ge(padded, FROM + 2)
                def four(q, more):
                    for e in range(Q):
                        multiply(q, e)
                        if e == 2:
                            add(q, 0)
                        finish(q, e)
                        if e == 1 and more:
                            select(q + 1)
                    if more:
                        copy_xs(q + 1)
                    add(q, 1)
                    if ctx_too:
                        add(q, 2)

                select(0)
                copy_xs(0)
                fours(dve, four)


def mixture(K, A, layer):
    with ExitStack() as ctx:
        tag = f"moe{layer}"
        w = [K.sb(f"{tag}x_w{s}", [P, 4096], ctx) for s in range(6)]
        w_ready = [K.sem(f"{tag}x_w_ready{s}") for s in range(6)]
        views = [w[s][:].rearrange("p (k n) -> p k n", n=512) for s in range(4)] + \
                [w[s][:].rearrange("p (k n) -> p k n", n=D) for s in (4, 5)]
        gate_w, up_w, down_w = (A["moe_" + n][layer] for n in ("gate", "up", "down"))

        def load(sp, n, s):
            m = (down_w if s >= 4 else (gate_w, up_w)[s % 2])[bass.ds(n, 1)]
            rows = m.rearrange("o (k p) f -> (o p) k f", p=P)
            src = rows[:, 4 * (s - 4):4 * (s - 4) + 4, :] if s >= 4 else rows[:, :, 512 * (s // 2):512 * (s // 2) + 512]
            sp.dma_start(views[s], src).then_inc(w_ready[s], 16)

        norm(K, tag + "n", layer, 1, ahead=lambda sp: [load(sp, 0, s) for s in range(3)])
        h2 = K.sb(f"{tag}_h2", [P, NT, D], ctx)
        slot = K.sb(f"{tag}_slot", [P, NT, E], ctx)
        aff = K.sb(f"{tag}_aff", [P, NT, E], ctx)
        route(K, A, tag + "r", layer, h2, slot, aff, ahead=lambda sp: [load(sp, 0, s) for s in range(3, 6)])
        experts(K, A, tag + "x", layer, h2, slot, aff, load, views, w_ready)


def mix_and_project(K, A, scr, hid):
    nc, h = K.nc, K.h
    JOBS = (("k", 2), ("v", 3), ("r", 0), ("w1", 1), ("a1", 4), ("g1", 5))
    LORA_F = {"w1": ACT.Tanh, "a1": ACT.Copy, "g1": ACT.Sigmoid}
    with ExitStack() as ctx:
        xx = K.sb("mp_xx", [P, KD, TOK], ctx)
        mix = [K.sb(f"mp_mix{j}", [P, KD, TOK], ctx) for j in range(2)]
        w = [K.sb(f"mp_w{j}", [P, KD, P], ctx) for j in range(2)]
        lw = [K.sb(f"mp_lw{n}", [P, KD, P], ctx) for n in range(3)]
        st = [K.sb(f"mp_st{j}", [P, TOK], ctx) for j in range(2)]
        ps = [K.ps(f"mp_p{j}", [P, 1024], ctx) for j in range(2)]
        w_ready = [K.sem(f"mp_w_ready{j}") for j in range(2)]
        prod = [K.sem(f"mp_product{j}") for j in range(2)]
        copied = [K.sem(f"mp_copied{j}") for j in range(2)]
        stored = [K.sem(f"mp_stored{j}") for j in range(2)]
        spilled = K.sem("mp_x_stored")
        lora_ready, edges, neighbours, mixed, lora = (K.sem(f"mp_{n}") for n in ("lora_ready", "edges", "neighbours", "mixed", "lora"))
        spans = ((LATR, slice(0, LAT)), (CTXR, slice(512, 512 + CTX)))
        n_it = KD // 2
        with nc.Block() as block:
            @block.sync
            def _(sp):
                for n, (name, _) in enumerate(JOBS[3:]):
                    sp.dma_start(lw[n][:], A[name]).then_inc(lora_ready, 16)
                sp.dma_start(scr["x"], K.x[:]).then_inc(spilled, 16)
                for m, (name, _) in enumerate(JOBS[:3]):
                    with sp.Fori(0, n_it) as i:
                        for j in range(2):
                            sp.wait_ge(prod[j], FROM + i + m * n_it)
                            sp.dma_start(w[j][:], A["rw_" + name][bass.ds(2 * i + j, 1)].rearrange("o p k n -> (o p) k n")
                                         ).then_inc(w_ready[j], 16)

            @block.gpsimd
            def _(pool):
                for r in (CTXR, LATR):
                    lo, hi = r.start, r.stop
                    nc.gpsimd.tensor_copy(xx[:, :, lo:lo + 1], h[:, :, lo + 1:lo + 2]).then_inc(edges, 1)
                    nc.gpsimd.tensor_copy(xx[:, :, hi - 1:hi], h[:, :, hi - 2:hi - 1]).then_inc(edges, 1)

            @block.vector
            def _(dve):
                for k in range(KD):
                    for r in (CTXR, LATR):
                        lo, hi = r.start, r.stop
                        nc.vector.tensor_tensor(xx[:, k, lo + 1:hi - 1], h[:, k, lo:hi - 2], h[:, k, lo + 2:hi], ALU.add).then_inc(neighbours, 1)
                    if k == 0:
                        dve.wait_ge(edges, FROM + 4)
                    dve.wait_ge(neighbours, FROM + 3 * k + 2)
                    nc.vector.scalar_tensor_tensor(out=xx[:, k, :], in0=xx[:, k, :], scalar=0.5, in1=h[:, k, :],
                                                   op0=ALU.mult, op1=ALU.subtract).then_inc(neighbours, 1)
                    dve.wait_ge(neighbours, FROM + 3 * k + 3)
                    nc.vector.scalar_tensor_tensor(out=mix[0][:, k, :], in0=xx[:, k, :], scalar=K.v("mu", JOBS[0][1] * KD + k),
                                                   in1=h[:, k, :], op0=ALU.mult, op1=ALU.add).then_inc(mixed, 1)
                for m, (name, row) in enumerate(JOBS):
                    if m == 0:
                        continue
                    if m >= 2 and m <= 4:
                        for j in range(2):
                            dve.wait_ge(prod[j], FROM + (m - 1) * n_it)
                    elif m == 5:
                        dve.wait_ge(lora, FROM + 1)
                    for k in range(KD):
                        nc.vector.scalar_tensor_tensor(out=mix[m % 2][:, k, :], in0=xx[:, k, :], scalar=K.v("mu", row * KD + k),
                                                       in1=h[:, k, :], op0=ALU.mult, op1=ALU.add).then_inc(mixed, 1)

            @block.tensor
            def _(pe):
                for m, (name, _) in enumerate(JOBS[:3]):
                    with pe.Fori(0, n_it) as i:
                        for j in range(2):
                            pe.wait_ge(w_ready[j], 16 * i + 16 * (m * n_it + 1))
                            pe.wait_ge(copied[j], FROM + i + m * n_it)
                            for r, b in spans:
                                for k in range(KD):
                                    if r is LATR:
                                        pe.wait_ge(mixed, FROM + KD * m + k + 1)
                                    last = nc.tensor.matmul(ps[j][:, b], w[j][:, k, :], mix[m % 2][:, k, r], start=k == 0, stop=k == KD - 1)
                            last.then_inc(prod[j], 1)
                pe.wait_ge(lora_ready, 48)
                for n, (name, _) in enumerate(JOBS[3:]):
                    m = 3 + n
                    pe.wait_ge(mixed, FROM + KD * (m + 1))
                    pe.wait_ge(copied[n % 2], FROM + 3 * n_it + n // 2)
                    for r, b in spans[0:1 if name == "g1" else 2]:
                        for k in range(KD):
                            last = nc.tensor.matmul(ps[n % 2][:, b], lw[n][:, k, :], mix[m % 2][:, k, r], start=k == 0, stop=k == KD - 1)
                    last.then_inc(lora, 1)

            @block.scalar
            def _(act):
                for m, (name, _) in enumerate(JOBS[:3]):
                    with act.Fori(0, n_it) as i:
                        for j in range(2):
                            act.wait_ge(prod[j], FROM + i + (m * n_it + 1))
                            for r, b in spans:
                                last = nc.scalar.activation(st[j][:, r], ps[j][:, b], ACT.Copy)
                            last.then_inc(copied[j], 1)
                            act.wait_ge(copied[j], FROM + i + (m * n_it + 1))
                            act.dma_start(scr[name][bass.ds(2 * i + j, 1)].rearrange("o p t -> (o p) t"), st[j][:]
                                          ).then_inc(stored[j], 16)
                        for j in range(2):
                            act.wait_ge(stored[j], 16 * i + 16 * (m * n_it + 1))
                for n, (name, _) in enumerate(JOBS[3:]):
                    act.wait_ge(lora, FROM + n + 1)
                    for r, b in spans[0:1 if name == "g1" else 2]:
                        to = hid[name][:] if name == "g1" else hid[name][:, r]
                        last = nc.scalar.activation(to, ps[n % 2][:, b], LORA_F[name])
                    last.then_inc(copied[n % 2], 1)
                for j in range(2):
                    act.wait_ge(stored[j], 16 * 3 * n_it)
                act.wait_ge(spilled, 16)


def rwkv(K, A, scr, hid, o):
    nc = K.nc
    NEG = -float(np.exp(np.float32(-0.5)))
    NC = TOK // CH
    LV = len(LEVELS)
    QUADS = range(3)
    n_it = KD
    GROUPS_T = [(lv, st, q) for lv in range(LV) for st in range(3) for q in QUADS]
    NG = len(GROUPS_T)

    def side(d, scan, feats, readout):
        after = [[] for _ in range(NG)]
        if readout:
            for m, name in enumerate(READOUT):
                after[1 + 2 * m].append((name, 0))
        if scan:
            for n in range(NC):
                after[int(3.6 * n)].append(("z", n))
                if n < NC - 1:
                    after[int(3.6 * n + 1.3)].append(("s", n))
        if feats:
            names = FEATS if d == 1 else [f for f in FEATS if f not in FEATS_HP]
            for m, name in enumerate(names):
                after[(m * 41) // len(names) + 2].append((name, 0))
        return after

    KK_REC = ["kk_rec0", "kk_rec1", "kk_rec2"]
    FEATS = ["kk_raw", "kk_sum", "kk_root"] + KK_REC + ["kk", "decay_in", "rate_in", "log_decay", "cumsum", "kd_half", "exp_L", "kd",
             "exp_Lx", "b", "exp_-L", "zr0", "zr1", "hats", "keep_kd", "zr2", "zr3"]
    FEATS_HP = FEATS[:7]
    READOUT = ["bonus", "gn_mean", "gn_var", "gn_norm", "y_back", "gate", "keep"]

    with ExitStack() as ctx:
        sb = lambda n, s: K.sb("rk_" + n, s, ctx)
        xm = K.x[:].rearrange("p k t -> p (k t)")
        zr = xm[:, 0:4 * TOK].rearrange("p (m t) -> p m t", m=4)
        Zz = xm[:, 4 * TOK:6 * TOK].rearrange("p (t h c) -> p t h c", t=NT, h=2)
        S = xm[:, 6 * TOK:6 * TOK + NC * P].rearrange("p (n c) -> p n c", c=P)
        spare = K.h[:].rearrange("p k t -> p (k t)")[:, KD * LAT:KD * TOK]
        U = spare[:, 0:TOK].rearrange("p (t c) -> p t c", c=P)
        TKT = spare[:, TOK:2 * TOK]
        Y = spare[:, 2 * TOK:2 * TOK + LAT].rearrange("p (t c) -> p t c", c=P)
        kT, rT = sb("k", [P, TOK]), sb("r", [P, LAT])
        vT = sb("v", [P, LAT])
        w2z = [sb(f"w2z{d}", [P, P]) for d in range(2)]
        a2z = [sb(f"a2z{d}", [P, P]) for d in range(2)]
        g2c = sb("g2c", [P, P])
        kk, sq, ms = sb("kk", [P, TOK]), sb("sq", [P, TOK]), sb("ms", [P, TOK])
        lw, L, aa, kd, eL = (sb(n, [P, TOK]) for n in ("lw", "L", "a", "kd", "eL"))
        b, Lx, emL, Bh, kh = sq, ms, L, lw, aa
        kds, bonus_in = sb("kds", [P, LAT]), sb("bonus_in", [P, LAT])
        Rt = [sb(f"Rt{j}", [P, LAT]) for j in range(2)]
        pc = [sb(f"pc{j}", [P, NC]) for j in range(2)]
        Bt, kt = sb("Bt", [P, TOK]), sb("kt", [P, TOK])
        Kz = sb("Kz", [P, NT, 2, P])
        AVz = Kz
        BKz = [sb(f"BKz{j}", [P, NT, 2, 2, P]) for j in range(2)]
        Vz = sb("Vz", [P, NT, 2, P])
        NA = sb("NA", [P, NT, 2, 2, P])
        QQ = [sb(f"Q{j}", [P, LAT // P, 2, 2, P]) for j in range(2)]
        A4, W4, TT4 = ([sb(f"{n}{q}", [P, 4, P]) for q in QUADS] for n in ("A4_", "W4_", "T4_"))
        aw = sb("AW", [P, len(QUADS) * 4, P])
        Y4 = [aw[:, 4 * q:4 * q + 4, :] for q in QUADS]
        vN = aw[:].rearrange("p m c -> p (m c)")[:, 0:TOK]
        stat = sb("stat", [P, 4, 8])
        bank = [K.ps(f"rk_b{n}", [P, 512], ctx) for n in range(8)]
        sem = lambda n: K.sem("rk_" + n)
        loaded, v_loaded, g_loaded, kk_made = sem("loaded"), sem("v_loaded"), sem("g_loaded"), sem("kk_made")
        kk_raw, kk_sq, kk_sum, kk_max, kk_root, kk_rec = (sem(n) for n in ("kk_raw", "kk_square", "kk_sum", "kk_max", "kk_root", "kk_rec"))
        v_turned, vz_made, vt_loaded, bonus_kept = (sem(n) for n in ("v_turned", "vz_made", "vt_loaded", "bonus_kept"))
        bonus, bonus_v, centred, gn_sum, gn_var, gn_root, normed, y_back, y_scaled, gate, out_made = (sem(n) for n in (
            "bonus", "bonus_v", "centred", "gn_sum", "gn_var", "gn_root", "normed", "y_turned", "y_scaled", "gate", "out_made"))
        gn_chain, zeroed, kds_half = sem("gn_steps"), sem("zeroed"), sem("kds_half")
        low, sig, scaled_lw, cum, lx, kd_half, kd_made, b_made, exps, zr_made, kds_made, hats, kept = (sem(n) for n in (
            "low_rank", "sigmoids", "log_decay", "cumsum", "exclusive", "kd_half", "kd_made", "b_made", "exps", "zr_made", "kds_made",
            "hats", "unit_kept"))
        turned_tok, tok_copied, aq, masked, n_turned, a_copied, w_first = (sem(n) for n in (
            "tokens_turned", "tokens_copied", "causal_products", "masked", "n_turned", "a_copied", "w_first"))
        w_turned, t_copied, y_prod, y_masked, w_prod, w_added = (sem(n) for n in (
            "w_turned", "t_copied", "aw_product", "aw_masked", "w_product", "w_added"))
        av, av_copied, utk, u_copied, tk_copied = (sem(n) for n in ("av", "av_copied", "u_and_tk", "u_copied", "tk_copied"))
        z_prod, z_added, s_prod, s_next, y_out, y_added = (sem(n) for n in (
            "z_product", "z_added", "s_product", "s_next", "y_out", "y_added"))
        diag = lambda ap: ap.rearrange("p h (a j) -> p (h a) j", j=NH)[:, 0:4:3, :]
        m4 = lambda t: t[:].rearrange("p (m c) -> p m c", c=P)
        spans = ((LATR, 0), (CTXR, 1))
        order = [list(range(NC)), list(range(CTX // CH))[::-1] + list(range(CTX // CH, NC))[::-1]]
        chunk_end = lambda d: CH - 1 if d == 0 else 0
        rows_of = lambda c: slice(CH * (c % 2), CH * (c % 2) + CH)

        def col(name, i, at=0):
            return K.vec[:, bass.ds(i + (VEC[name] + at), 1)]

        def run(eng, start, group, after, tail, loop):
            for name in FEATS:
                after(name, 0, 0, 0)

            def unit(i, d, scan=True, feats=True):
                start(i, d)
                readout = d == 1 and not (isinstance(i, int) and i == 0)
                plan = side(d, scan, feats, readout)
                for g, what in zip(GROUPS_T, plan):
                    group(i, d, *g)
                    for name, n in what:
                        if name in ("z", "s"):
                            after(name, i if d else i - 1, 1 - d, n)
                        elif name in READOUT:
                            after(name, i - 1, 0, 0)
                        else:
                            after(name, i + d, 1 - d, 0)
                tail(i, d, scan)

            unit(0, 0, scan=False)
            unit(0, 1)
            with loop(1, n_it - 1) as i:
                unit(i, 0)
                unit(i, 1)
            last = n_it - 1
            unit(last, 0)
            unit(last, 1, feats=False)
            for n in range(NC):
                after("z", last, 1, n)
                if n < NC - 1:
                    after("s", last, 1, n)
            after("y", last, 1, 0)
            for name in READOUT:
                if name != "keep":
                    after(name, last, 0, 0)

        with nc.Block() as block:
            @block.sync
            def _(sp):
                def load(i):
                    one = lambda t: t[bass.ds(i, 1)].rearrange("o p t -> (o p) t")
                    sp.dma_start(kT[:], one(scr["k"])).then_inc(loaded, 16)
                    sp.dma_start(rT[:], one(scr["r"])[:, LATR]).then_inc(loaded, 16)
                    for d in range(2):
                        sp.dma_start(w2z[d][64 * d:64 * d + 64, :], one(A["w2"])[64 * d:64 * d + 64, :]).then_inc(loaded, 16)
                        sp.dma_start(a2z[d][64 * d:64 * d + 64, :], one(A["a2"])[64 * d:64 * d + 64, :]).then_inc(loaded, 16)

                def load_g(i):
                    sp.dma_start(g2c[:], A["g2"][bass.ds(i, 1)].rearrange("o p t -> (o p) t")).then_inc(g_loaded, 16)

                def load_vt(i):
                    sp.dma_start(vT[:], scr["v"][bass.ds(i, 1)].rearrange("o p t -> (o p) t")[:, LATR]).then_inc(vt_loaded, 16)

                def load_v(i):
                    sp.wait_ge(w_prod, FROM + 3 * LV * (2 * i + 1))
                    sp.dma_start(vN, scr["v"][bass.ds(i, 1)].rearrange("o p t -> (o p) t")).then_inc(v_loaded, 16)

                def load_next(i):
                    sp.wait_ge(kd_made, FROM + 2 * i)
                    sp.wait_ge(zr_made, FROM + 8 * i)
                    sp.wait_ge(kds_made, FROM + 2 * i)
                    sp.wait_ge(low, FROM + 4 * i)
                    load(i)

                sp.wait_ge(zeroed, FROM + 4)
                load(0)
                load_g(0)
                load_vt(0)
                load_v(0)
                load_next(1)
                load_v(1)
                with sp.Fori(2, n_it) as i:
                    load_next(i)
                    sp.wait_ge(y_scaled, FROM + 2 * i - 2)
                    load_vt(i - 1)
                    sp.wait_ge(gate, FROM + i - 1)
                    load_g(i - 1)
                    load_v(i)
                sp.wait_ge(y_scaled, FROM + 2 * n_it - 2)
                load_vt(n_it - 1)
                sp.wait_ge(gate, FROM + n_it - 1)
                load_g(n_it - 1)

            @block.gpsimd
            def _(pool):
                for d in range(2):
                    nc.gpsimd.memset(w2z[d][:], 0.0).then_inc(zeroed, 1)
                    nc.gpsimd.memset(a2z[d][:], 0.0).then_inc(zeroed, 1)
                nc.gpsimd.memset(Vz[:], 0.0).then_inc(zeroed, 1)
                nc.gpsimd.memset(Zz, 0.0).then_inc(zeroed, 1)
                nc.gpsimd.memset(S, 0.0).then_inc(zeroed, 1)
                ends = lambda t, d: t[:].rearrange("p (c j) -> p c j", j=CH)[:, :, chunk_end(d):chunk_end(d) + 1]

                def start(i, d):
                    u = 2 * i + d
                    pool.wait_ge(zr_made, FROM + 4 * u + 4)
                    pool.wait_ge(exps, FROM + 3 * u + 3)
                    if not (isinstance(u, int) and u < 2):
                        pool.wait_ge(y_out, FROM + u - 1)
                        pool.wait_ge(s_next, FROM + (NC - 1) * (u - 1))
                    nc.gpsimd.tensor_tensor(Rt[d][:], zr[:, 2, LATR], zr[:, 3, LATR], ALU.add).then_inc(kept, 1)
                    nc.gpsimd.tensor_copy(pc[d][:].unsqueeze(2), ends(eL, d)).then_inc(kept, 1)

                def after(name, i, d, n):
                    u = 2 * i + d
                    if name == "exp_L":
                        pool.wait_ge(cum, FROM + u + 1)
                        pool.wait_ge(scaled_lw, FROM + u + 1)
                        if d == 0:
                            pool.wait_ge(kk_rec, FROM + 3 * i + 3)
                        if not (isinstance(u, int) and u == 0):
                            pool.wait_ge(zr_made, FROM + 4 * u)
                        nc.gpsimd.tensor_tensor(Lx[:], L[:], lw[:], ALU.subtract).then_inc(lx, 1)
                    elif name == "keep_kd" and d == 1:
                        pool.wait_ge(kd_made, FROM + u + 1)
                        pool.wait_ge(kds_made, FROM + u)
                        nc.gpsimd.tensor_tensor(kds[:], kds[:], kd[:, LATR], ALU.add).then_inc(kds_half, 1)
                    elif name == "hats":
                        pool.wait_ge(exps, FROM + 3 * u + 3)
                        pool.wait_ge(b_made, FROM + u + 1)
                        if not (isinstance(u, int) and u == 0):
                            pool.wait_ge(aq, FROM + 2 * NT * u)
                        nc.gpsimd.tensor_tensor(Bt[:], b[:], emL[:], ALU.mult).then_inc(hats, 1)
                        nc.gpsimd.tensor_tensor(kt[:], kd[:], emL[:], ALU.mult).then_inc(hats, 1)
                        pool.wait_ge(hats, FROM + 4 * u + 2)
                        whole = ends(eL, d).broadcast_to([P, NC, CH])
                        cj = lambda t: t[:].rearrange("p (c j) -> p c j", j=CH)
                        nc.gpsimd.tensor_tensor(cj(Bh), cj(Bt), whole, ALU.mult).then_inc(hats, 1)
                        nc.gpsimd.tensor_tensor(cj(kh), cj(kt), whole, ALU.mult).then_inc(hats, 1)

                run(pool, start, lambda *a: None, after, lambda *a: None, pool.Fori)

            @block.scalar
            def _(act):
                def start(i, d):
                    u = 2 * i + d
                    if isinstance(u, int) and u == 1:
                        act.wait_ge(kds_made, FROM + 2)
                        nc.scalar.activation(bonus_in[:], kds[:], ACT.Copy).then_inc(bonus_kept, 1)
                    for t in range(NT):
                        act.wait_ge(turned_tok, FROM + NT * u + t + 1)
                        if t == 0 and not (isinstance(u, int) and u < 2):
                            act.wait_ge(s_prod, FROM + (NC - 1) * (u - 1))
                        j = 2 * (t % 2)
                        nc.scalar.activation(Kz[:, t, :, :], bank[j][:, 0:2 * P].rearrange("p (h c) -> p h c", h=2), ACT.Copy)
                        for half in range(2):
                            last = nc.scalar.activation(BKz[d][:, t, half, :, :], bank[j + 1][:, 0:2 * P].rearrange("p (m c) -> p m c", m=2),
                                                        ACT.Copy, scale=K.c("half", 1, half))
                        last.then_inc(tok_copied, 1)
                    for q in QUADS:
                        act.wait_ge(n_turned, FROM + 3 * u + q + 1)
                        nc.scalar.activation(A4[q][:], m4(bank[q]), ACT.Copy).then_inc(a_copied, 1)

                def group(i, d, lv, st, q):
                    if st == 0:
                        u = 2 * i + d
                        act.wait_ge(w_turned, FROM + 3 * (LV * u + lv) + q + 1)
                        nc.scalar.activation(TT4[q][:], m4(bank[q]), ACT.Copy).then_inc(t_copied, 1)

                def after(name, i, d, n):
                    u = 2 * i + d
                    first = isinstance(u, int) and u == 0
                    if name == "kk_raw":
                        act.wait_ge(kk_raw, FROM + i + 1)
                        if not first:
                            act.wait_ge(hats, FROM + 4 * u)
                        nc.scalar.activation(sq[:], kk[:], ACT.Square).then_inc(kk_sq, 1)
                    elif name == "kk_root":
                        act.wait_ge(kk_max, FROM + 2 * i + 2)
                        nc.scalar.activation(ms[:], ms[:], ACT.Sqrt).then_inc(kk_root, 1)
                    elif name == "decay_in":
                        act.wait_ge(low, FROM + 2 * u + 1)
                        if not first:
                            act.wait_ge(turned_tok, FROM + NT * u)
                        for r, m in spans:
                            nc.scalar.activation(lw[:, r], bank[3 + m][:, 0:r.stop - r.start], ACT.Sigmoid, bias=col("w0", i, KD * d)).then_inc(sig, 1)
                    elif name == "rate_in":
                        act.wait_ge(low, FROM + 2 * u + 2)
                        for r, m in spans:
                            nc.scalar.activation(aa[:, r], bank[3 + m][:, 0:r.stop - r.start], ACT.Sigmoid, bias=col("a0", i, KD * d)).then_inc(sig, 1)
                    elif name == "exp_L":
                        act.wait_ge(cum, FROM + u + 1)
                        if not first:
                            act.wait_ge(kept, FROM + 2 * u)
                            act.wait_ge(hats, FROM + 4 * u)
                        if d == 0:
                            act.wait_ge(kk_made, FROM + i + 1)
                        nc.scalar.activation(eL[:], L[:], ACT.Exp).then_inc(exps, 1)
                    elif name == "exp_Lx":
                        act.wait_ge(lx, FROM + u + 1)
                        nc.scalar.activation(Lx[:], Lx[:], ACT.Exp).then_inc(exps, 1)
                    elif name == "exp_-L":
                        act.wait_ge(exps, FROM + 3 * u + 1)
                        nc.scalar.activation(emL[:], L[:], ACT.Exp, scale=-1.0).then_inc(exps, 1)
                    elif name == "keep_kd" and d == 0:
                        act.wait_ge(kd_made, FROM + u + 1)
                        if not first:
                            act.wait_ge(bonus_kept, FROM + i)
                        nc.scalar.activation(kds[:], kd[:, LATR], ACT.Copy).then_inc(kds_made, 1)
                    elif name == "keep":
                        act.wait_ge(out_made, FROM + i + 1)
                        act.wait_ge(kds_made, FROM + 2 * i + 4)
                        nc.scalar.activation(bonus_in[:], kds[:], ACT.Copy).then_inc(bonus_kept, 1)
                    elif name == "gn_var":
                        act.wait_ge(gn_var, FROM + i + 1)
                        nc.scalar.activation(stat[:, 3, :], stat[:, 2, :], ACT.Sqrt).then_inc(gn_root, 1)

                def tail(i, d, scan):
                    u = 2 * i + d
                    act.wait_ge(utk, FROM + 2 * u + 1)
                    for n in range(2):
                        w = (4, 2)[n] * P
                        nc.scalar.activation(TKT[:, 4 * P * n:4 * P * n + w], bank[n][:, 0:w], ACT.Copy).then_inc(tk_copied, 1)
                    act.wait_ge(utk, FROM + 2 * u + 2)
                    if scan:
                        act.wait_ge(z_added, FROM + NC * u)
                    for n in range(2):
                        w = (4, 2)[n]
                        nc.scalar.activation(U[:, 4 * n:4 * n + w, :], m4(bank[n])[:, 0:w, :], ACT.Copy).then_inc(u_copied, 1)

                run(act, start, group, after, tail, act.Fori)

            @block.tensor
            def _(pe):
                tile = lambda t: slice(t * P, (t + 1) * P)
                at = lambda q, m: (2 * q + m // 2, m % 2)

                def start(i, d):
                    u = 2 * i + d
                    first = isinstance(u, int) and u == 0
                    pe.wait_ge(zr_made, FROM + 4 * u + 4)
                    pe.wait_ge(hats, FROM + 4 * u + 4)
                    for t in range(NT):
                        if t >= 2:
                            pe.wait_ge(tok_copied, FROM + NT * u + t - 1)
                        elif not first:
                            pe.wait_ge(u_copied if t == 0 else av_copied, FROM + 2 * u)
                        j = 2 * (t % 2)
                        for hh in range(2):
                            nc.tensor.transpose(bank[j][:, hh * P:(hh + 1) * P], zr[:, hh, tile(t)], K.c("ident"))
                        nc.tensor.transpose(bank[j + 1][:, 0:P], Bh[:, tile(t)], K.c("ident"))
                        nc.tensor.transpose(bank[j + 1][:, P:2 * P], kh[:, tile(t)], K.c("ident")).then_inc(turned_tok, 1)
                        if t == 0:
                            if not (isinstance(u, int) and u < 2):
                                pe.wait_ge(y_added, FROM + u - 1)
                            if d == 1:
                                pe.wait_ge(vz_made, FROM + 4 * i + 4)
                        elif t >= 2:
                            pe.wait_ge(masked, FROM + 2 * (NT * u + t - 1))
                        w = 4 if t >= CT else 2
                        for n, m in enumerate((Bt, kt)):
                            nc.tensor.matmul(bank[4 + 2 * (t % 2) + n][:, 0:w * P], m[:, tile(t)], zr[:, 0:w, tile(t)],
                                             start=True, stop=True).then_inc(aq, 1)
                    pe.wait_ge(tok_copied, FROM + NT * u + NT)
                    for q in QUADS:
                        pe.wait_ge(masked, FROM + 2 * (NT * u + 2 * q + 2))
                        for m in range(4):
                            t, hh = at(q, m)
                            last = nc.tensor.transpose(bank[q][:, m * P:(m + 1) * P], NA[:, t, 0, hh, :], K.c("ident"))
                        last.then_inc(n_turned, 1)

                def group(i, d, lv, st, q):
                    u = 2 * i + d
                    k = 3 * (LV * u + lv) + q
                    if st == 0:
                        if lv == 0:
                            pe.wait_ge(w_first, FROM + 6 * u + 2 * q + 2)
                            pe.wait_ge(a_copied, FROM + 3 * u + q + 1)
                        else:
                            pe.wait_ge(w_added, FROM + k - 2)
                        for m in range(4):
                            last = nc.tensor.transpose(bank[q][:, m * P:(m + 1) * P], W4[q][:, m, :], K.c("ident"))
                        last.then_inc(w_turned, 1)
                    elif st == 1:
                        pe.wait_ge(t_copied, FROM + k + 1)
                        for m in range(4):
                            last = nc.tensor.matmul(bank[q][:, m * P:(m + 1) * P], A4[q][:, m, :], W4[q][:, m, :], start=True, stop=True)
                        last.then_inc(y_prod, 1)
                    else:
                        pe.wait_ge(y_masked, FROM + k + 1)
                        for m in range(4):
                            last = nc.tensor.matmul(bank[q][:, m * P:(m + 1) * P], TT4[q][:, m, :], Y4[q][:, m, :], start=True, stop=True)
                        last.then_inc(w_prod, 1)

                def low_rank(i, d, z, name):
                    for r, m in spans:
                        last = nc.tensor.matmul(bank[3 + m][:, 0:r.stop - r.start], z[d][:], hid[name][:, r], start=True, stop=True)
                    last.then_inc(low, 1)

                def after(name, i, d, n):
                    u = 2 * i + d
                    first = isinstance(u, int) and u == 0
                    if name == "kk_sum":
                        pe.wait_ge(kk_sq, FROM + i + 1)
                        for r, m in spans:
                            last = nc.tensor.matmul(bank[3 + m][:, 0:r.stop - r.start], K.c("heads"), sq[:, r], start=True, stop=True)
                        last.then_inc(kk_sum, 1)
                    elif name == "decay_in":
                        if d == 0:
                            pe.wait_ge(kk_max, FROM + 2 * i + 2)
                            pe.wait_ge(loaded, 96 * i + 96)
                        if first:
                            pe.wait_ge(zeroed, FROM + 7)
                        low_rank(i, d, w2z, "w1")
                    elif name == "rate_in":
                        pe.wait_ge(sig, FROM + 4 * u + 2)
                        low_rank(i, d, a2z, "a1")
                    elif name == "z":
                        c = order[d][n]
                        if n == 0:
                            pe.wait_ge(tk_copied, FROM + 2 * u + 2)
                        else:
                            pe.wait_ge(s_next, FROM + (NC - 1) * u + n)
                        nc.tensor.matmul(bank[6][rows_of(c), 0:P], TKT[:, c * CH:(c + 1) * CH], S[:, n, :], start=True, stop=True).then_inc(z_prod, 1)
                        if n < NC - 1:
                            if n == 0:
                                pe.wait_ge(vz_made, FROM + 4 * i + 4)
                            nc.tensor.matmul(bank[7][:, 0:P], BKz[d][:, c // 2, c % 2, 1, :], diag(Vz[:, c // 2]), start=True, stop=False)
                    elif name == "s":
                        c = order[d][n]
                        pe.wait_ge(z_added, FROM + NC * u + n + 1)
                        nc.tensor.matmul(bank[7][:, 0:P], BKz[d][:, c // 2, c % 2, 0, :], diag(Zz[:, c // 2]), start=False, stop=True).then_inc(s_prod, 1)
                    elif name == "y":
                        pe.wait_ge(z_added, FROM + NC * u + NC)
                        pe.wait_ge(kept, FROM + 2 * u + 2)
                        if d == 0 and not first:
                            pe.wait_ge(out_made, FROM + i)
                        elif d == 1:
                            pe.wait_ge(y_added, FROM + u)
                        for t in range(CT, NT):
                            oc = slice((t - CT) * P, (t - CT + 1) * P)
                            for half in range(2):
                                c = 2 * t + half
                                nc.tensor.matmul(bank[5][rows_of(c), oc], Rt[d][:, c * CH - CTX:(c + 1) * CH - CTX], S[:, order[d].index(c), :],
                                                 start=True, stop=False, skip_group_check=True)
                            for hh in range(2):
                                nc.tensor.matmul(bank[5][:, oc], QQ[d][:, t - CT, 0, hh, :], Zz[:, t, hh, :], start=False, stop=False, skip_group_check=True)
                                last = nc.tensor.matmul(bank[5][:, oc], QQ[d][:, t - CT, 1, hh, :], Vz[:, t, hh, :], start=False, stop=hh == 1, skip_group_check=True)
                        last.then_inc(y_out, 1)
                    elif name == "bonus":
                        pe.wait_ge(bonus_kept, FROM + i + 1)
                        pe.wait_ge(y_added, FROM + 2 * i + 2)
                        nc.tensor.matmul(bank[5][:], K.c("heads"), bonus_in[:], start=True, stop=True).then_inc(bonus, 1)
                    elif name == "y_back":
                        pe.wait_ge(normed, FROM + i + 1)
                        pe.wait_ge(bonus_v, FROM + i + 1)
                        for t in range(4):
                            last = nc.tensor.transpose(bank[5][:, t * P:(t + 1) * P], Y[:, t, :], K.c("ident"))
                        last.then_inc(y_back, 1)
                    elif name == "gate":
                        pe.wait_ge(g_loaded, 16 * i + 16)
                        pe.wait_ge(y_scaled, FROM + 2 * i + 1)
                        nc.tensor.matmul(bank[5][:], g2c[:], hid["g1"][:], start=True, stop=True).then_inc(gate, 1)

                def tail(i, d, scan):
                    u = 2 * i + d

                    def av_product():
                        for t in range(NT):
                            for hh in range(2):
                                last = nc.tensor.matmul(bank[6 + t // 4][:, (t % 4) * P:(t % 4 + 1) * P], NA[:, t, 1, hh, :], Vz[:, t, hh, :],
                                                        start=hh == 0, stop=hh == 1)
                        last.then_inc(av, 1)

                    if d == 1:
                        pe.wait_ge(z_added, FROM + NC * u)
                        av_product()
                    pe.wait_ge(w_added, FROM + 3 * LV * (u + 1))
                    for t in range(NT):
                        for hh in range(2):
                            last = nc.tensor.matmul(bank[t // 4][:, (t % 4) * P:(t % 4 + 1) * P], Kz[:, t, hh, :],
                                                    W4[t // 2][:, 2 * (t % 2) + hh, :], start=hh == 0, stop=hh == 1)
                    last.then_inc(utk, 1)
                    if scan:
                        after("y", i if d else i - 1, 1 - d, 0)
                    if d == 0:
                        pe.wait_ge(v_loaded, 16 * i + 16)
                        pe.wait_ge(sig, FROM + 4 * u + 8)
                        if scan:
                            pe.wait_ge(y_added, FROM + u)
                        for t in range(NT):
                            last = nc.tensor.transpose(bank[4 + t // 4][:, (t % 4) * P:(t % 4 + 1) * P], vN[:, tile(t)], K.c("ident"))
                        last.then_inc(v_turned, 1)
                        pe.wait_ge(vz_made, FROM + 4 * i + 4)
                        av_product()
                    pe.wait_ge(tk_copied, FROM + 2 * u + 2)
                    pe.wait_ge(av_copied, FROM + 2 * u + 2)
                    for t in range(NT):
                        for hh in range(2):
                            last = nc.tensor.matmul(bank[t // 4][:, (t % 4) * P:(t % 4 + 1) * P], W4[t // 2][:, 2 * (t % 2) + hh, :],
                                                    AVz[:, t, hh, :], start=hh == 0, stop=hh == 1)
                    last.then_inc(utk, 1)

                run(pe, start, group, after, tail, pe.Fori)

            @block.vector
            def _(dve):
                def start(i, d):
                    u = 2 * i + d
                    first = isinstance(u, int) and u == 0
                    if not (isinstance(u, int) and u < 2):
                        dve.wait_ge(y_out, FROM + u - 1)
                    for t in range(NT):
                        for n in range(2):
                            dve.wait_ge(aq, FROM + 2 * (NT * u + t) + n + 1)
                            pb = m4(bank[4 + 2 * (t % 2) + n])
                            mask = lambda m: K.c("causal", P, (2 * d + m) * P).unsqueeze(1).broadcast_to([P, 2, P])
                            last = nc.vector.tensor_tensor(NA[:, t, n, :, :], pb[:, 0:2, :], mask(0), ALU.mult)
                            if t >= CT:
                                last = nc.vector.tensor_tensor(QQ[d][:, t - CT, n, :, :], pb[:, 2:4, :], mask(1), ALU.mult)
                            last.then_inc(masked, 1)
                        if t % 2:
                            q = t // 2
                            dve.wait_ge(masked, FROM + 2 * (NT * u + t + 1))
                            for x in range(2):
                                last = nc.vector.tensor_tensor(Y4[q][:, 2 * x:2 * x + 2, :], NA[:, 2 * q + x, 0, :, :],
                                                               K.c("first", P, P * d).unsqueeze(1).broadcast_to([P, 2, P]), ALU.mult)
                            last.then_inc(w_first, 1)
                            dve.wait_ge(w_first, FROM + 6 * u + 2 * q + 1)
                            nc.vector.tensor_tensor(W4[q][:], Y4[q], K.c("ident").unsqueeze(1).broadcast_to([P, 4, P]), ALU.add).then_inc(w_first, 1)
                def group(i, d, lv, st, q):
                    k = 3 * (LV * (2 * i + d) + lv) + q
                    if st == 1:
                        dve.wait_ge(y_prod, FROM + k + 1)
                        nc.vector.tensor_tensor(Y4[q], m4(bank[q]), K.c("level", P, (d * LV + lv) * P).unsqueeze(1).broadcast_to([P, 4, P]),
                                                ALU.mult).then_inc(y_masked, 1)
                    elif st == 2:
                        dve.wait_ge(w_prod, FROM + k + 1)
                        nc.vector.tensor_tensor(W4[q][:], W4[q][:], m4(bank[q]), ALU.add).then_inc(w_added, 1)

                def after(name, i, d, n):
                    u = 2 * i + d
                    first = isinstance(u, int) and u == 0
                    if name == "kk_raw":
                        dve.wait_ge(loaded, 96 * i + 96)
                        nc.vector.tensor_scalar(kk[:], kT[:], col("k_k", i), None, ALU.mult).then_inc(kk_raw, 1)
                    elif name == "kk_sum":
                        dve.wait_ge(kk_sum, FROM + i + 1)
                        for r, m in spans:
                            nc.vector.tensor_scalar(ms[:, r], bank[3 + m][:, 0:r.stop - r.start], 1e-24, None, ALU.max).then_inc(kk_max, 1)
                    elif name in KK_REC:
                        m = KK_REC.index(name)
                        if m == 0:
                            dve.wait_ge(kk_root, FROM + i + 1)
                            if not first:
                                dve.wait_ge(kept, FROM + 2 * u)
                                dve.wait_ge(hats, FROM + 4 * u)
                        part = slice(m * TOK // 3, (m + 1) * TOK // 3)
                        nc.vector.reciprocal(eL[:, part], ms[:, part]).then_inc(kk_rec, 1)
                    elif name == "kk":
                        dve.wait_ge(kk_rec, FROM + 3 * i + 3)
                        nc.vector.tensor_tensor(kk[:], kk[:], eL[:], ALU.mult).then_inc(kk_made, 1)
                    elif name == "log_decay":
                        dve.wait_ge(sig, FROM + 4 * u + 2)
                        nc.vector.tensor_scalar(lw[:], lw[:], NEG, None, ALU.mult).then_inc(scaled_lw, 1)
                    elif name == "cumsum":
                        dve.wait_ge(scaled_lw, FROM + u + 1)
                        if not first:
                            dve.wait_ge(hats, FROM + 4 * u)
                        if d == 0:
                            ins = nc.vector.tensor_tensor_scan(L[:], K.c("start", TOK), lw[:], 0.0, ALU.mult, ALU.add)
                        else:
                            ins = nc.vector.tensor_tensor_scan(L[:, ::-1], K.c("start", TOK), lw[:, ::-1], 0.0, ALU.mult, ALU.add)
                        ins.then_inc(cum, 1)
                    elif name == "kd_half":
                        dve.wait_ge(sig, FROM + 4 * u + 4)
                        if not first:
                            dve.wait_ge(kds_made, FROM + u)
                        nc.vector.tensor_scalar(kd[:], aa[:], -1.0, col("k_a", i), ALU.add, ALU.mult).then_inc(kd_half, 1)
                    elif name == "kd":
                        dve.wait_ge(kd_half, FROM + u + 1)
                        nc.vector.scalar_tensor_tensor(out=kd[:], in0=kd[:], scalar=1.0, in1=kT[:], op0=ALU.add, op1=ALU.mult).then_inc(kd_made, 1)
                    elif name == "b":
                        if d == 0:
                            dve.wait_ge(kk_made, FROM + i + 1)
                            dve.wait_ge(kk_sum, FROM + i + 1)
                        nc.vector.scalar_tensor_tensor(out=b[:], in0=kk[:], scalar=-1.0, in1=aa[:], op0=ALU.mult, op1=ALU.mult).then_inc(b_made, 1)
                    elif name in ("zr0", "zr1"):
                        hh = int(name[2])
                        if hh == 0:
                            dve.wait_ge(exps, FROM + 3 * u + 2)
                            if not first:
                                dve.wait_ge(kept, FROM + 2 * u)
                                dve.wait_ge(aq, FROM + 2 * NT * u)
                        nc.vector.scalar_tensor_tensor(out=zr[:, hh, :], in0=kk[:], scalar=K.c("half", 1, hh), in1=Lx[:],
                                                       op0=ALU.mult, op1=ALU.mult).then_inc(zr_made, 1)
                    elif name in ("zr2", "zr3"):
                        hh = int(name[2]) - 2
                        nc.vector.scalar_tensor_tensor(out=zr[:, 2 + hh, LATR], in0=rT[:], scalar=K.c("half", 1, hh), in1=eL[:, LATR],
                                                       op0=ALU.mult, op1=ALU.mult).then_inc(zr_made, 1)
                    elif name == "keep_kd" and d == 1:
                        dve.wait_ge(kds_half, FROM + i + 1)
                        nc.vector.scalar_tensor_tensor(out=kds[:], in0=kds[:], scalar=col("r_k", i), in1=rT[:],
                                                       op0=ALU.mult, op1=ALU.mult).then_inc(kds_made, 1)
                    elif name == "z":
                        c = order[d][n]
                        rows, t = rows_of(c), c // 2
                        if n == 0:
                            dve.wait_ge(u_copied, FROM + 2 * u + 2)
                            if first:
                                dve.wait_ge(zeroed, FROM + 7)
                            else:
                                dve.wait_ge(y_out, FROM + u)
                        dve.wait_ge(z_prod, FROM + NC * u + n + 1)
                        nc.vector.tensor_tensor(diag(Zz[rows, t]), bank[6][rows, 0:P].rearrange("p (h j) -> p h j", h=2),
                                                U[rows, t, :].rearrange("p (h j) -> p h j", h=2), ALU.add).then_inc(z_added, 1)
                    elif name == "s":
                        c = order[d][n]
                        k = (NC - 1) * u + n
                        dve.wait_ge(s_prod, FROM + k + 1)
                        if not (first and n == 0):
                            dve.wait_ge(s_next, FROM + k)
                        if n == 0:
                            dve.wait_ge(kept, FROM + 2 * u + 2)
                        for hh in range(2):
                            m = slice(NH * hh, NH * hh + NH)
                            last = nc.vector.scalar_tensor_tensor(out=S[m, n + 1, m], in0=S[m, n, m], scalar=pc[d][m, c:c + 1],
                                                                  in1=bank[7][m, m], op0=ALU.mult, op1=ALU.add)
                        last.then_inc(s_next, 1)
                    elif name == "y":
                        dve.wait_ge(y_out, FROM + u + 1)
                        pb = bank[5][:].rearrange("p (t c) -> p t c", c=P)
                        if d == 0:
                            if not first:
                                dve.wait_ge(y_back, FROM + i)
                            nc.vector.tensor_copy(Y, pb).then_inc(y_added, 1)
                        else:
                            dve.wait_ge(y_added, FROM + u)
                            nc.vector.tensor_tensor(Y, Y, pb, ALU.add).then_inc(y_added, 1)
                    elif name in READOUT:
                        readout(name, i)

                y8 = Y.rearrange("p t (h j) -> p (t h) j", h=2)
                sqv = bonus_in[:].rearrange("p (x j) -> p x j", j=NH)
                bc = lambda n: stat[:, n, :].unsqueeze(2).broadcast_to([P, 8, NH])

                def readout(name, i):
                    if name == "bonus":
                        dve.wait_ge(bonus, FROM + i + 1)
                        dve.wait_ge(vt_loaded, 16 * i + 16)
                        nc.vector.tensor_tensor(vT[:], bank[5][:], vT[:], ALU.mult).then_inc(bonus_v, 1)
                    elif name == "gn_mean":
                        dve.wait_ge(y_added, FROM + 2 * i + 2)
                        nc.vector.tensor_reduce(stat[:, 0, :], y8, AX.X, ALU.add).then_inc(gn_chain, 1)
                        dve.wait_ge(gn_chain, FROM + 4 * i + 1)
                        nc.vector.tensor_scalar(stat[:, 0, :], stat[:, 0, :], 1.0 / NH, None, ALU.mult).then_inc(gn_chain, 1)
                        dve.wait_ge(gn_chain, FROM + 4 * i + 2)
                        nc.vector.tensor_tensor(y8, y8, bc(0), ALU.subtract).then_inc(centred, 1)
                    elif name == "gn_var":
                        dve.wait_ge(centred, FROM + i + 1)
                        dve.wait_ge(bonus, FROM + i + 1)
                        nc.vector.tensor_tensor(sqv, y8, y8, ALU.mult).then_inc(gn_chain, 1)
                        dve.wait_ge(gn_chain, FROM + 4 * i + 3)
                        nc.vector.tensor_reduce(stat[:, 1, :], sqv, AX.X, ALU.add).then_inc(gn_chain, 1)
                        dve.wait_ge(gn_chain, FROM + 4 * i + 4)
                        nc.vector.tensor_scalar(stat[:, 2, :], stat[:, 1, :], 1.0 / NH, GN_EPS, ALU.mult, ALU.add).then_inc(gn_var, 1)
                    elif name == "gn_norm":
                        dve.wait_ge(gn_root, FROM + i + 1)
                        nc.vector.reciprocal(stat[:, 1, :], stat[:, 3, :]).then_inc(gn_sum, 1)
                        dve.wait_ge(gn_sum, FROM + i + 1)
                        nc.vector.tensor_tensor(y8, y8, bc(1), ALU.mult).then_inc(normed, 1)
                    elif name == "y_back":
                        dve.wait_ge(y_back, FROM + i + 1)
                        nc.vector.tensor_scalar(bonus_in[:], bank[5][:], col("ln_w", i), col("ln_b", i), ALU.mult, ALU.add).then_inc(y_scaled, 1)
                        dve.wait_ge(y_scaled, FROM + 2 * i + 1)
                        dve.wait_ge(bonus_v, FROM + i + 1)
                        nc.vector.tensor_tensor(bonus_in[:], bonus_in[:], vT[:], ALU.add).then_inc(y_scaled, 1)
                    elif name == "gate":
                        dve.wait_ge(gate, FROM + i + 1)
                        dve.wait_ge(y_scaled, FROM + 2 * i + 2)
                        nc.vector.tensor_tensor(o[:, bass.ds(i, 1), :].rearrange("p o t -> p (o t)"), bonus_in[:], bank[5][:], ALU.mult
                                                ).then_inc(out_made, 1)

                def tail(i, d, scan):
                    u = 2 * i + d

                    def copy_av():
                        dve.wait_ge(av, FROM + u + 1)
                        dve.wait_ge(utk, FROM + 2 * u + 1)
                        for n in range(2):
                            w = (4, 2)[n]
                            for hh in range(2):
                                last = nc.vector.tensor_copy(AVz[:, 4 * n:4 * n + w, hh, NH * hh:NH * hh + NH],
                                                             m4(bank[6 + n])[:, 0:w, NH * hh:NH * hh + NH])
                            last.then_inc(av_copied, 1)

                    if d == 1:
                        copy_av()
                    if scan:
                        after("y", i if d else i - 1, 1 - d, 0)
                    if d == 0:
                        dve.wait_ge(v_turned, FROM + i + 1)
                        if isinstance(i, int) and i == 0:
                            dve.wait_ge(zeroed, FROM + 7)
                        for n in range(2):
                            w = (4, 2)[n]
                            for hh in range(2):
                                nc.vector.tensor_copy(Vz[:, 4 * n:4 * n + w, hh, NH * hh:NH * hh + NH],
                                                      m4(bank[4 + n])[:, 0:w, NH * hh:NH * hh + NH]).then_inc(vz_made, 1)
                        copy_av()

                run(dve, start, group, after, tail, dve.Fori)


def rwkv_layer(K, A, scr, layer):
    nc, x = K.nc, K.x
    norm(K, "n1", layer, 0)
    with ExitStack() as ctx:
        hid = {n: K.sb("hid_" + n, [P, w], ctx) for n, w in (("w1", TOK), ("a1", TOK), ("g1", LAT))}
        mix_and_project(K, A, scr, hid)
        o = K.h[:].rearrange("p k t -> p (k t)")[:, 0:KD * LAT].rearrange("p (k t) -> p k t", k=KD)
        rwkv(K, A, scr, hid, o)
    project_out(K, "out1", A["rw_o"], (o,), KD, layer, ((0, LATR),), spilled=scr["x"])


def build(nc, A, out):
    with ExitStack() as ctx:
        K = Core(nc, ctx)
        K.begin_stage("mixer0")
        mod_dram = nc.dram_tensor("mod_rows_scratch", (2, DEPTH * NCOL, 512), F32, kind="Internal").ap()
        scr = {n: nc.dram_tensor(f"rw_{n}_scratch", (KD, P, TOK), F32, kind="Internal").ap() for n in ("k", "v", "r")}
        scr["x"] = nc.dram_tensor("x_scratch", (P, KD, TOK), F32, kind="Internal").ap()
        with ExitStack() as first:
            K.hold("attn", first)
            modulation(K, A, mod_dram)
            norm(K, "n0", 0, 0)
            v = K.sb("v", [P, NT, NKV * HD], first)
            conv = K.sb("conv_out", [P, KD, TOK], first)
            project_v_conv(K, A, v, conv)
            qk = K.sb("qk", [P, NQ + NKV, TOK], first)
            project_qk(K, A, qk)
            o = K.sb("attn_out", [P, NQ, TOK], first)
            attend(K, qk, v, o)
            project_out(K, "out0", A["w_out"], (o, conv), NQ + KD, 0, RANGES)
        del K.con["attn"]
        K.begin_stage("moe0")
        mixture(K, A, 0)
        K.begin_stage("rwkv1")
        with ExitStack() as second:
            K.hold("rwkv", second)
            load_constants(K, A, "rwkv")
            rwkv_layer(K, A, scr, 1)
        K.begin_stage("moe1")
        mixture(K, A, 1)
        norm(K, "final", None, None, final=out)
    return K.named


def load_constants(K, A, group):
    nc = K.nc
    loaded = K.sem(f"con_{group}_loaded")
    with nc.Block() as block:
        @block.sync
        def _(sp):
            sp.dma_start(K.con[group][:], A["con_" + group]).then_inc(loaded, 16)
            sp.wait_ge(loaded, 16)


def lay_out(a):
    f = lambda n: np.asarray(a[n])
    cols = lambda *names: [f(n).reshape(-1, P) for n in names]
    w = {}
    rows = cols("c", "c_ctx", "ada_b", "norm_g", "final_g", "conv_w", "rw_mu", "rw_w0", "rw_a0", "rw_k_k", "rw_k_a",
                "rw_r_k", "rw_ln_w", "rw_ln_b", "q_norm_g", "k_norm_g")
    w["vecs"] = np.ascontiguousarray(np.concatenate(rows, 0).T)
    x = np.concatenate([f("ctx")[0], f("x")[0]], 0)
    w["xT"] = np.ascontiguousarray(x.T.reshape(KD, P, TOK).transpose(1, 0, 2))

    def by_columns(m, n=P):
        k, c = m.shape
        return np.ascontiguousarray(m.reshape(k // P, P, c // n, n).transpose(2, 1, 0, 3))

    w["ada"] = np.concatenate([by_columns(f("ada_w")[l], 512) for l in range(DEPTH)], 0)
    w["w_in"] = by_columns(f("mix_w_in")[0])
    w["w_out"] = by_columns(f("mix_w_out")[0])
    for n in ("r", "k", "v", "o"):
        w["rw_" + n] = by_columns(f("rw_w_" + n)[0])
    for n in ("w1", "a1"):
        m = f("rw_" + n)[0]
        w[n] = by_columns(np.concatenate([m[0], m[1]], 1))[0]
    w["g1"] = by_columns(f("rw_g1")[0])[0]
    for n in ("w2", "a2"):
        w[n] = np.ascontiguousarray(f("rw_" + n)[0].reshape(2 * 64, KD, P).transpose(1, 0, 2))
    w["g2"] = np.ascontiguousarray(f("rw_g2")[0].reshape(P, KD, P).transpose(1, 0, 2))
    w["router"] = np.ascontiguousarray(f("moe_router").reshape(DEPTH, KD, P, E).transpose(0, 2, 1, 3))
    for n in ("gate", "up", "down"):
        w["moe_" + n] = np.ascontiguousarray(f("moe_w_" + n))
    return w


def kernel(**inputs):
    import concourse.bacc as _bacc
    from concourse.bass_utils import run_bass_kernel_spmd as _run

    arrays = {**lay_out(inputs), **constants()}
    nc = _bacc.Bacc("TRN2", target_bir_lowering=False, num_devices=1)
    A = {n: nc.dram_tensor("in_" + n, a.shape, mybir.dt.from_np(a.dtype), kind="ExternalInput").ap() for n, a in arrays.items()}
    out = nc.dram_tensor("outT", (P, KD, LAT), F32, kind="ExternalOutput").ap()
    build(nc, A, out)
    r = _run(nc, [{"in_" + n: a for n, a in arrays.items()}], core_ids=[0]).results[0]["outT"]
    return np.ascontiguousarray(r.transpose(2, 1, 0).reshape(1, LAT, D))
```
